# Optimizing a Trainium2 kernel written in Bass

```python
import math
import jax, jax.numpy as jnp
from jax import lax
import numpy as np

D_MODEL = 1024
BATCH = 1
SEQ = 256
DEPTH = 2

PL_DIM = 256
N_EVEN = (DEPTH + 1) // 2
N_ODD = DEPTH // 2
CONV_A_WIDTH = D_MODEL
CONV_A_KERNEL = 3
GDN_HEADS = 8
GDN_HEAD_DIM = 128
GDN_WIDTH = GDN_HEADS * GDN_HEAD_DIM
GDN_CONV_KERNEL = 4
GDN_CHUNK = 64
HGRN_HEAD_DIM = 128
HGRN_WIDTH = 2 * D_MODEL
HGRN_HEADS = HGRN_WIDTH // HGRN_HEAD_DIM
HGRN_CHUNK = 32
EVEN_IN = 4 * CONV_A_WIDTH + 4 * GDN_WIDTH + 2 * GDN_HEADS
EVEN_MIX = CONV_A_WIDTH + GDN_WIDTH
ODD_IN = 4 * HGRN_WIDTH
ODD_MIX = HGRN_WIDTH
DEEPNORM_ALPHA = (2.0 * DEPTH) ** 0.25
DEEPNORM_BETA = (8.0 * DEPTH) ** -0.25
NORM_EPS = 1e-5


def layer_norm(x, g, b):
    xf = x.astype(jnp.float32)
    mu = jnp.mean(xf, axis=-1, keepdims=True)
    var = jnp.mean(jnp.square(xf - mu), axis=-1, keepdims=True)
    return ((xf - mu) * lax.rsqrt(var + NORM_EPS) * g.astype(jnp.float32) + b.astype(jnp.float32)).astype(x.dtype)

def rms_norm(x, g):
    xf = x.astype(jnp.float32)
    y = xf * lax.rsqrt(jnp.mean(jnp.square(xf), axis=-1, keepdims=True) + NORM_EPS)
    return (y * g.astype(jnp.float32)).astype(x.dtype)

def l2_normalize(x):
    xf = x.astype(jnp.float32)
    return (xf * lax.rsqrt(jnp.sum(jnp.square(xf), axis=-1, keepdims=True) + 1e-6)).astype(x.dtype)

def causal_depthwise_conv(x, w):
    k, c = w.shape
    return lax.conv_general_dilated(
        x, w[:, None, :].astype(x.dtype), window_strides=(1,), padding=[(k - 1, 0)],
        dimension_numbers=("NWC", "WIO", "NWC"), feature_group_count=c)

def _to_chunks(t, c):
    b, s, h, d = t.shape
    return t.reshape(b, s // c, c, h, d).transpose(0, 3, 1, 2, 4)

def _from_chunks(t):
    b, h, n, c, d = t.shape
    return t.transpose(0, 2, 3, 1, 4).reshape(b, n * c, h, d)

def gated_delta_rule(q, k, v, g, beta):
    dtype = v.dtype
    c = GDN_CHUNK
    dk, dv = q.shape[-1], v.shape[-1]
    q = _to_chunks(q.astype(jnp.float32) * (dk ** -0.5), c)
    k = _to_chunks(k.astype(jnp.float32), c)
    v = _to_chunks(v.astype(jnp.float32), c)
    g = _to_chunks(g.astype(jnp.float32)[..., None], c)[..., 0]
    beta = _to_chunks(beta.astype(jnp.float32)[..., None], c)
    gc = jnp.cumsum(g, axis=-1)
    incl = jnp.tril(jnp.ones((c, c), bool))
    strict = jnp.tril(jnp.ones((c, c), bool), -1)
    decay = jnp.exp(jnp.where(incl, gc[..., :, None] - gc[..., None, :], -jnp.inf))
    kb = k * beta
    low = jnp.where(strict, jnp.einsum("bhnid,bhnjd->bhnij", kb, k) * decay, 0.0)
    rhs = jnp.concatenate([v * beta, kb * jnp.exp(gc)[..., None]], axis=-1)
    sol = lax.linalg.triangular_solve(low + jnp.eye(c, dtype=jnp.float32), rhs,
                                      left_side=True, lower=True, unit_diagonal=True)
    u, w = sol[..., :dv], sol[..., dv:]
    attn = jnp.einsum("bhnid,bhnjd->bhnij", q, k) * decay
    q_dec = q * jnp.exp(gc)[..., None]
    g_last = gc[..., -1]
    k_dec = k * jnp.exp(g_last[..., None] - gc)[..., None]

    def step(state, xs):
        q_i, k_i, u_i, w_i, a_i, gl_i = xs
        v_new = u_i - jnp.einsum("bhcd,bhde->bhce", w_i, state)
        o_i = jnp.einsum("bhcd,bhde->bhce", q_i, state) + jnp.einsum("bhij,bhje->bhie", a_i, v_new)
        state = state * jnp.exp(gl_i)[..., None, None] + jnp.einsum("bhcd,bhce->bhde", k_i, v_new)
        return state, o_i

    mv = lambda t: jnp.moveaxis(t, 2, 0)
    s0 = jnp.zeros(q.shape[:2] + (dk, dv), jnp.float32)
    _, o = lax.scan(step, s0, (mv(q_dec), mv(k_dec), mv(u), mv(w), mv(attn), mv(g_last)))
    return _from_chunks(jnp.moveaxis(o, 0, 2)).astype(dtype)

def hgrn2_recurrence(q, k, v, logf):
    dtype = v.dtype
    c = HGRN_CHUNK
    q, k, v, logf = (jnp.moveaxis(_to_chunks(t.astype(jnp.float32), c), 2, 0) for t in (q, k, v, logf))
    b = jnp.cumsum(logf, axis=-2)
    incl = jnp.tril(jnp.ones((c, c), bool))[:, :, None]

    def step(state, xs):
        q_i, k_i, v_i, b_i = xs
        b_last = b_i[..., -1:, :]
        decay = jnp.exp(jnp.where(incl, b_i[..., :, None, :] - b_i[..., None, :, :], -jnp.inf))
        attn = jnp.einsum("bhtd,bhsd,bhtsd->bhts", q_i, k_i, decay)
        o_i = (jnp.einsum("bhtd,bhde->bhte", q_i * jnp.exp(b_i), state)
               + jnp.einsum("bhts,bhse->bhte", attn, v_i))
        state = (state * jnp.exp(b_last)[..., 0, :, None]
                 + jnp.einsum("bhsd,bhse->bhde", k_i * jnp.exp(b_last - b_i), v_i))
        return state, o_i

    s0 = jnp.zeros(q.shape[1:3] + (q.shape[-1], v.shape[-1]), jnp.float32)
    _, o = lax.scan(step, s0, (q, k, v, b))
    return _from_chunks(jnp.moveaxis(o, 0, 2)).astype(dtype)

def conv_gdn_mixer(x, w_in, conv_a_w, conv_b_w, a_log, dt_bias, gdn_norm_g, w_out):
    bsz, s, _ = x.shape
    wa, wg, h = CONV_A_WIDTH, GDN_WIDTH, GDN_HEADS
    proj = x @ w_in
    cuts = [wa, 2 * wa, 3 * wa, 4 * wa, 4 * wa + 3 * wg, 4 * wa + 4 * wg, 4 * wa + 4 * wg + h]
    h_a, c_a, b_a, z_a, qkv, z_b, beta_raw, a_raw = jnp.split(proj, cuts, axis=-1)
    y_a = b_a * causal_depthwise_conv(c_a * h_a, conv_a_w) * jax.nn.silu(z_a)
    qkv = jax.nn.silu(causal_depthwise_conv(qkv, conv_b_w))
    q, k, v = (t.reshape(bsz, s, h, GDN_HEAD_DIM) for t in jnp.split(qkv, 3, axis=-1))
    q, k = l2_normalize(q), l2_normalize(k)
    beta = jax.nn.sigmoid(beta_raw.astype(jnp.float32))
    g = -jnp.exp(a_log.astype(jnp.float32)) * jax.nn.softplus(a_raw.astype(jnp.float32) + dt_bias.astype(jnp.float32))
    o = gated_delta_rule(q, k, v, g, beta)
    o = rms_norm(o, gdn_norm_g) * jax.nn.silu(z_b.reshape(bsz, s, h, GDN_HEAD_DIM))
    y = jnp.concatenate([y_a, o.reshape(bsz, s, wg)], axis=-1)
    return y @ w_out

def hgrn2_mixer(x, w_in, lower_bound, hgrn_norm_g, w_out):
    bsz, s, _ = x.shape
    q_raw, f_raw, i_in, z = jnp.split(x @ w_in, 4, axis=-1)
    f = lower_bound + (1.0 - lower_bound) * jax.nn.sigmoid(f_raw.astype(jnp.float32))
    q = jax.nn.silu(q_raw)
    k = (1.0 - f).astype(x.dtype)
    logf = jnp.log(f)
    heads = lambda t: t.reshape(bsz, s, HGRN_HEADS, HGRN_HEAD_DIM)
    o = hgrn2_recurrence(heads(q), heads(k), heads(i_in), heads(logf))
    o = rms_norm(o, hgrn_norm_g) * jax.nn.silu(heads(z))
    return o.reshape(bsz, s, HGRN_WIDTH) @ w_out

def first_inputs(seed: int = 0) -> dict:
    key = jax.random.key(seed)
    ks = jax.random.split(key, 20)
    nrm = lambda k, shape, scale: jax.random.normal(k, shape, jnp.float32) * scale
    dt = jnp.exp(jax.random.uniform(ks[6], (N_EVEN, GDN_HEADS), jnp.float32)
                 * (math.log(0.1) - math.log(0.001)) + math.log(0.001))
    return {
        "x": nrm(ks[0], (BATCH, SEQ, D_MODEL), 1.0),
        "p": nrm(ks[1], (DEPTH, BATCH, SEQ, PL_DIM), 1.0),
        "w_in_even": nrm(ks[2], (N_EVEN, D_MODEL, EVEN_IN), D_MODEL ** -0.5),
        "conv_a_w": nrm(ks[3], (N_EVEN, CONV_A_KERNEL, CONV_A_WIDTH), CONV_A_KERNEL ** -0.5),
        "conv_b_w": nrm(ks[4], (N_EVEN, GDN_CONV_KERNEL, 3 * GDN_WIDTH), GDN_CONV_KERNEL ** -0.5),
        "a_log": jnp.log(jax.random.uniform(ks[5], (N_EVEN, GDN_HEADS), jnp.float32, 1.0, 16.0)),
        "dt_bias": dt + jnp.log(-jnp.expm1(-dt)),
        "gdn_norm_g": 1.0 + nrm(ks[7], (N_EVEN, GDN_HEAD_DIM), 0.02),
        "w_out_even": nrm(ks[8], (N_EVEN, EVEN_MIX, D_MODEL), EVEN_MIX ** -0.5 * DEEPNORM_BETA),
        "w_in_odd": nrm(ks[9], (N_ODD, D_MODEL, ODD_IN), D_MODEL ** -0.5),
        "lower_bounds": nrm(ks[10], (DEPTH, HGRN_WIDTH), 0.1),
        "hgrn_norm_g": 1.0 + nrm(ks[11], (N_ODD, HGRN_HEAD_DIM), 0.02),
        "w_out_odd": nrm(ks[12], (N_ODD, ODD_MIX, D_MODEL), ODD_MIX ** -0.5 * DEEPNORM_BETA),
        "ln_g": 1.0 + nrm(ks[13], (DEPTH, D_MODEL), 0.02),
        "ln_b": nrm(ks[14], (DEPTH, D_MODEL), 0.02),
        "w_pl": nrm(ks[15], (DEPTH, PL_DIM, D_MODEL), PL_DIM ** -0.5),
        "w_pl_gate": nrm(ks[16], (DEPTH, D_MODEL, D_MODEL), D_MODEL ** -0.5),
    }

def first_block(x, p, w_in_even, conv_a_w, conv_b_w, a_log, dt_bias, gdn_norm_g, w_out_even,
              w_in_odd, lower_bounds, hgrn_norm_g, w_out_odd, ln_g, ln_b, w_pl, w_pl_gate):
    lbs = jnp.cumsum(jax.nn.softmax(lower_bounds.astype(jnp.float32), axis=0), axis=0)
    lbs = lbs - lbs[0]
    for i in range(DEPTH):
        j = i // 2
        if i % 2 == 0:
            s = conv_gdn_mixer(x, w_in_even[j], conv_a_w[j], conv_b_w[j], a_log[j], dt_bias[j],
                               gdn_norm_g[j], w_out_even[j])
        else:
            s = hgrn2_mixer(x, w_in_odd[j], lbs[i], hgrn_norm_g[j], w_out_odd[j])
        x = layer_norm(DEEPNORM_ALPHA * x + s, ln_g[i], ln_b[i])
        gate = jax.nn.sigmoid((x @ w_pl_gate[i]).astype(jnp.float32))
        x = x + ((p[i] @ w_pl[i]).astype(jnp.float32) * gate).astype(x.dtype)
    return x


N_MIXERS = 2
N_CONV_LAYERS = (DEPTH + 1) // 2
N_ATTN_LAYERS = DEPTH // 2
N_HEADS = 16
HEAD_DIM = D_MODEL // N_HEADS
MOBA_BLOCK = 256
MOBA_TOP_K = 3
Q_CHUNK = 64
CONV_WIDTH = 31
D_FF = 4 * D_MODEL
N_MOD = 6
EPS = 1e-6


def rms_norm_2(x, g):
    xf = x.astype(jnp.float32)
    y = xf * lax.rsqrt(jnp.mean(xf * xf, axis=-1, keepdims=True) + EPS)
    return (y * g.astype(jnp.float32)).astype(x.dtype)

def layer_norm_2(x, g, b):
    xf = x.astype(jnp.float32)
    mu = jnp.mean(xf, axis=-1, keepdims=True)
    xc = xf - mu
    var = jnp.mean(xc * xc, axis=-1, keepdims=True)
    y = xc * lax.rsqrt(var + EPS) * g.astype(jnp.float32) + b.astype(jnp.float32)
    return y.astype(x.dtype)

def alibi_slopes(n_heads):
    return jnp.asarray(2.0 ** (-8.0 * np.arange(1, n_heads + 1) / n_heads), dtype=jnp.float32)

def conformer_conv(h, w_in, b_in, dw, dw_b, ln_g, ln_b, w_out, b_out):
    d = h.shape[-1]
    a, g = jnp.split(h @ w_in + b_in, 2, axis=-1)
    u = a * jax.nn.sigmoid(g)
    u = lax.conv_general_dilated(
        u, dw[:, None, :].astype(u.dtype), window_strides=(1,),
        padding=((CONV_WIDTH - 1, 0),),
        dimension_numbers=('NWC', 'WIO', 'NWC'),
        feature_group_count=d) + dw_b
    u = jax.nn.silu(layer_norm_2(u, ln_g, ln_b))
    return u @ w_out + b_out

def moba_attention(h, w_qkv, q_norm_g, k_norm_g, w_o):
    B, S, D = h.shape
    H, DH = N_HEADS, HEAD_DIM
    q, k, v = jnp.split(h @ w_qkv, 3, axis=-1)
    to_heads = lambda z: z.reshape(B, S, H, DH).transpose(0, 2, 1, 3)
    q = rms_norm_2(to_heads(q), q_norm_g)
    k = rms_norm_2(to_heads(k), k_norm_g)
    v = to_heads(v)

    nb = -(-S // MOBA_BLOCK)
    s_pad = nb * MOBA_BLOCK
    pad = ((0, 0), (0, 0), (0, s_pad - S), (0, 0))
    q, k, v = jnp.pad(q, pad), jnp.pad(k, pad), jnp.pad(v, pad)
    k_blocks = k.reshape(B, H, nb, MOBA_BLOCK, DH)
    v_blocks = v.reshape(B, H, nb, MOBA_BLOCK, DH)
    k_mean = jnp.mean(k_blocks.astype(jnp.float32), axis=3)

    topk = min(MOBA_TOP_K, nb)
    slopes = alibi_slopes(H)
    scale = 1.0 / math.sqrt(DH)
    n_chunks = s_pad // Q_CHUNK
    q_chunks = q.reshape(B, H, n_chunks, Q_CHUNK, DH).transpose(2, 0, 1, 3, 4)
    bi = jnp.arange(B)[:, None, None, None]
    hi = jnp.arange(H)[None, :, None, None]
    blk_ids = jnp.arange(nb)
    in_block = jnp.arange(MOBA_BLOCK)

    def chunk_fn(args):
        qc, ci = args
        t = ci * Q_CHUNK + jnp.arange(Q_CHUNK)
        blk = (ci * Q_CHUNK) // MOBA_BLOCK
        gate = jnp.einsum('bhqd,bhnd->bhqn', qc.astype(jnp.float32), k_mean)
        gate = jnp.where(blk_ids < blk, gate, -jnp.inf)
        gate_val, sel = lax.top_k(gate, topk)
        sel_ok = jnp.isfinite(gate_val)
        k_sel = k_blocks[bi, hi, sel]
        v_sel = v_blocks[bi, hi, sel]
        s_sel = jnp.einsum('bhqd,bhqcsd->bhqcs', qc, k_sel).astype(jnp.float32) * scale
        pos_sel = sel[..., None] * MOBA_BLOCK + in_block
        dist_sel = t[None, None, :, None, None] - pos_sel
        s_sel = s_sel - slopes[None, :, None, None, None] * dist_sel
        s_sel = jnp.where(sel_ok[..., None], s_sel, -jnp.inf)
        k_own = lax.dynamic_slice_in_dim(k, blk * MOBA_BLOCK, MOBA_BLOCK, axis=2)
        v_own = lax.dynamic_slice_in_dim(v, blk * MOBA_BLOCK, MOBA_BLOCK, axis=2)
        s_own = jnp.einsum('bhqd,bhsd->bhqs', qc, k_own).astype(jnp.float32) * scale
        dist_own = t[:, None] - (blk * MOBA_BLOCK + in_block)[None, :]
        s_own = jnp.where(dist_own >= 0, s_own - slopes[None, :, None, None] * dist_own, -jnp.inf)
        scores = jnp.concatenate([s_sel.reshape(B, H, Q_CHUNK, topk * MOBA_BLOCK), s_own], axis=-1)
        p = jax.nn.softmax(scores, axis=-1)
        p_sel = p[..., :topk * MOBA_BLOCK].reshape(B, H, Q_CHUNK, topk, MOBA_BLOCK).astype(v.dtype)
        p_own = p[..., topk * MOBA_BLOCK:].astype(v.dtype)
        return (jnp.einsum('bhqcs,bhqcsd->bhqd', p_sel, v_sel)
                + jnp.einsum('bhqs,bhsd->bhqd', p_own, v_own))

    out = lax.map(chunk_fn, (q_chunks, jnp.arange(n_chunks)))
    out = out.transpose(1, 2, 0, 3, 4).reshape(B, H, s_pad, DH)[:, :, :S]
    out = out.transpose(0, 2, 1, 3).reshape(B, S, D)
    return out @ w_o

def second_inputs(seed: int = 0) -> dict:
    key = jax.random.key(seed)
    ks = iter(jax.random.split(key, 32))
    nrm = lambda shape, s: jax.random.normal(next(ks), shape, jnp.float32) * s
    D = D_MODEL
    return {
        "x": nrm((BATCH, SEQ, D), 1.0),
        "c": nrm((BATCH, D), 1.0),
        "ada_w": nrm((DEPTH, D, N_MOD * D), 0.5 * D ** -0.5),
        "ada_b": nrm((DEPTH, N_MOD * D), 0.02),
        "mix_norm_g": 1.0 + nrm((DEPTH, D), 0.1),
        "mlp_norm_g": 1.0 + nrm((DEPTH, D), 0.1),
        "conv_w_in": nrm((N_CONV_LAYERS, D, 2 * D), D ** -0.5),
        "conv_b_in": nrm((N_CONV_LAYERS, 2 * D), 0.02),
        "conv_dw": nrm((N_CONV_LAYERS, CONV_WIDTH, D), CONV_WIDTH ** -0.5),
        "conv_dw_b": nrm((N_CONV_LAYERS, D), 0.02),
        "conv_ln_g": 1.0 + nrm((N_CONV_LAYERS, D), 0.1),
        "conv_ln_b": nrm((N_CONV_LAYERS, D), 0.02),
        "conv_w_out": nrm((N_CONV_LAYERS, D, D), D ** -0.5),
        "conv_b_out": nrm((N_CONV_LAYERS, D), 0.02),
        "attn_w_qkv": nrm((N_ATTN_LAYERS, D, 3 * D), D ** -0.5),
        "attn_q_norm_g": 1.0 + nrm((N_ATTN_LAYERS, HEAD_DIM), 0.1),
        "attn_k_norm_g": 1.0 + nrm((N_ATTN_LAYERS, HEAD_DIM), 0.1),
        "attn_w_o": nrm((N_ATTN_LAYERS, D, D), D ** -0.5),
        "mlp_w1": nrm((DEPTH, D, D_FF), D ** -0.5),
        "mlp_w2": nrm((DEPTH, D_FF, D), D_FF ** -0.5),
    }

def second_block(x, c, ada_w, ada_b, mix_norm_g, mlp_norm_g,
              conv_w_in, conv_b_in, conv_dw, conv_dw_b, conv_ln_g, conv_ln_b, conv_w_out, conv_b_out,
              attn_w_qkv, attn_q_norm_g, attn_k_norm_g, attn_w_o,
              mlp_w1, mlp_w2):
    cond = jax.nn.silu(c)
    for i in range(DEPTH):
        mod = cond @ ada_w[i] + ada_b[i]
        sh1, sc1, g1, sh2, sc2, g2 = [m[:, None, :] for m in jnp.split(mod, N_MOD, axis=-1)]
        h = rms_norm_2(x, mix_norm_g[i]) * (1.0 + sc1) + sh1
        j = i // N_MIXERS
        if i % N_MIXERS == 0:
            y = conformer_conv(h, conv_w_in[j], conv_b_in[j], conv_dw[j], conv_dw_b[j],
                               conv_ln_g[j], conv_ln_b[j], conv_w_out[j], conv_b_out[j])
        else:
            y = moba_attention(h, attn_w_qkv[j], attn_q_norm_g[j], attn_k_norm_g[j], attn_w_o[j])
        x = x + g1 * y
        h = rms_norm_2(x, mlp_norm_g[i]) * (1.0 + sc2) + sh2
        x = x + g2 * (jnp.square(jax.nn.relu(h @ mlp_w1[i])) @ mlp_w2[i])
    return x


def setup_inputs(seed=0):
    out = dict(first_inputs(seed))
    for name, value in second_inputs(seed + 1).items():
        if name != "x":
            out[name + "_2"] = value
    return out


def reference(
    x, p, w_in_even, conv_a_w, conv_b_w, a_log, dt_bias, gdn_norm_g, w_out_even, w_in_odd,
    lower_bounds, hgrn_norm_g, w_out_odd, ln_g, ln_b, w_pl, w_pl_gate, c_2, ada_w_2, ada_b_2,
    mix_norm_g_2, mlp_norm_g_2, conv_w_in_2, conv_b_in_2, conv_dw_2, conv_dw_b_2, conv_ln_g_2,
    conv_ln_b_2, conv_w_out_2, conv_b_out_2, attn_w_qkv_2, attn_q_norm_g_2, attn_k_norm_g_2,
    attn_w_o_2, mlp_w1_2, mlp_w2_2,
):
    x = first_block(
        x, p, w_in_even, conv_a_w, conv_b_w, a_log, dt_bias, gdn_norm_g, w_out_even, w_in_odd,
        lower_bounds, hgrn_norm_g, w_out_odd, ln_g, ln_b, w_pl, w_pl_gate,
    )
    return second_block(
        x, c_2, ada_w_2, ada_b_2, mix_norm_g_2, mlp_norm_g_2, conv_w_in_2, conv_b_in_2,
        conv_dw_2, conv_dw_b_2, conv_ln_g_2, conv_ln_b_2, conv_w_out_2, conv_b_out_2,
        attn_w_qkv_2, attn_q_norm_g_2, attn_k_norm_g_2, attn_w_o_2, mlp_w1_2, mlp_w2_2,
    )


_drawn_inputs = setup_inputs


def setup_inputs(seed=0):
    import zlib

    import numpy as np

    out = dict(_drawn_inputs(seed))
    spreads = {}
    factors = {'a_log': 2.769,
     'gdn_norm_g': 8.0,
     'lower_bounds': 8.0,
     'hgrn_norm_g': 8.0,
     'conv_b_in_2': 8.0,
     'conv_dw_b_2': 8.0,
     'conv_ln_g_2': 3.021,
     'conv_ln_b_2': 8.0,
     'conv_b_out_2': 8.0,
     'attn_q_norm_g_2': 8.0,
     'attn_k_norm_g_2': 8.0}
    for name, (base, spread) in spreads.items():
        noise = np.random.default_rng([zlib.crc32(name.encode()), seed]).standard_normal(out[name].shape)
        drawn = base * np.exp(spread * noise) if base else spread * noise
        out[name] = __import__('jax').numpy.asarray(drawn.astype(out[name].dtype))
    for name, factor in factors.items():
        out[name] = (out[name] * factor).astype(out[name].dtype)
    return out
```

```python
import numpy as np
import concourse.bass as bass
from concourse import mybir
from contextlib import ExitStack

T = 256
NR, NS = 3, 3
ALPHA = 4.0 ** 0.25
NEG = -1.0e30


COLS = [("conv_a_w", 24), ("conv_b_w", 96), ("gdn_g", 1), ("lb", 32), ("hgrn_g", 1), ("ln_g", 16), ("ln_b", 16),
        ("c", 8), ("ada_b", 96), ("mix_g", 16), ("mlp_g", 16), ("b_in", 16), ("dw", 248), ("dw_b", 8),
        ("cln_g", 8), ("cln_b", 8), ("b_out", 8), ("qn_g", 1), ("kn_g", 1), ("heads", 2), ("wbg", 128)]
COL0 = {}
_n = 0
for _name, _k in COLS:
    COL0[_name] = (_n, _k)
    _n += _k
NCOL = _n

CST = [("ident", 128), ("ones", 128), ("ones64", 128), ("neg", 128), ("gm", 896), ("dist", 384), ("sel", 1024)]
CST0 = {}
_n = 0
for _name, _k in CST:
    CST0[_name] = (_n, _k)
    _n += _k
NCST = _n


def constants():
    j = np.arange(128)[:, None]
    i = np.arange(128)[None, :]
    f = np.zeros((128, NCST), np.float32)

    def put(name, v):
        a, n = CST0[name]
        f[:v.shape[0], a:a + n] = v

    put("ident", (i == j).astype(np.float32))
    put("ones", np.ones((128, 128), np.float32))
    put("ones64", (i // 64 == j // 64).astype(np.float32))
    put("neg", np.where(i >= j, 0.0, NEG).astype(np.float32))
    lv = [((i // (2 * s) == j // (2 * s)) & ((i // s) % 2 == 1) & ((j // s) % 2 == 0)) for s in (1, 2, 4, 8, 16, 32, 64)]
    put("gm", np.concatenate(lv, 1).astype(np.float32))
    k = np.arange(256)[None, :]
    d0 = np.where(j >= i, -(j - i).astype(np.float32), np.float32(NEG))
    d1 = np.where(j + 128 >= k, -(j + 128 - k).astype(np.float32), np.float32(NEG))
    put("dist", np.concatenate([d0, d1], 1).astype(np.float32))
    sel = np.zeros((8, 8, 128), np.float32)
    for h in range(8):
        sel[h, h] = 1.0
    put("sel", sel.reshape(8, 1024))
    return f


class Lane:

    def __init__(self, sem):
        self.sem, self.q, self.n, self.seen = sem, [], 0, {}

    def wait(self, toks):
        for t in toks:
            if t is None:
                continue
            if isinstance(t, list):
                self.wait(t)
                continue
            sem, v = t
            if self.seen.get(id(sem), 0) < v:
                self.seen[id(sem)] = v
                self.q.append((sem, v))

    def last(self):
        return (self.sem, self.n) if self.n else None

    def do(self, fn, *toks, inc=True):
        self.wait(toks)
        self.q.append((fn, inc))
        if inc:
            self.n += 1
        return (self.sem, self.n)

    def play(self, eng):
        for a, b in self.q:
            if callable(a):
                ins = a(eng)
                if b:
                    ins.then_inc(self.sem, 1)
            else:
                eng.wait_ge(a, b)


def program(nc, xT, wst, cols, rows, pT, cst, out, plan):
    f32, fr, i32 = mybir.dt.float32, mybir.dt.float32r, mybir.dt.int32
    ALU, ACT, AX = mybir.AluOpType, mybir.ActivationFunctionType, mybir.AxisListType
    ctx = ExitStack()
    with ctx:
        def sb(name, shape, dt=f32):
            return ctx.enter_context(nc.sbuf_tensor(name, shape, dt))

        def sem(name):
            return ctx.enter_context(nc.semaphore(name))

        RAW = [sb(f"RAW{i}", [128, 2048]) for i in range(NR)]
        WH = [sb(f"WH{i}", [128, 2048], fr) for i in range(NS)]
        WL = [sb(f"WL{i}", [128, 2048], fr) for i in range(NS)]
        X = sb("X", [128, 8, T])
        XH = sb("XH", [128, 8, T], fr)
        XL = sb("XL", [128, 8, T], fr)
        YH = sb("YH", [128, 16, T], fr)
        YL = sb("YL", [128, 16, T], fr)
        C = sb("C", [128, NCOL])
        R8 = sb("R8", [8, 2])
        PT = sb("PT", [128, 2, 2, T])
        K = sb("K", [128, NCST])
        MOD = sb("MOD", [128, 96])
        SM = sb("SM", [128, 256])
        BIG = sb("BIG", [128, 14144])
        PS = [ctx.enter_context(nc.psum_tensor(f"PS{i}", [128, 512], f32)) for i in range(8)]

        s_pe, s_v, s_a, s_g = sem("s_pe"), sem("s_v"), sem("s_a"), sem("s_g")
        s_in, s_x, s_out = sem("s_in"), sem("s_x"), sem("s_out")
        s_raw = [sem(f"s_raw{i}") for i in range(NR)]

        def col(name, i=0, n=1, p=128):
            a = COL0[name][0] + i
            return C[0:p, a:a + n]

        def cs(name, i=0, n=128, p=128):
            a = CST0[name][0] + i
            return K[0:p, a:a + n]

        def emit(plan, specs):
            pe, ve, ac, gp, sp = Lane(s_pe), Lane(s_v), Lane(s_a), Lane(s_g), Lane(s_out)

            def V(fn, *w, free=False):
                return ve.do(fn, *(w if free else (ve.last(), *w)))

            def G(fn, *w, free=False):
                return gp.do(fn, *(w if free else (gp.last(), *w)))

            def tt(o, a, b, op, *w, free=False, E=V):
                return E(lambda e: e.tensor_tensor(o, a, b, op), *w, free=free)

            def ts(o, a, s1, s2, op0, op1, *w, free=False, E=V):
                if op1 is None:
                    return E(lambda e: e.tensor_scalar(o, a, s1, None, op0), *w, free=free)
                return E(lambda e: e.tensor_scalar(o, a, s1, s2, op0, op1), *w, free=free)

            def stt(o, a, s, b, op0, op1, *w, free=False):
                return V(lambda e: e.scalar_tensor_tensor(out=o, in0=a, scalar=s, in1=b, op0=op0, op1=op1), *w, free=free)

            def act(o, a, f, *w, free=False, **kw):
                return ac.do(lambda e: e.activation(o, a, f, **kw), *(w if free else (ac.last(), *w)))

            def mm(o, l, r, *w, start=True, stop=True, inc=False):
                return pe.do(lambda e: e.matmul(o, l, r, start=start, stop=stop), *w, inc=inc)

            def tr(o, a, *w, inc=False):
                n = a.shape[0]
                return pe.do(lambda e: e.transpose(o, a, cs("ident", 0, n, n)), *w, inc=inc)

            s_xt = (s_x, 16)
            s_all = (s_in, 80)

            def loads(e):
                e.dma_start(X[:, :, :], xT).then_inc(s_x, 16)
                for o, i in ((C[:, :], cols), (R8[:, :], rows), (K[:, :], cst),
                             (PT[:, 0, :, :], pT[0]), (PT[:, 1, :, :], pT[1])):
                    e.dma_start(o, i).then_inc(s_in, 16)

            raw_free = {}
            slot_free = {}
            sp_tok = {}
            st = {"load": 0, "split": 0, "ns": 0, "used": 0}
            slot_of = {}

            def raw_ready(u):
                return (s_raw[u % NR], 16 * (u // NR + 1))

            def load_more():
                while st["load"] < len(plan) and (st["load"] < NR or (st["load"] - NR) in raw_free):
                    u = st["load"]
                    sp.wait([raw_free.get(u - NR)])
                    sp.q.append((lambda e, u=u: e.dma_start(RAW[u % NR][:, :], wst[u]).then_inc(s_raw[u % NR], 16), False))
                    st["load"] += 1

            def split_next():
                u = st["split"]
                if u >= len(plan):
                    return False
                if plan[u][0] == "ada_w":
                    st["split"] += 1
                    return True
                n = st["ns"]
                if n >= NS and (n - NS) not in slot_free:
                    return False
                load_more()
                if u >= st["load"]:
                    return False
                s, free = n % NS, slot_free.get(n - NS)
                r = RAW[u % NR]
                a = act(WH[s][:, :], r[:, :], ACT.Copy, raw_ready(u), free, free=True)
                b = tt(WL[s][:, :], r[:, :], WH[s][:, :].bitcast(f32), ALU.subtract, a, raw_ready(u), free, free=True)
                sp_tok[u] = [a, b]
                raw_free[u] = [a, b]
                slot_of[u] = (s, n)
                st["ns"] += 1
                st["split"] += 1
                load_more()
                return True

            def pump():
                load_more()
                while split_next():
                    pass

            def unit(*spec):
                specs.append(spec)
                u = st["used"]
                st["used"] += 1
                if u < len(plan):
                    assert plan[u] == spec, (u, plan[u], spec)
                    pump()
                    assert spec[0] == "ada_w" or u in slot_of
                return u

            bank = {"n": 0}
            bfree = [None] * 8

            def take_bank():
                b = bank["n"] % 3
                bank["n"] += 1
                return b

            def wparts(u, nk):
                s = slot_of[u][0] if u in slot_of else 0
                return (WH[s][:, :].rearrange("p (k n) -> p k n", k=nk), WL[s][:, :].rearrange("p (k n) -> p k n", k=nk))

            def release(u, tok):
                if u in slot_of:
                    slot_free[slot_of[u][1]] = tok
                    pump()

            def three(o, l, r, first, lastk, *w, inc=False):
                mm(o, l[0], r[0], *w, start=first, stop=False)
                mm(o, l[0], r[1], start=False, stop=False)
                return mm(o, l[1], r[0], start=False, stop=lastk, inc=inc)

            def product(spec, act_hl, k0, post, *w):
                u = unit(*spec)
                b = take_bank()
                h, l = act_hl
                wh, wl = wparts(u, 8)
                for n in range(2):
                    for k in range(8):
                        t = three(PS[b][:, n * T:(n + 1) * T],
                                  (wh[:, k, n * 128:(n + 1) * 128], wl[:, k, n * 128:(n + 1) * 128]),
                                  (h[:, k0 + k, :], l[:, k0 + k, :]), k == 0, k == 7,
                                  *((sp_tok.get(u), bfree[b], *w) if n == 0 and k == 0 else ()), inc=(k == 7))
                    if n == 0:
                        yield
                bfree[b] = post(PS[b][:, :].rearrange("p (n t) -> p n t", n=2), t)
                release(u, t)
                yield

            def product_tok(spec, act_hl, post, *w):
                u = unit(*spec)
                b = take_bank()
                h, l = act_hl
                wh, wl = wparts(u, 8)
                for n in range(2):
                    for k in range(8):
                        t = three(PS[b][:, n * T:(n + 1) * T],
                                  (h[:, k, n * 128:(n + 1) * 128], l[:, k, n * 128:(n + 1) * 128]),
                                  (wh[:, k, :], wl[:, k, :]), k == 0, k == 7,
                                  *((sp_tok.get(u), bfree[b], *w) if n == 0 and k == 0 else ()), inc=(k == 7))
                    if n == 0:
                        yield
                bfree[b] = post(PS[b][:, :].rearrange("p (n t) -> p n t", n=2), t)
                release(u, t)
                yield

            def run(g):
                for _ in g:
                    pass

            ada = {"n": 0, "tok": None}
            csil = SM[:, 0:8]
            csil_tok = [None]

            def ada_unit():
                n = ada["n"]
                ada["n"] += 1
                u = unit("ada_w", n // 24, 0, (n % 24) * 256)
                w = RAW[u % NR][:, :].rearrange("p (k n) -> p k n", k=8)
                for m in range(2):
                    for k in range(8):
                        t = mm(PS[7][:, 2 * n + m:2 * n + m + 1], w[:, k, m * 128:(m + 1) * 128], csil[:, k:k + 1],
                               raw_ready(u), csil_tok[0], ada.get("free"), start=(k == 0), stop=(k == 7), inc=(k == 7))
                    if m == 0:
                        yield
                raw_free[u] = [t]
                ada["tok"] = t
                pump()
                yield

            fillers = []

            def fill(n=1, keep=0):
                while n > 0 and fillers:
                    try:
                        next(fillers[0])
                        n -= 1
                    except StopIteration:
                        fillers.pop(0)

            def fill_all():
                while fillers:
                    fill(1)

            def ada_fill(n):
                for _ in range(n):
                    if ada["n"] < 48:
                        run(ada_unit())

            pump()
            XHL = (XH, XL)
            YHL = (YH, YL)

            def split_act(hl, lo, n, src, *w):
                a = act(hl[0][:, lo:lo + n, :], src, ACT.Copy, *w)
                b = tt(hl[1][:, lo:lo + n, :], src, hl[0][:, lo:lo + n, :].bitcast(f32), ALU.subtract, a, *w)
                return [a, b]

            xs = split_act(XHL, 0, 8, X[:, :, :], s_xt)

            def view(off, *shape):
                n = int(np.prod(shape))
                assert off + n <= 14144, (off, shape)
                v = BIG[:, off:off + n]
                if len(shape) == 2:
                    v = v.rearrange("p (a b) -> p a b", a=shape[0])
                return v

            def bc(ap, n):
                return ap.unsqueeze(2).broadcast_to([ap.shape[0], ap.shape[1], n])

            def bm(ap, n):
                return ap.unsqueeze(1).broadcast_to([ap.shape[0], n, ap.shape[1]])

            lb = col("lb", 0, 32)
            LB, OLB = SM[:, 16:32], SM[:, 32:48]
            mx, e0, e1, sm = SM[:, 48:64], SM[:, 64:80], SM[:, 80:96], SM[:, 96:112]
            tt(mx, lb[:, 0:16], lb[:, 16:32], ALU.max, s_all)
            tt(e0, lb[:, 0:16], mx, ALU.subtract)
            t = tt(e1, lb[:, 16:32], mx, ALU.subtract)
            t = act(SM[:, 64:96], SM[:, 64:96], ACT.Exp, t)
            tt(sm, e0, e1, ALU.add, t)
            V(lambda e: e.reciprocal(sm, sm))
            tt(e0, e0, sm, ALU.mult)
            tt(e1, e1, sm, ALU.mult)
            tt(e1, e1, e0, ALU.add)
            tt(LB, e1, e0, ALU.subtract)
            ts(OLB, LB, -1.0, 1.0, ALU.mult, ALU.add)

            RW = ctx_rw
            beta, aa, ab, gc = RW[:, 0, :], RW[:, 1, :], RW[:, 2, :], RW[:, 3, :]
            wbg = col("wbg", 0, 128).rearrange("p (k n) -> p k n", k=8)
            for q in range(2):
                for k in range(8):
                    t = mm(PS[3][0:8, q * T:(q + 1) * T], wbg[:, k, q * 8:(q + 1) * 8], X[:, k, :], s_all, s_xt,
                           start=(k == 0), stop=(k == 7), inc=(k == 7))
            nea = SM[0:8, 120:121]
            act(nea, R8[:, 0:1], ACT.Exp, s_all)
            act(aa, PS[3][0:8, T:2 * T], ACT.Identity, t, bias=R8[:, 1:2])
            act(ab, aa, ACT.Abs)
            ac.do(lambda e: e.preload_act_table_set("natural_log_exp_and_others"), inc=False)
            act(ab, ab, ACT.Exp, scale=-1.0)
            t2 = act(ab, ab, ACT.Ln, bias=1.0)
            stt(aa, aa, 0.0, ab, ALU.max, ALU.add, t2)
            ts(aa, aa, nea, -1.0, ALU.mult, ALU.mult, t2)
            for c in range(2):
                V(lambda e, c=c: e.tensor_tensor_scan(gc[:, c * 128:(c + 1) * 128], cs("ones", 0, 128, 8),
                                                      aa[:, c * 128:(c + 1) * 128], 0.0, ALU.mult, ALU.add))
            gct = ve.last()
            bt = act(beta, PS[3][0:8, 0:T], ACT.Sigmoid)
            bfree[3] = [gct, bt]
            csil_tok[0] = act(csil, col("c", 0, 8), ACT.Silu, s_all)
            for c in range(2):
                tr(PS[3][:, c * 8:c * 8 + 8], gc[:, c * 128:(c + 1) * 128], gct, bt, bfree[3])
                t = tr(PS[3][:, 16 + c * 8:24 + c * 8], beta[:, c * 128:(c + 1) * 128], inc=True)
            GCT = SM[:, 128:144]
            BT = SM[:, 144:160]
            EG = SM[:, 160:176]
            KB = SM[:, 176:192]
            KD = SM[:, 192:200]
            V(lambda e: e.tensor_copy(SM[:, 128:160], PS[3][:, 0:32]), t)
            bfree[3] = ve.last()
            colt = ve.last()

            QKV = view(0, 24, T)
            CB = [view(6144 + 512 * i + 8 * i, 2, 260) for i in range(2)]
            AC = [view(7200 + 512 * i, 2, T) for i in range(2)]
            for i in range(2):
                t = G(lambda e, i=i: e.memset(CB[i][:, :, 0:4], 0.0))
            zt = t
            cb = {"n": 0, "free": [None, None], "acf": [None, None]}
            qkv_tok = {}

            def qkv_post(which, hp):
                def post(ps, t):
                    i = cb["n"] % 2
                    cb["n"] += 1
                    a = act(CB[i][:, :, 4:260], ps, ACT.Copy, t, cb["free"][i], zt)
                    for m in range(2):
                        j = which * 8 + 2 * hp + m
                        ts(AC[i][:, m, :], CB[i][:, m, 1:257], col("conv_b_w", j * 4), None, ALU.mult, None, a, cb["acf"][i])
                        for q in range(1, 4):
                            v = stt(AC[i][:, m, :], CB[i][:, m, 1 + q:257 + q], col("conv_b_w", j * 4 + q), AC[i][:, m, :],
                                    ALU.mult, ALU.add)
                    cb["free"][i] = v
                    j = which * 8 + 2 * hp
                    s = act(QKV[:, j:j + 2, :], AC[i], ACT.Silu, v)
                    cb["acf"][i] = s
                    qkv_tok[(which, hp)] = s
                    return a
                return post

            for hp in range(4):
                for which in range(3):
                    run(product(("w_in_even", 0, 0, 4096 + 1024 * which + 256 * hp), XHL, 0, qkv_post(which, hp), xs))

            HS = view(8240, 1, T)
            CH = view(8496, 1, 260)
            AA = view(8756, 1, T)
            YA = view(9012, 2, T)
            ZA = view(9524, 2, T)
            zch = G(lambda e: e.memset(CH[:, :, 0:4], 0.0))
            ga = {"ya": None, "ysplit": [], "pend": None}

            def a_tile(j):
                def post1(ps, t):
                    a = act(HS[:, 0, :], ps[:, 0, :], ACT.Copy, t, ga.get("ch"))
                    v = tt(CH[:, 0, 4:260], ps[:, 1, :], HS[:, 0, :], ALU.mult, a, zch)
                    ga["ch"] = v
                    ts(AA[:, 0, :], CH[:, 0, 2:258], col("conv_a_w", j * 3), None, ALU.mult, None)
                    for q in range(1, 3):
                        stt(AA[:, 0, :], CH[:, 0, 2 + q:258 + q], col("conv_a_w", j * 3 + q), AA[:, 0, :], ALU.mult, ALU.add)
                    return [a, v]

                def post2(ps, t):
                    m = j % 2
                    v = tt(YA[:, m, :], ps[:, 0, :], AA[:, 0, :], ALU.mult, t, ga["ya"])
                    a = act(ZA[:, m, :], ps[:, 1, :], ACT.Copy, t, ga["ya"], v)
                    ga["pend"] = [v, a]
                    if m:
                        a_flush(j - 1)
                    return [v, a]

                yield from product(("w_in_even", 0, 0, (128 * j, 1024 + 128 * j)), XHL, 0, post1, xs)
                yield from product(("w_in_even", 0, 0, (2048 + 128 * j, 3072 + 128 * j)), XHL, 0, post2, xs)

            def a_flush(j):
                a = act(ZA, ZA, ACT.Silu, ga["pend"])
                v = tt(YA, YA, ZA, ALU.mult, a)
                ga["ysplit"] = split_act(YHL, j, 2, YA, v)
                ga["ya"] = ga["ysplit"]

            B0 = 10036
            names = ["D", "LT", "ML", "XX", "YY"]
            slots = {}

            def gt(name, i):
                slots[name] = view(B0 + 512 * i, 4, 128)
                return slots[name]

            DD, LT, ML, XX, YY, PP, AT, VB = [gt(n, i) for i, n in enumerate(["D", "LT", "ML", "X", "Y", "P", "AT", "VB"])]
            gc1 = [XX, YY]
            KBE, UU, SS, WT = [view(6144 + 512 * i, 4, 128) for i in range(4)]
            SQ = view(B0, 4, T)
            SQ2 = view(B0 + 1024, 4, T)

            qk_tok = {}

            def l2(which, g):
                j = which * 8 + 4 * g
                src = QKV[:, j:j + 4, :]
                sq = G(lambda e: e.tensor_tensor(SQ, src, src, ALU.mult), qkv_tok[(which, 2 * g)], qkv_tok[(which, 2 * g + 1)],
                       pe.last(), ac.last())
                ts_ = []
                for m in range(4):
                    b = 3 + m // 2
                    t = mm(PS[b][:, (m % 2) * T:(m % 2 + 1) * T], cs("ones"), SQ[:, m, :], sq, bfree[b], inc=True)
                fill(1)
                a1 = act(SQ2[:, 0:2, :], PS[3][:, :].rearrange("p (a b) -> p a b", a=2), ACT.Ln, t, ve.last(), bias=EPSC["1e-6"])
                a2 = act(SQ2[:, 2:4, :], PS[4][:, :].rearrange("p (a b) -> p a b", a=2), ACT.Ln, bias=EPSC["1e-6"])
                bfree[3] = a1
                bfree[4] = a2
                if which == 0:
                    a = act(SQ2, SQ2, ACT.Exp, scale=-0.5, bias=EPSC["lnq"])
                else:
                    a = act(SQ2, SQ2, ACT.Exp, scale=-0.5)
                return tt(src, src, SQ2, ALU.mult, a)

            epst = [G(lambda e, o=o, v=v: e.memset(o, v)) for o, v in EPSV]
            epst = epst[-1]
            ac.wait([epst])
            for j in range(8):
                fillers.append(a_tile(j))
            ac.do(lambda e: e.preload_act_table_set("natural_log_exp_and_others"), inc=False)
            act(EG, GCT, ACT.Exp, colt)
            v = tt(KB, BT, EG, ALU.mult, ac.last())
            for g in range(2):
                for which in range(2):
                    qk_tok[g] = l2(which, g)

            def grp(b):
                return PS[b][:, :].rearrange("p (a b) -> p a b", a=4)

            def gdn(g, c):
                hs = [4 * g + m for m in range(4)]
                tok = slice(c * 128, (c + 1) * 128)
                ac.do(lambda e: e.preload_act_table_set("natural_log_exp_and_others"), inc=False)
                for m, h in enumerate(hs):
                    t = mm(PS[3][:, m * 128:(m + 1) * 128], cs("sel", h * 128, 128, 8), gc[:, tok], bfree[3], inc=(m == 3))
                for m, h in enumerate(hs):
                    t2 = mm(PS[4][:, m * 128:(m + 1) * 128], cs("sel", h * 128, 128, 8), beta[:, tok], bfree[4], inc=(m == 3))
                tt(DD, grp(3), bc(GCT[:, c * 8 + 4 * g:c * 8 + 4 * g + 4], 128), ALU.subtract, t, gfree["D"])
                v = tt(DD, DD, bm(cs("neg"), 4), ALU.add)
                kd = KD[:, 4 * g:4 * g + 4]
                if c == 0:
                    v = tt(kd, grp(3)[:, :, 127], GCT[:, 4 * g:4 * g + 4], ALU.subtract)
                    a = act(kd, kd, ACT.Exp, v)
                else:
                    a = act(ML, grp(3), ACT.Exp, t, v, gfree["ML"])
                    v = tt(ML, ML, QKV[:, 4 * g:4 * g + 4, tok], ALU.mult, a, qk_tok[g])
                qd = ve.last()
                d = act(DD, DD, ACT.Exp, v)
                bfree[3] = [ve.last(), a]
                fill(1)
                for m, h in enumerate(hs):
                    kT, qT = QKV[:, 8 + h, tok], QKV[:, h, tok]
                    mm(PS[5][:, m * 128:(m + 1) * 128], kT, kT, qk_tok[g], bfree[5])
                    t3 = mm(PS[6][:, m * 128:(m + 1) * 128], kT, qT, bfree[6], inc=(m == 3))
                tt(LT, DD, grp(4), ALU.mult, t2, d, gfree["LT"])
                bfree[4] = ve.last()
                tt(LT, LT, grp(5), ALU.mult, t3)
                bfree[5] = ve.last()
                tt(AT, DD, grp(6), ALU.mult, gfree["AT"])
                bfree[6] = ve.last()
                gfree["D"] = ve.last()
                for m, h in enumerate(hs):
                    tr(PS[3][:, m * 128:(m + 1) * 128], QKV[:, 8 + h, tok], bfree[3], qk_tok[g])
                    t4 = tr(PS[5][:, m * 128:(m + 1) * 128], QKV[:, 16 + h, tok], bfree[5], qkv_tok[(2, 2 * g)], qkv_tok[(2, 2 * g + 1)],
                            inc=(m == 3))
                fill(1)
                if c == 0:
                    tt(KBE, grp(3), bc(kd, 128), ALU.mult, t4, a, gfree["KBE"])
                else:
                    tt(KBE, grp(3), bc(KB[:, 8 + 4 * g:12 + 4 * g], 128), ALU.mult, t4, gfree["KBE"])
                bfree[3] = ve.last()
                kt = ve.last()
                tt(VB, grp(5), bc(BT[:, c * 8 + 4 * g:c * 8 + 4 * g + 4], 128), ALU.mult, gfree["VB"])
                vt = ve.last()
                bfree[5] = ve.last()
                QD = WT
                if c == 1:
                    V(lambda e: e.tensor_copy(QD, ML), gfree["WT"])
                qd = ve.last()
                V(lambda e: e.tensor_copy(XX, bm(cs("ident"), 4)), gfree["X"])
                V(lambda e: e.tensor_copy(YY, bm(cs("ident"), 4)))
                for s in range(7):
                    v = tt(ML, LT, bm(cs("gm", 128 * s), 4), ALU.mult, pe.last())
                    for m in range(4):
                        t = mm(PS[3][:, m * 128:(m + 1) * 128], ML[:, m, :], XX[:, m, :], v, bfree[3], inc=(m == 3))
                    a = act(PP, grp(3), ACT.Copy, t)
                    bfree[3] = a
                    if s % 2 == 0:
                        fill(1)
                    for m in range(4):
                        if s < 6:
                            mm(PS[4][:, m * 128:(m + 1) * 128], YY[:, m, :], PP[:, m, :], a, bfree[4])
                        t = mm(PS[5][:, m * 128:(m + 1) * 128], PP[:, m, :], YY[:, m, :], a, bfree[5], inc=(m == 3))
                    if s < 6:
                        bfree[4] = tt(XX, XX, grp(4), ALU.subtract, t)
                    bfree[5] = tt(YY, YY, grp(5), ALU.subtract, t)
                y = ve.last()
                gfree["LT"] = ve.last()
                gfree["ML"] = pe.last()
                for m in range(4):
                    t = mm(PS[3][:, m * 128:(m + 1) * 128], YY[:, m, :], VB[:, m, :], y, vt, bfree[3], inc=(m == 3))
                gfree["VB"] = t
                if c == 0:
                    u = act(UU, grp(3), ACT.Copy, t, gfree["U"])
                    bfree[3] = u
                    fill(1)
                    for m in range(4):
                        t = mm(PS[4][:, m * 128:(m + 1) * 128], KBE[:, m, :], UU[:, m, :], u, kt, bfree[4], inc=(m == 3))
                    gfree["KBE"] = t
                    bfree[4] = act(SS, grp(4), ACT.Copy, t, gfree["S"])
                    ss_tok[0] = bfree[4]
                else:
                    for m in range(4):
                        t2 = mm(PS[4][:, m * 128:(m + 1) * 128], KBE[:, m, :], YY[:, m, :], kt, bfree[4], inc=(m == 3))
                    gfree["KBE"] = t2
                    w = act(PP, grp(4), ACT.Copy, t2)
                    bfree[4] = w
                    fill(1)
                    for m in range(4):
                        t2 = mm(PS[5][:, m * 128:(m + 1) * 128], PP[:, m, :], SS[:, m, :], w, ss_tok[0], bfree[5], inc=(m == 3))
                    a = act(UU, grp(3), ACT.Copy, t, gfree["U"])
                    bfree[3] = a
                    u = tt(UU, UU, grp(5), ALU.subtract, t2, a)
                    bfree[5] = u
                gfree["X"] = pe.last()
                fill(1)
                for m, h in enumerate(hs):
                    t = mm(PS[6][:, m * 128:(m + 1) * 128], UU[:, m, :], AT[:, m, :], u, gfree["D"], bfree[6], stop=(c == 0), inc=(m == 3))
                    if c == 1:
                        t = mm(PS[6][:, m * 128:(m + 1) * 128], SS[:, m, :], QD[:, m, :], qd, start=False, inc=(m == 3))
                gfree["U"] = gfree["AT"] = gfree["S"] = gfree["WT"] = t
                bfree[6] = act(QKV[:, 4 * g:4 * g + 4, tok], grp(6), ACT.Copy, t)

            ss_tok = [None]
            gfree = {n: None for n in ("D", "LT", "ML", "X", "AT", "VB", "KBE", "U", "S", "WT")}
            for g in range(2):
                for c in range(2):
                    gdn(g, c)
            fill_all()

            def resid(n0, first):
                def post(ps, t):
                    xv = X[:, 2 * n0:2 * n0 + 2, :]
                    if first:
                        return stt(xv, xv, ALPHA, ps, ALU.mult, ALU.add, t, pe_x[0])
                    return tt(xv, xv, ps, ALU.add, t)
                return post

            pe_x = [pe.last()]
            for n in range(4):
                fillers.append(product(("w_out_even", 0, 0, 256 * n), YHL, 0, resid(n, True), ga["ysplit"]))

            def rms_heads(src, nt, base, EPSN, ones, w, tmp, tmp2, gap=1):
                tk = []
                q = G(lambda e: e.tensor_tensor(tmp, src, src, ALU.mult), w)
                for m in range(0, nt, 2):
                    b = 3 + (m // 2) % 4
                    for i in range(2):
                        t = mm(PS[b][:, i * T:(i + 1) * T], ones, tmp[:, m + i, :], q, bfree[b], inc=(i == 1))
                    bfree[b] = act(tmp2[:, m:m + 2, :], PS[b][:, :].rearrange("p (a b) -> p a b", a=2), ACT.Ln, t,
                                   scale=base, bias=EPSC[EPSN])
                return act(tmp2, tmp2, ACT.Exp, scale=-0.5)

            OT = QKV[:, 0:8, :]
            RS = view(10036, 4, T)
            SQ3 = view(11060, 4, T)
            ac.do(lambda e: e.preload_act_table_set("natural_log_exp_and_others"), inc=False)
            fill(2)
            for g in range(2):
                o = OT[:, 4 * g:4 * g + 4, :]
                a = rms_heads(o, 4, 1.0 / 128, "1e-5", cs("ones"), [ac.last(), ve.last(), pe.last()], SQ3, RS)
                stt(o, o, col("gdn_g"), RS, ALU.mult, ALU.mult, a)
                fill(2)
            ys = []

            def zb_post(n):
                def post(ps, t):
                    a = act(ZB[:, :, :], ps, ACT.Silu, t, ve.last())
                    v = tt(ZB, ZB, OT[:, 2 * n:2 * n + 2, :], ALU.mult, a)
                    ys.extend(split_act(YHL, 8 + 2 * n, 2, ZB, v))
                    return a
                return post

            ZB = view(9012, 2, T)
            for n in range(4):
                run(product(("w_in_even", 0, 0, 7168 + 256 * n), XHL, 0, zb_post(n), xs))
                fill(1)
            fill_all()
            for n in range(4):
                run(product(("w_out_even", 0, 8, 256 * n), YHL, 8, resid(n, False), ys))

            def sum_channels(src, b, ones, *w):
                red = view(6656, 1, T)
                v = V(lambda e: e.tensor_reduce(red[:, 0, :], src.rearrange("p k t -> p t k"), AX.X, ALU.add), *w, pe.last())
                return mm(PS[b][:, 0:T], ones, red[:, 0, :], v, bfree[b], inc=True)

            def stat(src, sq, eps, fillf, mean=True):
                pass

            NX, NQ = view(0, 8, T), view(2048, 8, T)
            NR_ = view(4096, 1, T)
            NMU = view(4352, 1, T)

            def layer_norm(src, dst, g, b, eps, fillf):
                fillf()
                t = sum_channels(src, 3, cs("ones"), ac.last())
                fillf()
                a = act(NMU[:, 0, :], PS[3][:, 0:T], ACT.Copy, t, ve.last(), scale=1.0 / 1024)
                bfree[3] = a
                v = tt(NX, src, bm(NMU[:, 0, :], 8), ALU.subtract, a)
                a = act(NQ, NX, ACT.Square, v)
                t = sum_channels(NQ, 4, cs("ones"), a)
                fillf()
                ac.do(lambda e: e.preload_act_table_set("natural_log_exp_and_others"), inc=False)
                a = act(NR_[:, 0, :], PS[4][:, 0:T], ACT.Ln, t, scale=1.0 / 1024, bias=EPSC[eps])
                bfree[4] = a
                a = act(NR_[:, 0, :], NR_[:, 0, :], ACT.Exp, scale=-0.5)
                v = tt(NX, NX, bm(NR_[:, 0, :], 8), ALU.mult, a)
                for k in range(8):
                    a = act(dst[:, k, :], NX[:, k, :], ACT.Identity, v, scale=g[:, k:k + 1], bias=b[:, k:k + 1])
                fillf()
                return a

            def rms_mod(g1, sh, hl, fillf):
                a = act(NQ, X[:, :, :], ACT.Square, ve.last())
                fillf()
                t = sum_channels(NQ, 3, cs("ones"), a)
                fillf()
                ac.do(lambda e: e.preload_act_table_set("natural_log_exp_and_others"), inc=False)
                a = act(NR_[:, 0, :], PS[3][:, 0:T], ACT.Ln, t, scale=1.0 / 1024, bias=EPSC["1e-6"])
                bfree[3] = a
                a = act(NR_[:, 0, :], NR_[:, 0, :], ACT.Exp, scale=-0.5)
                v = tt(NX, X[:, :, :], bm(NR_[:, 0, :], 8), ALU.mult, a)
                for k in range(8):
                    a = act(NX[:, k, :], NX[:, k, :], ACT.Identity, v, scale=g1[:, k:k + 1], bias=sh[:, k:k + 1])
                fillf()
                return split_act(hl, 0, 8, NX, a, pe.last())

            def f1():
                ada_fill(1)

            def pl_layer(i):
                a = layer_norm(X[:, :, :], X[:, :, :], col("ln_g", 8 * i, 8), col("ln_b", 8 * i, 8), "1e-5", f1)
                xs = split_act(XHL, 0, 8, X[:, :, :], a, pe.last())
                ph = split_act(YHL, 0, 2, PT[:, i, :, :], pe.last())
                PL = view(4608, 8, T)
                u = unit("w_pl", i, 0, 0)
                wh, wl = wparts(u, 2)
                for n in range(0, 8, 2):
                    b = take_bank()
                    for m in range(2):
                        for k in range(2):
                            s = slice((n + m) * 128, (n + m + 1) * 128)
                            t = three(PS[b][:, m * T:(m + 1) * T], (wh[:, k, s], wl[:, k, s]), (YH[:, k, :], YL[:, k, :]),
                                      k == 0, k == 1, sp_tok.get(u), bfree[b], ph, inc=(k == 1))
                    bfree[b] = act(PL[:, n:n + 2, :], PS[b][:, :].rearrange("p (a b) -> p a b", a=2), ACT.Copy, t)
                release(u, t)

                def post_n(n):
                    def post(ps, t):
                        SG = view(6656, 2, T)
                        a = act(SG, ps, ACT.Sigmoid, t, ve.last())
                        tt(SG, SG, PL[:, 2 * n:2 * n + 2, :], ALU.mult, a)
                        tt(X[:, 2 * n:2 * n + 2, :], X[:, 2 * n:2 * n + 2, :], SG, ALU.add)
                        return a
                    return post

                for n in range(4):
                    run(product(("w_pl_gate", i, 0, 256 * n), XHL, 0, post_n(n), xs))
                return split_act(XHL, 0, 8, X[:, :, :], ve.last(), pe.last())

            xs = pl_layer(0)

            Hq, Hk, PR, SF, HT = [view(512 * i, 2, T) for i in range(5)]
            QL = [view(2560 + 1024 * i, 2, T) for i in range(2)]
            KL = [view(3072 + 1024 * i, 2, T) for i in range(2)]
            HV = view(4608, 2, T)
            ATT = [view(5120 + 768 * i, 6, 128) for i in range(2)]
            OH = view(6656, 16, T)
            HZ = view(10752, 4, T)
            HR = view(11776, 4, T)
            HQ = view(12800, 4, T)
            for i in range(2):
                t = G(lambda e, i=i: e.memset(QL[i], 0.0), ve.last(), ac.last())
                t = G(lambda e, i=i: e.memset(KL[i], 0.0))
            lt0 = t
            ys = []
            hz = {"z": [], "qf": None}

            def hg_pair(hp):
                tk = {}

                def q_post(ps, t):
                    a = act(HT, ps, ACT.Sigmoid, t, ve.last())
                    tk["q"] = tt(Hq, HT, ps, ALU.mult, a, t, pe.last())
                    return tk["q"]

                def f_post(ps, t):
                    a = act(HT, ps, ACT.Sigmoid, t, ve.last())
                    for m in range(2):
                        h = 2 * hp + m
                        ts(PR[:, m, :], HT[:, m, :], OLB[:, h:h + 1], LB[:, h:h + 1], ALU.mult, ALU.add, a, pe.last())
                    tk["f"] = ts(Hk, PR, -1.0, 1.0, ALU.mult, ALU.add)
                    V(lambda e: e.memset(SF, 1.0))
                    return a

                def v_post(ps, t):
                    tk["v"] = act(HV, ps, ACT.Copy, t, hz.get("pe"))
                    return tk["v"]

                run(product(("w_in_odd", 0, 0, 256 * hp), XHL, 0, q_post, xs))
                run(product(("w_in_odd", 0, 0, 2048 + 256 * hp), XHL, 0, f_post, xs))
                at = ATT[hp % 2]
                g = G(lambda e: e.memset(at, 0.0), hz.get("pe"))
                gen = product_tok(("w_in_odd", 0, 0, 4096 + 256 * hp), XHL, v_post, xs)
                genz = product(("w_in_odd", 0, 0, 6144 + 256 * hp), XHL, 0, z_post(hp), xs)
                atd = at.rearrange("p (m b) t -> p m b t", m=2)
                pend = []

                def level(lv):
                    if lv == -1:
                        ql, kl = Hq, Hk
                        v = tk["f"]
                    else:
                        w = 1 << lv
                        i = lv % 2
                        ql, kl = QL[i], KL[i]
                        nb = T // (2 * w)

                        def pairs(x):
                            return x.rearrange("p m (b r w) -> p (m b) r w", r=2, w=w)
                        tt(pairs(ql)[:, :, 1, :], pairs(Hq)[:, :, 1, :], pairs(PR)[:, :, 1, :], ALU.mult, lfree[i], lt0)
                        v = tt(pairs(kl)[:, :, 0, :], pairs(Hk)[:, :, 0, :], pairs(SF)[:, :, 0, :], ALU.mult, lfree[i])
                        if lv < 7:
                            tot = pairs(PR)[:, :, :, w - 1:w]
                            tmp = HT.rearrange("p m t -> p (m t)")[:, 0:4 * nb].rearrange("p (b r w) -> p b r w", r=2, w=1)
                            V(lambda e: e.tensor_copy(tmp, tot))
                            tt(pairs(PR)[:, :, 1, :], pairs(PR)[:, :, 1, :], tmp[:, :, 0, :].broadcast_to([128, 2 * nb, w]), ALU.mult)
                            tt(pairs(SF)[:, :, 0, :], pairs(SF)[:, :, 0, :], tmp[:, :, 1, :].broadcast_to([128, 2 * nb, w]), ALU.mult)
                    b = 3 + (lv + 1) % 4
                    if lv < 7:
                        for m in range(2):
                            for c in range(2):
                                s = slice(c * 128, (c + 1) * 128)
                                t = mm(PS[b][:, (m * 2 + c) * 128:(m * 2 + c + 1) * 128], kl[:, m, s], ql[:, m, s], v, tk["q"], bfree[b],
                                       inc=(m == 1 and c == 1))
                        mk = (cs("gm", 128 * lv) if lv >= 0 else cs("ident")).bitcast(i32)

                        def fin():
                            for m in range(2):
                                bfree[b] = V(lambda e, m=m: e.copy_predicated(at[:, 3 * m:3 * m + 2, :], bm(mk, 2),
                                             PS[b][:, m * 256:(m + 1) * 256].rearrange("p (c t) -> p c t", c=2)), t, g)
                    else:
                        for m in range(2):
                            t = mm(PS[b][:, m * 128:(m + 1) * 128], kl[:, m, 0:128], ql[:, m, 128:256], v, bfree[b], inc=(m == 1))

                        def fin():
                            bfree[b] = act(atd[:, :, 2, :], PS[b][:, 0:256].rearrange("p (m t) -> p m t", m=2), ACT.Copy, t, g)
                    if lv >= 0:
                        lfree[lv % 2] = t
                    return fin

                fin = None
                for lv in range(-1, 8):
                    f2 = level(lv)
                    if fin:
                        fin()
                    fin = f2
                    if lv == 0 or lv == 2:
                        next(gen)
                    if lv == 4 or lv == 6:
                        next(genz)
                fin()
                run(gen)
                run(genz)
                b = 3 + hp % 4
                for m in range(2):
                    h = slice(m * 128, (m + 1) * 128)
                    mm(PS[b][:, m * T:m * T + 128], HV[:, 0, h], at[:, 3 * m, :], tk["v"], ve.last(), ac.last(), bfree[b])
                    mm(PS[b][:, m * T + 128:m * T + 256], HV[:, 0, h], at[:, 3 * m + 2, :], stop=False)
                    t = mm(PS[b][:, m * T + 128:m * T + 256], HV[:, 1, h], at[:, 3 * m + 1, :], start=False, inc=(m == 1))
                hz["pe"] = t
                bfree[b] = act(OH[:, 2 * hp:2 * hp + 2, :], PS[b][:, :].rearrange("p (a b) -> p a b", a=2), ACT.Copy, t)

            def z_post(hp):
                i = 2 * (hp % 2)

                def post(ps, t):
                    a = act(HZ[:, i:i + 2, :], ps, ACT.Sigmoid, t, ve.last())
                    return tt(HZ[:, i:i + 2, :], HZ[:, i:i + 2, :], ps, ALU.mult, a)
                return post

            lfree = [None, None]
            for hp in range(8):
                hg_pair(hp)
                if hp % 2:
                    o = OH[:, 2 * hp - 2:2 * hp + 2, :]
                    ac.do(lambda e: e.preload_act_table_set("natural_log_exp_and_others"), inc=False)
                    a = rms_heads(o, 4, 1.0 / 128, "1e-5", cs("ones"), [ac.last(), ve.last(), pe.last()], HQ, HR)
                    stt(o, o, col("hgrn_g"), HR, ALU.mult, ALU.mult, a)
                    v = tt(o, o, HZ, ALU.mult)
                    ys.extend(split_act(YHL, 2 * hp - 2, 4, o, v, pe.last()))
            for n in range(4):
                pe_x = [None]
                run(product(("w_out_odd", 0, 0, 256 * n), YHL, 0, resid(n, True), ys))
                run(product(("w_out_odd", 0, 8, 256 * n), YHL, 8, resid(n, False), ys))
            xs = pl_layer(1)
            while ada["n"] < 24:
                ada_fill(1)

            def mods(i):
                tt(MOD[:, 48 * i:48 * i + 48], PS[7][:, 48 * i:48 * i + 48], col("ada_b", 48 * i, 48), ALU.add, ada["tok"])
                ada["free"] = ve.last()
                for q, nm in ((1, "mix_g"), (4, "mlp_g")):
                    m = MOD[:, 48 * i + 8 * q:48 * i + 8 * q + 8]
                    stt(m, m, 1.0, col(nm, 8 * i, 8), ALU.add, ALU.mult)
                ac.wait([ve.last()])

            def mod(i, q):
                return MOD[:, 48 * i + 8 * q:48 * i + 8 * q + 8]

            def gated(i, q, n0):
                def post(ps, t):
                    for m in range(2):
                        k = 2 * n0 + m
                        v = stt(X[:, k, :], ps[:, m, :], mod(i, q)[:, k:k + 1], X[:, k, :], ALU.mult, ALU.add, t)
                    return v
                return post

            def mlp(i, fillf):
                xs = rms_mod(mod(i, 4), mod(i, 3), XHL, fillf)
                RL = view(7168, 2, T)
                hs = {}

                def w1_post(n):
                    def post(ps, t):
                        o = 8 * ((n // 4) % 2) + 2 * (n % 4)
                        a = act(RL, ps, ACT.Relu, t, ve.last())
                        v = tt(RL, RL, RL, ALU.mult, a)
                        hs.setdefault(n // 4, []).extend(split_act(YHL, o, 2, RL, v, hfree.get(n // 4 - 2)))
                        return a
                    return post

                hfree = {}

                def w2(g):
                    for n in range(4):
                        run(product(("mlp_w2", i, 8 * g, 256 * n), YHL, 8 * (g % 2), gated(i, 5, n), hs[g]))
                    hfree[g] = pe.last()

                for g in range(4):
                    for n in range(4 * g, 4 * g + 4):
                        run(product(("mlp_w1", i, 0, 256 * n), XHL, 0, w1_post(n), xs))
                    if g:
                        w2(g - 1)
                w2(3)

            mods(0)
            xs = rms_mod(mod(0, 1), mod(0, 0), XHL, f1)
            U = [view(7168 + 288 * i, 1, 286) for i in range(2)]
            CO = view(7744, 8, T)
            zu = [G(lambda e, i=i: e.memset(U[i][:, :, 0:30], 0.0), ve.last(), ac.last()) for i in range(2)]
            SGC = view(9792, 1, T)
            AV = view(10048, 1, T)

            def glu_post(j):
                def post(ps, t):
                    u = U[j % 2][:, 0, :]
                    a = act(SGC[:, 0, :], ps[:, 1, :], ACT.Sigmoid, t, ve.last(), bias=col("b_in", 8 + j))
                    v = stt(u[:, 30:286], ps[:, 0, :], col("b_in", j), SGC[:, 0, :], ALU.add, ALU.mult, a, zu)
                    ts(CO[:, j, :], u[:, 0:256], col("dw", 31 * j), col("dw_b", j), ALU.mult, ALU.add)
                    for q in range(1, 31):
                        stt(CO[:, j, :], u[:, q:256 + q], col("dw", 31 * j + q), CO[:, j, :], ALU.mult, ALU.add)
                    return [a, v]
                return post

            for j in range(8):
                run(product(("conv_w_in", 0, 0, (128 * j, 1024 + 128 * j)), XHL, 0, glu_post(j), xs))
            a = layer_norm(CO, CO, col("cln_g", 0, 8), col("cln_b", 0, 8), "1e-6", f1)
            a = act(CO, CO, ACT.Silu)
            xs = split_act(XHL, 0, 8, CO, a, pe.last())

            def cout_post(n):
                def post(ps, t):
                    for m in range(2):
                        k = 2 * n + m
                        ts(AV[:, 0, :], ps[:, m, :], col("b_out", k), mod(0, 2)[:, k:k + 1], ALU.add, ALU.mult, t)
                        v = tt(X[:, k, :], X[:, k, :], AV[:, 0, :], ALU.add)
                    return v
                return post

            for n in range(4):
                run(product(("conv_w_out", 0, 0, 256 * n), XHL, 0, cout_post(n), xs))
            mlp(0, f1)
            while ada["n"] < 48:
                ada_fill(1)
            mods(1)

            xs = rms_mod(mod(1, 1), mod(1, 0), XHL, f1)
            AQ = view(4608, 16, T)
            AV2 = view(8704, 2, 1024)
            qt = {}

            def qk_post(n):
                def post(ps, t):
                    qt[n] = act(AQ[:, 2 * n:2 * n + 2, :], ps, ACT.Copy, t)
                    return qt[n]
                return post

            def av_post(n):
                def post(ps, t):
                    qt["v"] = act(AV2[:, :, 256 * n:256 * n + 256], ps, ACT.Copy, t)
                    return qt["v"]
                return post

            for n in range(8):
                run(product(("attn_w_qkv", 0, 0, 256 * n), XHL, 0, qk_post(n), xs))
            ac.do(lambda e: e.preload_act_table_set("natural_log_exp_and_others"), inc=False)
            AS, AR = view(0, 4, T), view(1024, 4, T)
            gens = [product_tok(("attn_w_qkv", 0, 0, 2048 + 256 * n), XHL, av_post(n), xs) for n in range(4)]
            fillers.extend(gens)
            for g in range(4):
                o = AQ[:, 4 * g:4 * g + 4, :]
                fill(1)
                a = rms_heads(o, 4, 1.0 / 64, "1e-6", cs("ones64"), [ac.last(), ve.last(), pe.last()], AS, AR)
                stt(o, o, col("qn_g" if g < 2 else "kn_g"), AR, ALU.mult, ALU.mult, a)
            fill_all()
            nt = ve.last()
            SCB = [view(384 * i, 1, 384) for i in range(4)]
            PTB = [view(1536 + 384 * i, 1, 384) for i in range(4)]
            AO = view(3072, 2, T)
            mxs = [SM[:, 200 + 4 * i:204 + 4 * i] for i in range(4)]
            AOF = view(10752, 8, T)
            sct = {}

            def scores(h):
                i = h % 4
                kt, p0 = h // 2, 64 * (h % 2)
                q, k = AQ[p0:p0 + 64, kt, :], AQ[p0:p0 + 64, 8 + kt, :]
                b = 3 + h % 2
                mm(PS[b][:, 0:128], q[:, 0:128], k[:, 0:128], nt, bfree[b])
                t = mm(PS[b][:, 128:384], q[:, 128:256], k, inc=True)
                sc = SCB[i][:, 0, :]
                slope = float(2.0 ** (-0.5 * (h + 1)))
                bfree[b] = stt(sc, cs("dist", 0, 384), slope * 8.0, PS[b][:, 0:384], ALU.mult, ALU.add, t, sct.get(("x", i)))
                mx = mxs[i]
                V(lambda e: e.tensor_reduce(mx[:, 0:1], sc[:, 0:128], AX.X, ALU.max))
                V(lambda e: e.tensor_reduce(mx[:, 1:2], sc[:, 128:384], AX.X, ALU.max))
                v = ts(mx[:, 0:2], mx[:, 0:2], -0.125, None, ALU.mult, None)
                act(sc[:, 0:128], sc[:, 0:128], ACT.Exp, v, bias=mx[:, 0:1], scale=0.125, accum_out=mx[:, 2:3])
                a = act(sc[:, 128:384], sc[:, 128:384], ACT.Exp, bias=mx[:, 1:2], scale=0.125, accum_out=mx[:, 3:4])
                V(lambda e: e.reciprocal(mx[:, 2:4], mx[:, 2:4]), a)
                ts(sc[:, 0:128], sc[:, 0:128], mx[:, 2:3], None, ALU.mult, None)
                sct[h] = ts(sc[:, 128:384], sc[:, 128:384], mx[:, 3:4], None, ALU.mult, None)

            def values(h):
                i = h % 4
                sc, pt = SCB[i][:, 0, :], PTB[i][:, 0, :]
                for q in range(3):
                    t = tr(PS[5][:, q * 128:(q + 1) * 128], sc[:, q * 128:(q + 1) * 128], sct[h], bfree[5], inc=(q == 2))
                sct[("x", i)] = t
                a = act(pt, PS[5][:, 0:384], ACT.Copy, t, sct.get(("p", i)))
                bfree[5] = a
                p0 = 64 * (h % 2)
                hc = slice(64 * h, 64 * h + 64)
                o = PS[6][p0:p0 + 64, :]
                mm(o[:, 0:128], AV2[:, 0, hc], pt[:, 0:128], a, bfree[6] if p0 == 0 else bf6[0], qt["v"])
                mm(o[:, 128:256], AV2[:, 0, hc], pt[:, 128:256], stop=False)
                t = mm(o[:, 128:256], AV2[:, 1, hc], pt[:, 256:384], start=False, inc=True)
                sct[("p", i)] = t
                if p0 == 64:
                    bf6[0] = bfree[6] = act(AOF[:, h // 2, :], PS[6][:, 0:T], ACT.Copy, t)

            bf6 = [None]
            scores(0)
            scores(1)
            for h in range(16):
                if h + 2 < 16:
                    scores(h + 2)
                values(h)
            ao = split_act(YHL, 0, 8, AOF, ac.last(), pe.last())
            for n in range(4):
                run(product(("attn_w_o", 0, 0, 256 * n), YHL, 0, gated(1, 2, n), ao))
            mlp(1, lambda: None)

            sp.wait([ve.last()])
            sp.q.append((lambda e: e.dma_start(out, X[:, :, :]).then_inc(s_out, 16), False))
            sp.q.append((s_out, 16))
            if plan:
                assert st["used"] == len(plan) == st["load"], (st, len(plan))
            return pe, ve, ac, gp, sp, loads

        ctx_rw = sb("RW", [8, 4, T])
        EP = sb("EP", [128, 4])
        EPSC = {"1e-6": EP[:, 0:1], "1e-5": EP[:, 1:2], "lnq": EP[:, 2:3]}
        EPSV = [(EP[:, 0:1], 1e-6), (EP[:, 1:2], 1e-5), (EP[:, 2:3], float(np.log(128.0 ** -0.5)))]
        specs = []
        pe, ve, ac, gp, sp, loads = emit(plan, specs)
        if not plan:
            return specs
        block = ctx.enter_context(nc.Block())

        @block.sync
        def _(eng):
            loads(eng)
            sp.play(eng)

        @block.gpsimd
        def _(eng):
            gp.play(eng)

        @block.scalar
        def _(eng):
            ac.play(eng)

        @block.vector
        def _(eng):
            ve.play(eng)

        @block.tensor
        def _(eng):
            pe.play(eng)
    return specs


def _tiles(v):
    import numpy as _np
    return _np.ascontiguousarray(v.reshape(-1, 128).T)


def kernel(**inputs):
    import numpy as _np
    import concourse.bacc as _bacc
    from concourse import mybir as _mybir
    from concourse.bass_utils import run_bass_kernel_spmd as _run

    a = {k: _np.asarray(v) for k, v in inputs.items()}
    parts = {
        "conv_a_w": a["conv_a_w"][0].reshape(3, 8, 128).transpose(2, 1, 0).reshape(128, 24),
        "conv_b_w": a["conv_b_w"][0].reshape(4, 24, 128).transpose(2, 1, 0).reshape(128, 96),
        "gdn_g": _tiles(a["gdn_norm_g"]), "lb": _tiles(a["lower_bounds"]), "hgrn_g": _tiles(a["hgrn_norm_g"]),
        "ln_g": _tiles(a["ln_g"]), "ln_b": _tiles(a["ln_b"]), "c": _tiles(a["c_2"]), "ada_b": _tiles(a["ada_b_2"]),
        "mix_g": _tiles(a["mix_norm_g_2"]), "mlp_g": _tiles(a["mlp_norm_g_2"]), "b_in": _tiles(a["conv_b_in_2"]),
        "dw": a["conv_dw_2"][0].reshape(31, 8, 128).transpose(2, 1, 0).reshape(128, 248),
        "dw_b": _tiles(a["conv_dw_b_2"]), "cln_g": _tiles(a["conv_ln_g_2"]), "cln_b": _tiles(a["conv_ln_b_2"]),
        "b_out": _tiles(a["conv_b_out_2"]),
        "qn_g": _np.concatenate([a["attn_q_norm_g_2"][0]] * 2).reshape(128, 1),
        "kn_g": _np.concatenate([a["attn_k_norm_g_2"][0]] * 2).reshape(128, 1),
        "heads": _np.zeros((128, 2), _np.float32),
        "wbg": a["w_in_even"][0][:, 8192:8208].reshape(8, 128, 16).transpose(1, 0, 2).reshape(128, 128),
    }
    cols = _np.ascontiguousarray(_np.concatenate([parts[n] for n, _ in COLS], 1))
    rows = _np.ascontiguousarray(_np.stack([a["a_log"][0], a["dt_bias"][0]], 1))
    xT = _np.ascontiguousarray(a["x"][0].T.reshape(8, 128, T).transpose(1, 0, 2))
    pT = _np.ascontiguousarray(a["p"][:, 0].transpose(0, 2, 1).reshape(2, 2, 128, T).transpose(0, 2, 1, 3))
    cst = constants()
    names = {n: (n if n in a else n + "_2") for n in
             ("w_in_even", "w_out_even", "w_in_odd", "w_out_odd", "w_pl", "w_pl_gate", "ada_w", "conv_w_in", "conv_w_out",
              "attn_w_qkv", "attn_w_o", "mlp_w1", "mlp_w2")}
    f = _mybir.dt.float32

    def build(plan):
        nc = _bacc.Bacc("TRN2", target_bir_lowering=False, num_devices=1)

        def dram(name, shape, dt=f, kind="ExternalInput"):
            return nc.dram_tensor(name, shape, dt, kind=kind).ap()

        specs = program(nc, dram("xT", (128, 8, T)), dram("wst", (max(len(plan), 1), 128, 2048)), dram("cols", cols.shape),
                        dram("rows", rows.shape), dram("pT", pT.shape), dram("cst", cst.shape),
                        dram("outT", (128, 8, T), kind="ExternalOutput"), plan)
        return nc, specs

    plan = build([])[1]
    wst = _np.empty((len(plan), 128, 2048), _np.float32)
    for u, (name, layer, k0, c0) in enumerate(plan):
        w = a[names[name]][layer]
        if name == "w_pl":
            wst[u] = w.reshape(2, 128, 1024).transpose(1, 0, 2).reshape(128, 2048)
            continue
        w = w[128 * k0:128 * k0 + 1024]
        if isinstance(c0, tuple):
            w = _np.concatenate([w[:, c:c + 128] for c in c0], 1)
        else:
            w = w[:, c0:c0 + 256]
        wst[u] = w.reshape(8, 128, 256).transpose(1, 0, 2).reshape(128, 2048)
    nc, _ = build(plan)
    r = _run(nc, [{"xT": xT, "wst": wst, "cols": cols, "rows": rows, "pT": pT, "cst": cst}], core_ids=[0])
    o = _np.asarray(r.results[0]["outT"])
    return _np.ascontiguousarray(o.transpose(2, 1, 0).reshape(1, T, 1024))
```

```python
import numpy as np
import concourse.bass as bass
from concourse import mybir
from contextlib import ExitStack

T = 256
NR, NS = 3, 3
BW = 16448
ALPHA = 4.0 ** 0.25
NEG = -1.0e30


COLS = [("conv_a_w", 24), ("conv_b_w", 96), ("gdn_g", 1), ("lb", 32), ("hgrn_g", 1), ("ln_g", 16), ("ln_b", 16),
        ("ada_b", 96), ("mix_g", 16), ("mlp_g", 16), ("b_in", 16), ("dw", 248), ("dw_b", 8),
        ("cln_g", 8), ("cln_b", 8), ("b_out", 8), ("qn_g", 1), ("kn_g", 1), ("wbg", 128)]
COL0 = {}
_n = 0
for _name, _k in COLS:
    COL0[_name] = (_n, _k)
    _n += _k
NCOL = _n

CST = [("ident", 128), ("ones", 128), ("neg", 128), ("gm", 896)]
CST0 = {}
_n = 0
for _name, _k in CST:
    CST0[_name] = (_n, _k)
    _n += _k
NCST = _n


def constants():
    j = np.arange(128)[:, None]
    i = np.arange(128)[None, :]
    f = np.zeros((128, NCST), np.float32)

    def put(name, v):
        a, n = CST0[name]
        f[:v.shape[0], a:a + n] = v

    put("ident", (i == j).astype(np.float32))
    put("ones", np.ones((128, 128), np.float32))
    put("neg", np.where(i >= j, 0.0, NEG).astype(np.float32))
    lv = [((i // (2 * s) == j // (2 * s)) & ((i // s) % 2 == 1) & ((j // s) % 2 == 0)) for s in (1, 2, 4, 8, 16, 32, 64)]
    put("gm", np.concatenate(lv, 1).astype(np.float32))
    k = np.arange(256)[None, :]
    d0 = np.where(j >= i, -(j - i).astype(np.float32), np.float32(NEG))
    d1 = np.where(j + 128 >= k, -(j + 128 - k).astype(np.float32), np.float32(NEG))
    late = np.concatenate([i // 64 == j // 64, d0, d1], 1).astype(np.float32)
    return f, late


class Lane:

    def __init__(self, sem):
        self.sem, self.q, self.n, self.seen = sem, [], 0, {}

    def wait(self, toks):
        for t in toks:
            if t is None:
                continue
            if isinstance(t, list):
                self.wait(t)
                continue
            sem, v = t
            if self.seen.get(id(sem), 0) < v:
                self.seen[id(sem)] = v
                self.q.append((sem, v))

    def last(self):
        return (self.sem, self.n) if self.n else None

    def do(self, fn, *toks, inc=True):
        self.wait(toks)
        self.q.append((fn, inc))
        if inc:
            self.n += 1
        return (self.sem, self.n)

    def play(self, eng):
        for a, b in self.q:
            if callable(a):
                ins = a(eng)
                if b:
                    ins.then_inc(self.sem, 1)
            else:
                eng.wait_ge(a, b)


def program(nc, xT, wst, cols, rows, crow, pT, cst, late, out, plan):
    f32, fr, i32 = mybir.dt.float32, mybir.dt.float32r, mybir.dt.int32
    ALU, ACT, AX = mybir.AluOpType, mybir.ActivationFunctionType, mybir.AxisListType
    ctx = ExitStack()
    with ctx:
        def sb(name, shape, dt=f32):
            return ctx.enter_context(nc.sbuf_tensor(name, shape, dt))

        def sem(name):
            return ctx.enter_context(nc.semaphore(name))

        RAW = [sb(f"RAW{i}", [128, 2048]) for i in range(NR)]
        WH = [sb(f"WH{i}", [128, 2048], fr) for i in range(NS)]
        WL = [sb(f"WL{i}", [128, 2048], fr) for i in range(NS)]
        X = sb("X", [128, 8, T])
        XH = sb("XH", [128, 8, T], fr)
        XL = sb("XL", [128, 8, T], fr)
        YH = sb("YH", [128, 16, T], fr)
        YL = sb("YL", [128, 16, T], fr)
        C = sb("C", [128, NCOL])
        R8 = sb("R8", [8, 2])
        CB1 = sb("CB1", [128, 1024])
        K = sb("K", [128, NCST])
        MOD = sb("MOD", [128, 96])
        SM = sb("SM", [128, 256])
        BIG = sb("BIG", [128, BW])
        PS = [ctx.enter_context(nc.psum_tensor(f"PS{i}", [128, 512], f32)) for i in range(8)]

        s_pe, s_v, s_a, s_g = sem("s_pe"), sem("s_v"), sem("s_a"), sem("s_g")
        s_in, s_x, s_out = sem("s_in"), sem("s_x"), sem("s_out")
        s_p = [sem("s_p0"), sem("s_p1"), sem("s_late")]
        s_raw = [sem(f"s_raw{i}") for i in range(NR)]

        def col(name, i=0, n=1, p=128):
            a = COL0[name][0] + i
            return C[0:p, a:a + n]

        def cs(name, i=0, n=128, p=128):
            a = CST0[name][0] + i
            return K[0:p, a:a + n]

        def emit(plan, specs):
            pe, ve, ac, gp, sp = Lane(s_pe), Lane(s_v), Lane(s_a), Lane(s_g), Lane(s_out)

            def V(fn, *w, free=False):
                return ve.do(fn, *(w if free else (ve.last(), *w)))

            def G(fn, *w, free=False):
                return gp.do(fn, *(w if free else (gp.last(), *w)))

            def tt(o, a, b, op, *w, free=False, E=V):
                return E(lambda e: e.tensor_tensor(o, a, b, op), *w, free=free)

            def ts(o, a, s1, s2, op0, op1, *w, free=False, E=V):
                if op1 is None:
                    return E(lambda e: e.tensor_scalar(o, a, s1, None, op0), *w, free=free)
                return E(lambda e: e.tensor_scalar(o, a, s1, s2, op0, op1), *w, free=free)

            def stt(o, a, s, b, op0, op1, *w, free=False):
                return V(lambda e: e.scalar_tensor_tensor(out=o, in0=a, scalar=s, in1=b, op0=op0, op1=op1), *w, free=free)

            def act(o, a, f, *w, free=False, **kw):
                return ac.do(lambda e: e.activation(o, a, f, **kw), *(w if free else (ac.last(), *w)))

            def mm(o, l, r, *w, start=True, stop=True, inc=False):
                return pe.do(lambda e: e.matmul(o, l, r, start=start, stop=stop), *w, inc=inc)

            def tr(o, a, *w, inc=False):
                n = a.shape[0]
                return pe.do(lambda e: e.transpose(o, a, cs("ident", 0, n, n)), *w, inc=inc)

            s_xt = (s_x, 16)
            s_all = (s_in, 64)

            def loads(e):
                e.dma_start(X[:, :, :], xT).then_inc(s_x, 16)
                for o, i in ((C[:, :], cols), (R8[:, :], rows), (K[:, :], cst), (CB1[:, :], crow.broadcast_to([128, 1024]))):
                    e.dma_start(o, i).then_inc(s_in, 16)

            raw_free = {}
            slot_free = {}
            sp_tok = {}
            st = {"load": 0, "split": 0, "ns": 0, "used": 0}
            slot_of = {}

            def raw_ready(u):
                return (s_raw[u % NR], 16 * (u // NR + 1))

            def load_more():
                while st["load"] < len(plan) and (st["load"] < NR or (st["load"] - NR) in raw_free):
                    u = st["load"]
                    sp.wait([raw_free.get(u - NR)])
                    sp.q.append((lambda e, u=u: e.dma_start(RAW[u % NR][:, :], wst[u]).then_inc(s_raw[u % NR], 16), False))
                    st["load"] += 1

            def split_next():
                u = st["split"]
                if u >= len(plan):
                    return False
                if plan[u][0] == "ada_w":
                    load_more()
                    if u >= st["load"]:
                        return False
                    st["split"] += 1
                    ada_unit(u)
                    load_more()
                    return True
                n = st["ns"]
                if n >= NS and (n - NS) not in slot_free:
                    return False
                load_more()
                if u >= st["load"]:
                    return False
                s, free = n % NS, slot_free.get(n - NS)
                r = RAW[u % NR]
                a = act(WH[s][:, :], r[:, :], ACT.Copy, raw_ready(u), free, free=True)
                flush()
                late_lo.append((u, s, r, a, free))
                slot_of[u] = (s, n)
                st["ns"] += 1
                st["split"] += 1
                if st["used"] + 1 >= u:
                    flush()
                return True

            late_lo = []

            def flush():
                if late_lo:
                    u, s, r, a, free = late_lo.pop()
                    b = tt(WL[s][:, :], r[:, :], WH[s][:, :].bitcast(f32), ALU.subtract, a, raw_ready(u), free, free=True)
                    sp_tok[u] = [a, b]
                    raw_free[u] = [a, b]
                    load_more()

            def ada_unit(u):
                n = plan[u][1] * 24 + plan[u][3] // 256
                for m in range(2):
                    w = RAW[u % NR][:, m * 1024:(m + 1) * 1024]
                    o = MOD[:, 2 * n + m:2 * n + m + 1]
                    t = V(lambda e, w=w, o=o: e.tensor_tensor_reduce(
                        out=w, in0=w, in1=CB1[:, :], scale=1.0, scalar=0.0, op0=ALU.mult, op1=ALU.add, accum_out=o),
                        raw_ready(u), cb_tok, free=True)
                raw_free[u] = [t]

            def pump():
                flush()
                load_more()
                while split_next():
                    pass

            def unit(*spec):
                specs.append(spec)
                u = st["used"]
                st["used"] += 1
                if u < len(plan):
                    assert plan[u] == spec, (u, plan[u], spec)
                    pump()
                    if spec[0] != "ada_w":
                        assert u in slot_of
                        if u not in sp_tok:
                            flush()
                return u

            bank = {"n": 0, "of": 3, "w": 0}
            bfree = [None] * 8

            def take_bank():
                b = bank["n"] % bank["of"]
                bank["n"] += 1
                return b

            def wparts(u, nk):
                s = slot_of[u][0] if u in slot_of else 0
                return (WH[s][:, :].rearrange("p (k n) -> p k n", k=nk), WL[s][:, :].rearrange("p (k n) -> p k n", k=nk))

            def release(u, tok):
                if u in slot_of:
                    slot_free[slot_of[u][1]] = tok
                    pump()

            def three(o, l, r, first, lastk, *w, inc=False):
                mm(o, l[0], r[0], *w, start=first, stop=False)
                mm(o, l[0], r[1], start=False, stop=False)
                return mm(o, l[1], r[0], start=False, stop=lastk, inc=inc)

            def work_bank():
                bank["w"] += 1
                return 3 + bank["w"] % 5

            def product(spec, act_hl, k0, post, *w, kw=None):
                u = unit(*spec)
                b = take_bank()
                h, l = act_hl
                wh, wl = wparts(u, 8)
                for n in range(2):
                    for k in range(8):
                        t = three(PS[b][:, n * T:(n + 1) * T],
                                  (wh[:, k, n * 128:(n + 1) * 128], wl[:, k, n * 128:(n + 1) * 128]),
                                  (h[:, k0 + k, :], l[:, k0 + k, :]), k == 0, k == 7, kw[k] if kw else None,
                                  *((sp_tok.get(u), bfree[b], *w) if n == 0 and k == 0 else ()), inc=(k == 7))
                    yield
                    flush()
                bfree[b] = post(PS[b][:, :].rearrange("p (n t) -> p n t", n=2), t)
                release(u, t)

            def product_tok(spec, act_hl, post, *w):
                u = unit(*spec)
                b = take_bank()
                h, l = act_hl
                wh, wl = wparts(u, 8)
                for n in range(2):
                    for k in range(8):
                        t = three(PS[b][:, n * T:(n + 1) * T],
                                  (h[:, k, n * 128:(n + 1) * 128], l[:, k, n * 128:(n + 1) * 128]),
                                  (wh[:, k, :], wl[:, k, :]), k == 0, k == 7,
                                  *((sp_tok.get(u), bfree[b], *w) if n == 0 and k == 0 else ()), inc=(k == 7))
                    yield
                    flush()
                bfree[b] = post(PS[b][:, :].rearrange("p (n t) -> p n t", n=2), t)
                release(u, t)

            def run(g):
                for _ in g:
                    pass

            ada = {"n": 0}

            def ada_fill(count):
                for _ in range(count):
                    n = ada["n"]
                    if n == 48:
                        return
                    ada["n"] += 1
                    unit("ada_w", n // 24, 0, (n % 24) * 256)

            fillers = []

            def fill(n=1, keep=0):
                while n > 0 and fillers:
                    try:
                        next(fillers[0])
                        n -= 1
                    except StopIteration:
                        fillers.pop(0)

            def fill_all():
                while fillers:
                    fill(1)

            load_more()
            XHL = (XH, XL)
            YHL = (YH, YL)

            def split_act(hl, lo, n, src, *w):
                a = act(hl[0][:, lo:lo + n, :], src, ACT.Copy, *w)
                b = tt(hl[1][:, lo:lo + n, :], src, hl[0][:, lo:lo + n, :].bitcast(f32), ALU.subtract, a, *w)
                return [a, b]

            cb_tok = act(CB1[:, :], CB1[:, :], ACT.Silu, s_all)
            xs = split_act(XHL, 0, 8, X[:, :, :], s_xt)

            def view(off, *shape):
                n = int(np.prod(shape))
                assert off + n <= BW, (off, shape)
                v = BIG[:, off:off + n]
                if len(shape) == 2:
                    v = v.rearrange("p (a b) -> p a b", a=shape[0])
                return v

            def bc(ap, n):
                return ap.unsqueeze(2).broadcast_to([ap.shape[0], ap.shape[1], n])

            def bm(ap, n):
                return ap.unsqueeze(1).broadcast_to([ap.shape[0], n, ap.shape[1]])

            lb = col("lb", 0, 32)
            LB, OLB = SM[:, 16:32], SM[:, 32:48]
            mx, e0, e1, sm = SM[:, 48:64], SM[:, 64:80], SM[:, 80:96], SM[:, 96:112]
            tt(mx, lb[:, 0:16], lb[:, 16:32], ALU.max, s_all)
            tt(e0, lb[:, 0:16], mx, ALU.subtract)
            t = tt(e1, lb[:, 16:32], mx, ALU.subtract)
            t = act(SM[:, 64:96], SM[:, 64:96], ACT.Exp, t)
            tt(sm, e0, e1, ALU.add, t)
            V(lambda e: e.reciprocal(sm, sm))
            tt(e0, e0, sm, ALU.mult)
            tt(e1, e1, sm, ALU.mult)
            tt(e1, e1, e0, ALU.add)
            tt(LB, e1, e0, ALU.subtract)
            ts(OLB, LB, -1.0, 1.0, ALU.mult, ALU.add)

            RW = ctx_rw
            beta, gc = RW[:, 0, :], RW[:, 1, :]
            aa, ab = view(0, 1, T)[0:8, 0, :], view(T, 1, T)[0:8, 0, :]
            wbg = col("wbg", 0, 128).rearrange("p (k n) -> p k n", k=8)
            for q in range(2):
                for k in range(8):
                    t = mm(PS[3][0:8, q * T:(q + 1) * T], wbg[:, k, q * 8:(q + 1) * 8], X[:, k, :], s_all, s_xt,
                           start=(k == 0), stop=(k == 7), inc=(k == 7))
            nea = SM[0:8, 120:121]
            act(nea, R8[:, 0:1], ACT.Exp, s_all)
            act(aa, PS[3][0:8, T:2 * T], ACT.Identity, t, bias=R8[:, 1:2])
            act(ab, aa, ACT.Abs)
            ac.do(lambda e: e.preload_act_table_set("natural_log_exp_and_others"), inc=False)
            act(ab, ab, ACT.Exp, scale=-1.0)
            t2 = act(ab, ab, ACT.Ln, bias=1.0)
            stt(aa, aa, 0.0, ab, ALU.max, ALU.add, t2)
            ts(aa, aa, nea, -1.0, ALU.mult, ALU.mult, t2)
            for c in range(2):
                V(lambda e, c=c: e.tensor_tensor_scan(gc[:, c * 128:(c + 1) * 128], cs("ones", 0, 128, 8),
                                                      aa[:, c * 128:(c + 1) * 128], 0.0, ALU.mult, ALU.add))
            gct = ve.last()
            bt = act(beta, PS[3][0:8, 0:T], ACT.Sigmoid)
            bfree[3] = [gct, bt]
            for c in range(2):
                tr(PS[3][:, c * 8:c * 8 + 8], gc[:, c * 128:(c + 1) * 128], gct, bt, bfree[3])
                t = tr(PS[3][:, 16 + c * 8:24 + c * 8], beta[:, c * 128:(c + 1) * 128], inc=True)
            GCT = SM[:, 128:144]
            BT = SM[:, 144:160]
            EG = SM[:, 160:176]
            KB = SM[:, 176:192]
            KD = SM[:, 192:200]
            V(lambda e: e.tensor_copy(SM[:, 128:160], PS[3][:, 0:32]), t)
            bfree[3] = ve.last()
            colt = ve.last()

            QKV = view(0, 24, T)
            CB = [view(6144 + 520 * i, 2, 260) for i in range(2)]
            AC = [view(7184 + 512 * i, 2, T) for i in range(2)]
            for i in range(2):
                t = G(lambda e, i=i: e.memset(CB[i][:, :, 0:4], 0.0))
            zt = t
            cb = {"n": 0, "silu": None, "free": [None, None], "acf": [None, None]}
            qkv_tok = {}

            def qkv_post(which, hp):
                def post(ps, t):
                    i = cb["n"] % 2
                    cb["n"] += 1
                    act(CB[i][:, :, 4:260], ps, ACT.Copy, t, cb["free"][i], zt)
                    for m in range(2):
                        j = which * 8 + 2 * hp + m
                        a = act(AC[i][:, m, :], ps[:, m, :], ACT.Copy, cb["acf"][i], scale=col("conv_b_w", j * 4 + 3))
                    if cb["silu"]:
                        cb["silu"]()
                    for q in range(3):
                        for m in range(2):
                            j = which * 8 + 2 * hp + m
                            v = stt(AC[i][:, m, :], CB[i][:, m, 1 + q:257 + q], col("conv_b_w", j * 4 + q), AC[i][:, m, :],
                                    ALU.mult, ALU.add, a)
                    cb["free"][i] = v
                    j = which * 8 + 2 * hp

                    def silu():
                        cb["acf"][i] = qkv_tok[(which, hp)] = act(QKV[:, j:j + 2, :], AC[i], ACT.Silu, v)
                    cb["silu"] = silu
                    return a
                return post

            for hp in range(4):
                for which in range(3):
                    run(product(("w_in_even", 0, 0, 4096 + 1024 * which + 256 * hp), XHL, 0, qkv_post(which, hp), xs))

            cb["silu"]()

            HS = view(14336, 1, T)
            CH = view(14592, 1, 260)
            AA = view(14852, 1, T)
            YA = view(15108, 2, T)
            ZA = view(15620, 2, T)
            zch = G(lambda e: e.memset(CH[:, :, 0:4], 0.0))
            ga = {"ya": None, "ysplit": [], "pend": None}

            def a_tile(j):
                def post1(ps, t):
                    a = act(HS[:, 0, :], ps[:, 0, :], ACT.Copy, t, ga.get("ch"))
                    v = tt(CH[:, 0, 4:260], ps[:, 1, :], HS[:, 0, :], ALU.mult, a, zch)
                    ga["ch"] = v
                    ts(AA[:, 0, :], CH[:, 0, 2:258], col("conv_a_w", j * 3), None, ALU.mult, None)
                    for q in range(1, 3):
                        stt(AA[:, 0, :], CH[:, 0, 2 + q:258 + q], col("conv_a_w", j * 3 + q), AA[:, 0, :], ALU.mult, ALU.add)
                    return [a, v]

                def post2(ps, t):
                    m = j % 2
                    v = tt(YA[:, m, :], ps[:, 0, :], AA[:, 0, :], ALU.mult, t, ga["ya"])
                    a = act(ZA[:, m, :], ps[:, 1, :], ACT.Copy, t, ga["ya"], v)
                    ga["pend"] = [v, a]
                    if m:
                        a_flush(j - 1)
                    return [v, a]

                yield from product(("w_in_even", 0, 0, (128 * j, 1024 + 128 * j)), XHL, 0, post1, xs)
                yield from product(("w_in_even", 0, 0, (2048 + 128 * j, 3072 + 128 * j)), XHL, 0, post2, xs)

            def a_flush(j):
                a = act(ZA, ZA, ACT.Silu, ga["pend"])
                v = tt(YA, YA, ZA, ALU.mult, a)
                ga["ysplit"] = split_act(YHL, j, 2, YA, v)
                ga["ya"] = ga["ysplit"]

            def chunk_buffers(g):
                return [view(6144 + 4096 * g + 512 * i, 4, 128) for i in range(8)]

            def l2(which, g):
                j = which * 8 + 4 * g
                src = QKV[:, j:j + 4, :]
                base = 6144 + 4096 * g + 2048 * which
                sq, rs = view(base, 4, T), view(base + 1024, 4, T)
                s = act(sq, src, ACT.Square, qkv_tok[(which, 2 * g)], qkv_tok[(which, 2 * g + 1)], ve.last())
                yield
                for m in range(4):
                    b = GB[g][m // 2]
                    t = mm(PS[b][:, (m % 2) * T:(m % 2 + 1) * T], cs("ones"), sq[:, m, :], s, bfree[b], inc=True)
                    if m % 2:
                        bfree[b] = act(rs[:, m - 1:m + 1, :], PS[b][:, :].rearrange("p (a b) -> p a b", a=2), ACT.Ln, t,
                                       bias=EPSC["1e-6"])
                if which == 0:
                    a = act(rs, rs, ACT.Exp, scale=-0.5, bias=EPSC["lnq"])
                else:
                    a = act(rs, rs, ACT.Exp, scale=-0.5)
                yield
                qk_tok[g] = tt(src, src, rs, ALU.mult, a)

            qk_tok = {}
            GB = [(2, 3, 4), (5, 6, 7)]
            epst = [G(lambda e, o=o, v=v: e.memset(o, v)) for o, v in EPSV]
            epst = epst[-1]
            ac.wait([epst])
            for j in range(8):
                fillers.append(a_tile(j))
            ac.do(lambda e: e.preload_act_table_set("natural_log_exp_and_others"), inc=False)
            act(EG, GCT, ACT.Exp, colt)
            kbt = tt(KB, BT, EG, ALU.mult, ac.last())

            def grp(b):
                return PS[b][:, :].rearrange("p (a b) -> p a b", a=4)

            def row(x, h):
                return cs("ident", h, 1, 8).broadcast_to([8, 128])

            def gdn(g, c):
                b0, b1, b2 = GB[g]
                DD, LT, ML, XX, YY, AT, SS, QD = chunk_buffers(g)
                PP, UU, VB, KBE = DD, LT, ML, XX
                hs = [4 * g + m for m in range(4)]
                tok = slice(c * 128, (c + 1) * 128)
                blk = [slice(m * 128, (m + 1) * 128) for m in range(4)]
                free = gfree[g]
                for m, h in enumerate(hs):
                    t = mm(PS[b0][:, blk[m]], row(gc, h), gc[:, tok], bfree[b0], inc=(m == 3))
                for m, h in enumerate(hs):
                    t2 = mm(PS[b1][:, blk[m]], row(beta, h), beta[:, tok], bfree[b1], inc=(m == 3))
                for m, h in enumerate(hs):
                    kT = QKV[:, 8 + h, tok]
                    t3 = mm(PS[b2][:, blk[m]], kT, kT, qk_tok[g], bfree[b2], inc=(m == 3))
                yield
                v = tt(DD, grp(b0), bc(GCT[:, c * 8 + 4 * g:c * 8 + 4 * g + 4], 128), ALU.subtract, t, free)
                kd = KD[:, 4 * g:4 * g + 4]
                if c == 0:
                    v = tt(kd, grp(b0)[:, :, 127], GCT[:, 4 * g:4 * g + 4], ALU.subtract)
                v = tt(DD, DD, bm(cs("neg"), 4), ALU.add)
                d = act(DD, DD, ACT.Exp, v)
                if c == 0:
                    kdt = act(kd, kd, ACT.Exp)
                    bfree[b0] = v
                else:
                    a = act(QD, grp(b0), ACT.Exp, t, v, free)
                    bfree[b0] = a
                tt(LT, DD, grp(b1), ALU.mult, t2, d, free)
                bfree[b1] = ve.last()
                bfree[b2] = tt(LT, LT, grp(b2), ALU.mult, t3)
                lt = ve.last()
                if c == 1:
                    qd = tt(QD, QD, QKV[:, 4 * g:4 * g + 4, tok], ALU.mult, a, qk_tok[g])
                for m, h in enumerate(hs):
                    t3 = mm(PS[b0][:, blk[m]], QKV[:, 8 + h, tok], QKV[:, h, tok], bfree[b0], inc=(m == 3))
                V(lambda e: e.tensor_copy(XX, bm(cs("ident"), 4)), free)
                V(lambda e: e.tensor_copy(YY, bm(cs("ident"), 4)))
                yield
                at = tt(AT, DD, grp(b0), ALU.mult, t3, free)
                bfree[b0] = at
                for s in range(7):
                    v = tt(ML, LT, bm(cs("gm", 128 * s), 4), ALU.mult, gml[g])
                    for m in range(4):
                        t = mm(PS[b0][:, blk[m]], ML[:, m, :], XX[:, m, :], v, bfree[b0], inc=(m == 3))
                    gml[g] = t
                    yield
                    a = act(PP, grp(b0), ACT.Copy, t, at)
                    bfree[b0] = a
                    for m in range(4):
                        if s < 6:
                            mm(PS[b1][:, blk[m]], YY[:, m, :], PP[:, m, :], a, bfree[b1])
                        t = mm(PS[b2][:, blk[m]], PP[:, m, :], YY[:, m, :], a, bfree[b2], inc=(m == 3))
                    yield
                    if s < 6:
                        bfree[b1] = tt(XX, XX, grp(b1), ALU.subtract, t)
                    bfree[b2] = tt(YY, YY, grp(b2), ALU.subtract, t)
                y = ve.last()
                for m, h in enumerate(hs):
                    tr(PS[b0][:, blk[m]], QKV[:, 8 + h, tok], bfree[b0], qk_tok[g])
                    t4 = tr(PS[b1][:, blk[m]], QKV[:, 16 + h, tok], bfree[b1], qkv_tok[(2, 2 * g)], qkv_tok[(2, 2 * g + 1)],
                            inc=(m == 3))
                yield
                vt = tt(VB, grp(b1), bc(BT[:, c * 8 + 4 * g:c * 8 + 4 * g + 4], 128), ALU.mult, t4, gml[g])
                bfree[b1] = vt
                if c == 0:
                    kt = tt(KBE, grp(b0), bc(kd, 128), ALU.mult, t4, kdt)
                else:
                    kt = tt(KBE, grp(b0), bc(KB[:, 8 + 4 * g:12 + 4 * g], 128), ALU.mult, t4, kbt)
                bfree[b0] = kt
                for m in range(4):
                    t = mm(PS[b2][:, blk[m]], YY[:, m, :], VB[:, m, :], y, vt, bfree[b2], inc=(m == 3))
                if c == 0:
                    yield
                    u = act(UU, grp(b2), ACT.Copy, t, y)
                    bfree[b2] = u
                    for m in range(4):
                        t = mm(PS[b1][:, blk[m]], KBE[:, m, :], UU[:, m, :], u, kt, bfree[b1], inc=(m == 3))
                    yield
                    bfree[b1] = ss_tok[g] = act(SS, grp(b1), ACT.Copy, t)
                else:
                    for m in range(4):
                        t2 = mm(PS[b0][:, blk[m]], KBE[:, m, :], YY[:, m, :], kt, bfree[b0], inc=(m == 3))
                    yield
                    w = act(PP, grp(b0), ACT.Copy, t2)
                    bfree[b0] = w
                    a = act(UU, grp(b2), ACT.Copy, t, y)
                    bfree[b2] = a
                    for m in range(4):
                        t2 = mm(PS[b1][:, blk[m]], PP[:, m, :], SS[:, m, :], w, ss_tok[g], bfree[b1], inc=(m == 3))
                    yield
                    u = tt(UU, UU, grp(b1), ALU.subtract, t2, a)
                    bfree[b1] = u
                for m, h in enumerate(hs):
                    t = mm(PS[b2][:, blk[m]], UU[:, m, :], AT[:, m, :], u, at, bfree[b2], stop=(c == 0), inc=(m == 3))
                    if c == 1:
                        t = mm(PS[b2][:, blk[m]], SS[:, m, :], QD[:, m, :], qd, start=False, inc=(m == 3))
                gfree[g] = [t]
                yield
                bfree[b2] = act(QKV[:, 4 * g:4 * g + 4, tok], grp(b2), ACT.Copy, t)

            ss_tok = [None, None]
            gfree = [None, None]
            gml = [None, None]
            pe_x = [None]

            def resid(n0, first, hook=None):
                def post(ps, t):
                    xv = X[:, 2 * n0:2 * n0 + 2, :]
                    if first:
                        v = stt(xv, xv, ALPHA, ps, ALU.mult, ALU.add, t, pe_x[0])
                    else:
                        v = tt(xv, xv, ps, ALU.add, t)
                    if hook:
                        hook(n0, v)
                    return v
                return post

            def group(g):
                yield from l2(0, g)
                yield from l2(1, g)
                for c in range(2):
                    yield from gdn(g, c)

            def w_out_a():
                for n in range(4):
                    yield from product(("w_out_even", 0, 0, 256 * n), YHL, 0, resid(n, True), ga["ysplit"])

            fillers.append(w_out_a())
            bank["of"], bank["n"] = 2, 0
            gens = [group(0), group(1)]
            rounds = 0
            while gens:
                for gen in list(gens):
                    try:
                        next(gen)
                    except StopIteration:
                        gens.remove(gen)
                fill(1)
                if rounds % 2 == 0 and ada["n"] < 24:
                    ada_fill(1)
                rounds += 1
            late_wait = [ve.last(), ac.last()]
            gp.wait(late_wait)
            bank["of"] = 3

            def rms_heads(src, nt, base, EPSN, ones, w, tmp, tmp2, gap=1):
                tk = []
                q = G(lambda e: e.tensor_tensor(tmp, src, src, ALU.mult), w)
                for m in range(0, nt, 2):
                    b = 3 + (m // 2) % 4
                    for i in range(2):
                        t = mm(PS[b][:, i * T:(i + 1) * T], ones, tmp[:, m + i, :], q, bfree[b], inc=(i == 1))
                    bfree[b] = act(tmp2[:, m:m + 2, :], PS[b][:, :].rearrange("p (a b) -> p a b", a=2), ACT.Ln, t,
                                   scale=base, bias=EPSC[EPSN])
                return act(tmp2, tmp2, ACT.Exp, scale=-0.5)

            OT = QKV[:, 0:8, :]
            RS = view(6144, 4, T)
            SQ3 = view(7168, 4, T)
            ac.do(lambda e: e.preload_act_table_set("natural_log_exp_and_others"), inc=False)
            for g in range(2):
                o = OT[:, 4 * g:4 * g + 4, :]
                a = rms_heads(o, 4, 1.0 / 128, "1e-5", cs("ones"), [ac.last(), ve.last(), pe.last()], SQ3, RS)
                stt(o, o, col("gdn_g"), RS, ALU.mult, ALU.mult, a)
                fill(1)
            ys = []
            ZB = [view(8192 + 512 * i, 2, T) for i in range(2)]

            def zb_post(n):
                def post(ps, t):
                    z = ZB[n % 2]
                    a = act(z, ps, ACT.Silu, t, ve.last())
                    v = tt(z, z, OT[:, 2 * n:2 * n + 2, :], ALU.mult, a)
                    ys.extend(split_act(YHL, 8 + 2 * n, 2, z, v))
                    return a
                return post

            for n in range(4):
                run(product(("w_in_even", 0, 0, 7168 + 256 * n), XHL, 0, zb_post(n), xs))
                fill(1)
            fill_all()

            PTB = view(14336, 2, T)
            LATE = view(14848, 1, 512)[:, 0, :]
            ldt = [ve.last(), ac.last()]
            gp.do(lambda e: e.dma_start(PTB, pT[0]).then_inc(s_p[0], 16), ldt, inc=False)
            gp.do(lambda e: e.dma_start(LATE, late).then_inc(s_p[2], 16), inc=False)

            XC = view(0, 8, T)
            SQP = [view(2048 + 512 * i, 2, T) for i in range(2)]
            ACC = view(3072, 2, T)
            NRS, NMU = view(3584, 1, T)[:, 0, :], view(3840, 1, T)[:, 0, :]
            PL = view(4096, 8, T)
            SG = [view(6144 + 512 * i, 2, T) for i in range(2)]
            hk = {}

            def add_pairs(n, src, prev, *w):
                if n == 0:
                    return None
                if n == 1:
                    return tt(ACC, prev, src, ALU.add, *w, hk.get("acc"))
                return tt(ACC, ACC, src, ALU.add, *w)

            def hook_mean(src):
                def hook(n, t):
                    hk["sum"] = add_pairs(n, src[:, 2 * n:2 * n + 2, :], src[:, 0:2, :], t)
                return hook

            def square(n, src, *w):
                a = act(SQP[n % 2], src[:, 2 * n:2 * n + 2, :], ACT.Square, *w, hk.get(("sq", n % 2)))
                return a

            def hook_sq(src):
                def hook(n, t):
                    a = square(n, src, t)
                    hk["sum"] = v = add_pairs(n, SQP[n % 2], SQP[0], a)
                    if n:
                        hk[("sq", n % 2)] = v
                        if n == 1:
                            hk[("sq", 0)] = v
                return hook

            def channel_sum():
                b = work_bank()
                mm(PS[b][:, 0:T], cs("ones"), ACC[:, 0, :], hk["sum"], bfree[b], stop=False)
                t = hk["acc"] = mm(PS[b][:, 0:T], cs("ones"), ACC[:, 1, :], start=False, inc=True)
                return b, t

            def rstd(eps):
                b, t = channel_sum()
                ac.do(lambda e: e.preload_act_table_set("natural_log_exp_and_others"), inc=False)
                bfree[b] = act(NRS, PS[b][:, 0:T], ACT.Ln, t, ve.last(), scale=1.0 / 1024, bias=EPSC[eps])
                return act(NRS, NRS, ACT.Exp, scale=-0.5)

            def layer_norm(src, eps, mid):
                b, t = channel_sum()
                a = act(NMU, PS[b][:, 0:T], ACT.Copy, t, ve.last(), scale=1.0 / 1024)
                bfree[b] = a
                mid()
                for n in range(5):
                    if n < 4:
                        v = tt(XC[:, 2 * n:2 * n + 2, :], src[:, 2 * n:2 * n + 2, :], bm(NMU, 2), ALU.subtract, a)
                    if n > 0:
                        m = n - 1
                        hk["sum"] = s = add_pairs(m, SQP[m % 2], SQP[0], pq)
                        if m:
                            hk[("sq", m % 2)] = s
                            if m == 1:
                                hk[("sq", 0)] = s
                    if n < 4:
                        pq = square(n, XC, v)
                a = rstd(eps)
                mid()
                for n in range(4):
                    yield n, tt(XC[:, 2 * n:2 * n + 2, :], XC[:, 2 * n:2 * n + 2, :], bm(NRS, 2), ALU.mult, a)

            def rms_mod(g1, sh, hl):
                a = rstd("1e-6")
                out = []
                old = pe.last()
                for k in range(8):
                    v = stt(XC[:, k, :], X[:, k, :], g1[:, k:k + 1], NRS, ALU.mult, ALU.mult, a)
                    h = act(hl[0][:, k, :], XC[:, k, :], ACT.Identity, v, old, bias=sh[:, k:k + 1])
                    out.append([h, stt(hl[1][:, k, :], XC[:, k, :], sh[:, k:k + 1], hl[0][:, k, :].bitcast(f32),
                                       ALU.add, ALU.subtract, h)])
                return out

            def pl_layer(i, hook):
                ph = split_act(YHL, 0, 2, PTB, (s_p[i], 16), pe.last())
                if i == 0:
                    gp.do(lambda e: e.dma_start(PTB, pT[1]).then_inc(s_p[1], 16), ph, inc=False)
                u = unit("w_pl", i, 0, 0)
                wh, wl = wparts(u, 2)
                pln = iter((0, 2, 4, 6))
                plt = {}

                def mid():
                    for n in (next(pln), next(pln)):
                        b = take_bank()
                        for m in range(2):
                            for k in range(2):
                                s = slice((n + m) * 128, (n + m + 1) * 128)
                                t = three(PS[b][:, m * T:(m + 1) * T], (wh[:, k, s], wl[:, k, s]), (YH[:, k, :], YL[:, k, :]),
                                          k == 0, k == 1, sp_tok.get(u), bfree[b], ph, inc=(k == 1))
                        bfree[b] = plt[n] = act(PL[:, n:n + 2, :], PS[b][:, :].rearrange("p (a b) -> p a b", a=2), ACT.Copy, t)
                    if n == 6:
                        release(u, t)

                kw = []
                old = pe.last()
                for n, v in layer_norm(X, "1e-5", mid):
                    for k in (2 * n, 2 * n + 1):
                        v = ts(X[:, k, :], XC[:, k, :], col("ln_g", 8 * i + k), col("ln_b", 8 * i + k), ALU.mult, ALU.add, v)
                    kw += [split_act(XHL, 2 * n, 2, X[:, 2 * n:2 * n + 2, :], v, old)] * 2

                def post_n(n):
                    def post(ps, t):
                        g = SG[n % 2]
                        a = act(g, ps, ACT.Sigmoid, t, ve.last())
                        tt(g, g, PL[:, 2 * n:2 * n + 2, :], ALU.mult, a, plt[2 * n])
                        v = tt(X[:, 2 * n:2 * n + 2, :], X[:, 2 * n:2 * n + 2, :], g, ALU.add)
                        if hook:
                            hook(n, v)
                        return a
                    return post

                for n in range(4):
                    run(product(("w_pl_gate", i, 0, 256 * n), XHL, 0, post_n(n), kw=kw))

            for n in range(4):
                run(product(("w_out_even", 0, 8, 256 * n), YHL, 8, resid(n, False, hook_mean(X)), ys))
            pl_layer(0, None)
            kw = []
            old = pe.last()
            for n in range(4):
                kw += [split_act(XHL, 2 * n, 2, X[:, 2 * n:2 * n + 2, :], ve.last(), old)] * 2

            HQ = [view(512 * i, 2, T) for i in range(2)]
            HK = [view(1024 + 512 * i, 2, T) for i in range(2)]
            HF = [view(2048 + 512 * i, 2, T) for i in range(2)]
            HT = view(3072, 2, T)
            TOT = BIG[:, 3584:4096]
            ATT = [view(4096 + 512 * i, 4, 128) for i in range(2)]
            AT2 = [view(5120 + 256 * i, 2, 128) for i in range(2)]
            HV = [view(5632 + 512 * i, 2, T) for i in range(2)]
            OH = [view(6656 + 512 * i, 2, T) for i in range(2)]
            HZ = [view(7680 + 512 * i, 2, T) for i in range(2)]
            HR, HSQ = view(8704, 2, T), view(9216, 2, T)
            ys = []
            tk = [dict() for _ in range(9)]
            base_v, base_a = ve.last(), ac.last()

            def old_of(hp, name):
                return tk[hp - 2].get(name) if hp >= 2 else [base_v, base_a]

            def hg_proj(hp):
                i, tn = hp % 2, tk[hp]

                def q_post(ps, t):
                    tn["q"] = act(HQ[i], ps, ACT.Silu, t, old_of(hp, "qk_free"))
                    return tn["q"]

                def f_post(ps, t):
                    tn["sg"] = act(HT, ps, ACT.Sigmoid, t, ve.last())
                    return tn["sg"]

                def f_rest():
                    for m in range(2):
                        h = 2 * hp + m
                        ts(HF[i][:, m, :], HT[:, m, :], OLB[:, h:h + 1], LB[:, h:h + 1], ALU.mult, ALU.add, tn["sg"])
                    tn["k"] = ts(HK[i], HF[i], -1.0, 1.0, ALU.mult, ALU.add, old_of(hp, "qk_free"))

                def v_post(ps, t):
                    tn["v"] = act(HV[i], ps, ACT.Copy, t, old_of(hp, "av"))
                    return tn["v"]

                def z_post(ps, t):
                    tn["z"] = act(HZ[i], ps, ACT.Silu, t, old_of(hp, "z_free"))
                    return tn["z"]

                yield from product(("w_in_odd", 0, 0, 256 * hp), XHL, 0, q_post, kw=kw)
                yield from product(("w_in_odd", 0, 0, 2048 + 256 * hp), XHL, 0, f_post, kw=kw)
                g = product_tok(("w_in_odd", 0, 0, 4096 + 256 * hp), XHL, v_post, *kw)
                next(g)
                yield
                f_rest()
                yield from g
                yield from product(("w_in_odd", 0, 0, 6144 + 256 * hp), XHL, 0, z_post, kw=kw)

            def hg_attend(hp):
                i, tn = hp % 2, tk[hp]
                b = tn["bank"] = work_bank()
                for m in range(2):
                    h = slice(m * 128, (m + 1) * 128)
                    mm(PS[b][:, m * T:m * T + 128], HV[i][:, 0, h], ATT[i][:, 2 * m, :], tn["v"], tn["fin"], bfree[b])
                    mm(PS[b][:, m * T + 128:m * T + 256], HV[i][:, 0, h], AT2[i][:, m, :], stop=False)
                    t = mm(PS[b][:, m * T + 128:m * T + 256], HV[i][:, 1, h], ATT[i][:, 2 * m + 1, :], start=False, inc=(m == 1))
                tn["av"] = t
                pb = PS[b][:, :].rearrange("p (a b) -> p a b", a=2)
                a = act(OH[i], pb, ACT.Copy, t, old_of(hp, "o_free"))
                tn["sq"] = act(HSQ, pb, ACT.Square, tk[hp - 1].get("ones") if hp else None)
                bfree[b] = tn["sq"]

            def hg_norm(hp):
                i, tn = hp % 2, tk[hp]
                b = work_bank()
                for m in range(2):
                    t = mm(PS[b][:, m * T:(m + 1) * T], cs("ones"), HSQ[:, m, :], tn["sq"], bfree[b], inc=(m == 1))
                tn["ones"] = t
                ac.do(lambda e: e.preload_act_table_set("natural_log_exp_and_others"), inc=False)
                bfree[b] = act(HR, PS[b][:, :].rearrange("p (a b) -> p a b", a=2), ACT.Ln, t, tk[hp - 1].get("n") if hp else None,
                               scale=1.0 / 128, bias=EPSC["1e-5"])
                a = act(HR, HR, ACT.Exp, scale=-0.5)
                yield
                o = OH[i]
                tn["n"] = stt(o, o, col("hgrn_g"), HR, ALU.mult, ALU.mult, a)
                v = tn["z_free"] = tt(o, o, HZ[i], ALU.mult, tn["z"])
                tn["y"] = tn["o_free"] = split_act(YHL, 2 * hp, 2, o, v)
                ys.extend(tn["y"])

            def hg_levels(hp, slot):
                i, tn = hp % 2, tk[hp]
                q, k, f, at = HQ[i], HK[i], HF[i], ATT[i]
                g = G(lambda e: e.memset(at, 0.0), old_of(hp, "av"))
                pt = None
                tot = f.rearrange("p m t -> p (m t)")
                off = 0
                uq, uk, ut = tn["q"], tn["k"], tn["k"]
                fin = None
                for lv in range(-1, 8):
                    if lv == 0:
                        uq = tt(q, q, f, ALU.mult, pt, uq, ut)
                    elif lv > 0:
                        w = 1 << (lv - 1)
                        nb = 2 * T // (2 * w)

                        def pairs(x):
                            return x.rearrange("p m (b r w) -> p (m b) r w", r=2, w=w)
                        tp = tot.rearrange("p (b r) -> p b r", r=2)
                        uk = tt(pairs(k)[:, :, 0, :], pairs(k)[:, :, 0, :], bc(tp[:, :, 1], w), ALU.mult, pt, uk, ut, free=True)
                        uq = tt(pairs(q)[:, :, 1, :], pairs(q)[:, :, 1, :], bc(tp[:, :, 0], w), ALU.mult, pt, uq, ut, free=True)
                        if lv < 7:
                            nt = TOT[:, off:off + nb]
                            off += nb
                            ut = tt(nt, tp[:, :, 0], tp[:, :, 1], ALU.mult, ut, tk[hp - 1].get("lv") if hp else None, free=True)
                            tot = nt
                    b = work_bank()
                    if lv < 7:
                        for m in range(4):
                            s = slice((m % 2) * 128, (m % 2 + 1) * 128)
                            pt = mm(PS[b][:, m * 128:(m + 1) * 128], k[:, m // 2, s], q[:, m // 2, s], uq, uk, bfree[b], inc=(m == 3))
                    else:
                        for m in range(2):
                            pt = mm(PS[b][:, m * 128:(m + 1) * 128], k[:, m, 0:128], q[:, m, 128:256], uq, uk, bfree[b], inc=(m == 1))
                    if fin:
                        fin()

                    def fin(lv=lv, b=b, t=pt):
                        ps = PS[b][:, :].rearrange("p (m t) -> p m t", m=4)
                        if lv < 5:
                            mk = (cs("gm", 128 * lv) if lv >= 0 else cs("ident")).bitcast(i32)
                            bfree[b] = V(lambda e: e.copy_predicated(at, bm(mk, 4), ps), t, g)
                            tn["fv"] = bfree[b]
                        elif lv == 5:
                            act(at[0:32, :, 32:64], ps[0:32, :, 32:64], ACT.Copy, t, tn["fv"])
                            bfree[b] = act(at[64:96, :, 96:128], ps[64:96, :, 96:128], ACT.Copy)
                        elif lv == 6:
                            bfree[b] = act(at[0:64, :, 64:128], ps[0:64, :, 64:128], ACT.Copy, t)
                        else:
                            bfree[b] = act(AT2[i], ps[:, 0:2, :], ACT.Copy, t, old_of(hp, "av"))
                            tn["fin"] = [bfree[b], tn["fv"]]
                    if lv < 7:
                        slot(lv)
                    if hp:
                        if lv == -1:
                            hg_attend(hp - 1)
                        if lv == 1:
                            norm = hg_norm(hp - 1)
                            next(norm)
                        if lv == 2:
                            run(norm)
                fin()
                tn["qk_free"] = pt
                tn["lv"] = ve.last()

            def w_out_first():
                for n in range(4):
                    yield from product(("w_out_odd", 0, 0, 256 * n), YHL, 0, resid(n, True), tk[0]["y"], tk[1]["y"], tk[2]["y"], tk[3]["y"])

            run(hg_proj(0))
            for hp in range(8):
                nxt = hg_proj(hp + 1) if hp < 7 else w_out_first()

                def slot(lv):
                    if hp == 7 and lv >= 5:
                        return
                    next(nxt)
                    if lv in (2, 5) and ada["n"] < 40:
                        ada_fill(1)
                hg_levels(hp, slot)
                if hp < 7:
                    run(nxt)
            hg_attend(7)
            next(nxt)
            run(hg_norm(7))
            run(nxt)
            for n in range(4):
                run(product(("w_out_odd", 0, 8, 256 * n), YHL, 8, resid(n, False, hook_mean(X)), ys))
            pl_layer(1, hook_sq(X))
            while ada["n"] < 24:
                ada_fill(1)

            def mods(i):
                m = MOD[:, 48 * i:48 * i + 48]
                tt(m, m, col("ada_b", 48 * i, 48), ALU.add)
                for q, nm in ((1, "mix_g"), (4, "mlp_g")):
                    m = MOD[:, 48 * i + 8 * q:48 * i + 8 * q + 8]
                    stt(m, m, 1.0, col(nm, 8 * i, 8), ALU.add, ALU.mult)
                ac.wait([ve.last()])

            def mod(i, q):
                return MOD[:, 48 * i + 8 * q:48 * i + 8 * q + 8]

            def gated(i, q, n0, hook=None):
                def post(ps, t):
                    for m in range(2):
                        k = 2 * n0 + m
                        v = stt(X[:, k, :], ps[:, m, :], mod(i, q)[:, k:k + 1], X[:, k, :], ALU.mult, ALU.add, t)
                    if hook:
                        hook(n0, v)
                    return v
                return post

            def mlp(i, hook, adas):
                kw = rms_mod(mod(i, 4), mod(i, 3), XHL)
                RL = [view(7168 + 512 * j, 2, T) for j in range(2)]
                hs = {}
                rl = [None, None]

                def w1_post(n):
                    def post(ps, t):
                        o = 8 * ((n // 4) % 2) + 2 * (n % 4)
                        r = RL[n % 2]
                        a = act(r, ps, ACT.Relu, t, rl[n % 2])
                        v = tt(r, r, r, ALU.mult, a)
                        rl[n % 2] = split_act(YHL, o, 2, r, v, hfree.get(n // 4 - 2))
                        hs.setdefault(n // 4, []).extend(rl[n % 2])
                        return a
                    return post

                hfree = {-1: None}

                def w2(g):
                    for n in range(4):
                        run(product(("mlp_w2", i, 8 * g, 256 * n), YHL, 8 * (g % 2), gated(i, 5, n, hook if g == 3 else None), hs[g]))
                        if adas:
                            ada_fill(1)
                    hfree[g] = pe.last()

                for g in range(4):
                    for n in range(4 * g, 4 * g + 4):
                        run(product(("mlp_w1", i, 0, 256 * n), XHL, 0, w1_post(n), kw=kw))
                        if adas:
                            ada_fill(1)
                    if g:
                        w2(g - 1)
                w2(3)

            mods(0)
            kw = rms_mod(mod(0, 1), mod(0, 0), XHL)
            NV = 19
            NP = 31 - NV
            U = [view(7168 + 288 * i, 1, 286)[:, 0, :] for i in range(2)]
            CO = view(7744, 8, T)
            SGC = [view(9792 + 256 * i, 1, T)[:, 0, :] for i in range(2)]
            AV = view(10304, 1, T)
            DG = [view(10560 + NP * 128 * i, NP, 128) for i in range(2)]
            zu = [G(lambda e, i=i: e.memset(U[i][:, 0:30], 0.0), ve.last(), ac.last()) for i in range(2)]
            ut = {}

            def glu_post(j):
                def post(ps, t):
                    u = U[j % 2]
                    a = act(SGC[j % 2], ps[:, 1, :], ACT.Sigmoid, t, ut.get(("sg", j - 2)), bias=col("b_in", 8 + j))
                    v = stt(u[:, 30:286], ps[:, 0, :], col("b_in", j), SGC[j % 2], ALU.add, ALU.mult, a, zu, ut.get(("pe", j - 2)))
                    ut[("sg", j)] = ut[("u", j)] = v
                    d = ut.get(("pe", j - 2))
                    for q in range(NP):
                        a2 = act(DG[j % 2][:, q, :], cs("ident"), ACT.Copy, d, ac.last() if q == 0 else None, free=True,
                                 scale=col("dw", 31 * j + NV + q))
                    ut[("dg", j)] = a2
                    ts(CO[:, j, :], u[:, 0:256], col("dw", 31 * j), col("dw_b", j), ALU.mult, ALU.add)
                    for q in range(1, NV):
                        ut[("co", j)] = stt(CO[:, j, :], u[:, q:256 + q], col("dw", 31 * j + q), CO[:, j, :], ALU.mult, ALU.add)
                    return [a, v]
                return post

            def taps(j):
                b = work_bank()
                u = U[j % 2]
                for q in range(NP):
                    t = mm(PS[b][:, 0:T], DG[j % 2][:, q, :], u[:, NV + q:NV + q + 256], ut[("dg", j)], ut[("u", j)], bfree[b],
                           start=(q == 0), stop=(q == NP - 1), inc=(q == NP - 1))
                ut[("pe", j)] = t
                v = bfree[b] = tt(CO[:, j, :], CO[:, j, :], PS[b][:, 0:T], ALU.add, t)
                if j % 2:
                    hook_mean(CO)(j // 2, v)

            for j in range(8):
                g = product(("conv_w_in", 0, 0, (128 * j, 1024 + 128 * j)), XHL, 0, glu_post(j), kw=kw)
                next(g)
                if j:
                    taps(j - 1)
                run(g)
            taps(7)
            kw = []
            old = pe.last()
            for n, v in layer_norm(CO, "1e-6", lambda: None):
                for k in (2 * n, 2 * n + 1):
                    v = ts(CO[:, k, :], XC[:, k, :], col("cln_g", k), col("cln_b", k), ALU.mult, ALU.add, v)
                p = CO[:, 2 * n:2 * n + 2, :]
                a = act(p, p, ACT.Silu, v)
                kw += [split_act(XHL, 2 * n, 2, p, a, old)] * 2

            def cout_post(n):
                def post(ps, t):
                    for m in range(2):
                        k = 2 * n + m
                        ts(AV[:, 0, :], ps[:, m, :], col("b_out", k), mod(0, 2)[:, k:k + 1], ALU.add, ALU.mult, t)
                        v = tt(X[:, k, :], X[:, k, :], AV[:, 0, :], ALU.add)
                    hook_sq(X)(n, v)
                    return v
                return post

            for n in range(4):
                run(product(("conv_w_out", 0, 0, 256 * n), XHL, 0, cout_post(n), kw=kw))
            mlp(0, hook_sq(X), True)
            while ada["n"] < 48:
                ada_fill(1)
            mods(1)

            kw = rms_mod(mod(1, 1), mod(1, 0), XHL)
            AQ = view(4096, 16, T)
            AV2 = view(8192, 2, 1024)
            NB = [(view(10240 + 2048 * i, 4, T), view(11264 + 2048 * i, 4, T)) for i in range(2)]
            ones64, dist = LATE[:, 0:128], LATE[:, 128:512]
            qt = {}

            def qk_post(n):
                def post(ps, t):
                    qt[n] = act(AQ[:, 2 * n:2 * n + 2, :], ps, ACT.Copy, t)
                    return qt[n]
                return post

            def av_post(n):
                def post(ps, t):
                    qt["v"] = act(AV2[:, :, 256 * n:256 * n + 256], ps, ACT.Copy, t)
                    return qt["v"]
                return post

            def qk_norm(g):
                sq, rs = NB[g % 2]
                src = AQ[:, 4 * g:4 * g + 4, :]
                s = act(sq, src, ACT.Square, qt.get(("pe", g - 2)))
                yield
                for m in range(0, 4, 2):
                    b = work_bank()
                    for i in range(2):
                        t = mm(PS[b][:, i * T:(i + 1) * T], ones64, sq[:, m + i, :], s, bfree[b], (s_p[2], 16), inc=(i == 1))
                    if m == 0:
                        ac.do(lambda e: e.preload_act_table_set("natural_log_exp_and_others"), inc=False)
                    bfree[b] = act(rs[:, m:m + 2, :], PS[b][:, :].rearrange("p (a b) -> p a b", a=2), ACT.Ln, t,
                                   qt.get(("v", g - 2)), scale=1.0 / 64, bias=EPSC["1e-6"])
                qt[("pe", g)] = t
                yield
                a = act(rs, rs, ACT.Exp, scale=-0.5)
                qt[("v", g)] = stt(src, src, col("qn_g" if g < 2 else "kn_g"), rs, ALU.mult, ALU.mult, a)
                yield

            bg = []

            def halves(gen):
                for _ in gen:
                    for x in list(bg):
                        try:
                            next(x)
                        except StopIteration:
                            bg.remove(x)

            for n in range(8):
                halves(product(("attn_w_qkv", 0, 0, 256 * n), XHL, 0, qk_post(n), kw=kw))
                if n % 2:
                    bg.append(qk_norm(n // 2))
            for n in range(4):
                halves(product_tok(("attn_w_qkv", 0, 0, 2048 + 256 * n), XHL, av_post(n), *kw))
            while bg:
                run(bg.pop(0))
            nt = ve.last()
            SCB = [view(768 * i, 2, 384) for i in range(2)]
            PTA = [view(1536 + 768 * i, 2, 384) for i in range(2)]
            mxs = [SM[:, 200 + 8 * i:208 + 8 * i] for i in range(2)]
            sct = {}

            def scores(p):
                i = p % 2
                sc = SCB[i]
                for hh in range(2):
                    h = 2 * p + hh
                    b = 3 + hh
                    q, k = AQ[64 * hh:64 * hh + 64, p, :], AQ[64 * hh:64 * hh + 64, 8 + p, :]
                    mm(PS[b][:, 0:128], q[:, 0:128], k[:, 0:128], nt, bfree[b])
                    t = mm(PS[b][:, 128:384], q[:, 128:256], k, inc=True)
                    slope = float(2.0 ** (-0.5 * (h + 1)))
                    bfree[b] = stt(sc[:, hh, :], dist, slope * 8.0, PS[b][:, 0:384], ALU.mult, ALU.add, t, sct.get(("tr", p - 2)))
                mx = mxs[i][:, 0:4].rearrange("p (h q) -> p h q", h=2)
                rs = mxs[i][:, 4:8].rearrange("p (h q) -> p h q", h=2)
                V(lambda e: e.tensor_reduce(mx[:, :, 0], sc[:, :, 0:128], AX.X, ALU.max))
                V(lambda e: e.tensor_reduce(mx[:, :, 1], sc[:, :, 128:384], AX.X, ALU.max), free=True)
                v = ts(mxs[i][:, 0:4], mxs[i][:, 0:4], -0.125, None, ALU.mult, None)
                sct[("mx", p)] = v

                def rest():
                    for hh in range(2):
                        act(sc[:, hh, 0:128], sc[:, hh, 0:128], ACT.Exp, v, bias=mx[:, hh, 0:1], scale=0.125, accum_out=rs[:, hh, 0:1])
                        a = act(sc[:, hh, 128:384], sc[:, hh, 128:384], ACT.Exp, bias=mx[:, hh, 1:2], scale=0.125,
                                accum_out=rs[:, hh, 1:2])
                    V(lambda e: e.reciprocal(mxs[i][:, 4:8], mxs[i][:, 4:8]), a)
                    tt(sc[:, :, 0:128], sc[:, :, 0:128], bc(rs[:, :, 0], 128), ALU.mult)
                    sct[p] = tt(sc[:, :, 128:384], sc[:, :, 128:384], bc(rs[:, :, 1], 256), ALU.mult)
                return rest

            def values(p):
                sc, pt = SCB[p % 2], PTA[p % 2]
                for hh in range(2):
                    b = 5 + hh
                    for q in range(3):
                        t = tr(PS[b][:, q * 128:(q + 1) * 128], sc[:, hh, q * 128:(q + 1) * 128], sct[p], bfree[b], inc=(q == 2))
                    a = bfree[b] = act(pt[:, hh, :], PS[b][:, 0:384], ACT.Copy, t, sct.get(("pv", p - 2)))
                sct[("tr", p)] = t
                for hh in range(2):
                    hc = slice(64 * (2 * p + hh), 64 * (2 * p + hh) + 64)
                    o = PS[7][64 * hh:64 * hh + 64, :]
                    mm(o[:, 0:128], AV2[:, 0, hc], pt[:, hh, 0:128], a, bfree[7], qt["v"])
                    mm(o[:, 128:256], AV2[:, 0, hc], pt[:, hh, 128:256], stop=False)
                    t = mm(o[:, 128:256], AV2[:, 1, hc], pt[:, hh, 256:384], start=False, inc=True)
                sct[("pv", p)] = t
                o = PS[7][:, 0:T]
                h = act(YH[:, p, :], o, ACT.Copy, t)
                bfree[7] = tt(YL[:, p, :], o, YH[:, p, :].bitcast(f32), ALU.subtract, h)
                return [h, bfree[7]]

            yt = []
            r0 = scores(0)
            r0()
            for p in range(8):
                r1 = scores(p + 1) if p < 7 else None
                yt.append(values(p))
                if r1:
                    r1()
            for n in range(4):
                run(product(("attn_w_o", 0, 0, 256 * n), YHL, 0, gated(1, 2, n, hook_sq(X)), kw=yt))

            def store(n, t):
                sp.wait([t])
                sp.q.append((lambda e: e.dma_start(out[:, 2 * n:2 * n + 2, :], X[:, 2 * n:2 * n + 2, :]).then_inc(s_out, 16), False))

            mlp(1, store, False)
            sp.q.append((s_out, 64))
            if plan:
                assert st["used"] == len(plan) == st["load"], (st, len(plan))
            return pe, ve, ac, gp, sp, loads

        ctx_rw = sb("RW", [8, 2, T])
        EP = sb("EP", [128, 4])
        EPSC = {"1e-6": EP[:, 0:1], "1e-5": EP[:, 1:2], "lnq": EP[:, 2:3]}
        EPSV = [(EP[:, 0:1], 1e-6), (EP[:, 1:2], 1e-5), (EP[:, 2:3], float(np.log(128.0 ** -0.5)))]
        specs = []
        pe, ve, ac, gp, sp, loads = emit(plan, specs)
        if not plan:
            return specs
        block = ctx.enter_context(nc.Block())

        @block.sync
        def _(eng):
            loads(eng)
            sp.play(eng)

        @block.gpsimd
        def _(eng):
            gp.play(eng)

        @block.scalar
        def _(eng):
            ac.play(eng)

        @block.vector
        def _(eng):
            ve.play(eng)

        @block.tensor
        def _(eng):
            pe.play(eng)
    return specs


def _tiles(v):
    import numpy as _np
    return _np.ascontiguousarray(v.reshape(-1, 128).T)


def kernel(**inputs):
    import numpy as _np
    import concourse.bacc as _bacc
    from concourse import mybir as _mybir
    from concourse.bass_utils import run_bass_kernel_spmd as _run

    a = {k: _np.asarray(v) for k, v in inputs.items()}
    parts = {
        "conv_a_w": a["conv_a_w"][0].reshape(3, 8, 128).transpose(2, 1, 0).reshape(128, 24),
        "conv_b_w": a["conv_b_w"][0].reshape(4, 24, 128).transpose(2, 1, 0).reshape(128, 96),
        "gdn_g": _tiles(a["gdn_norm_g"]), "lb": _tiles(a["lower_bounds"]), "hgrn_g": _tiles(a["hgrn_norm_g"]),
        "ln_g": _tiles(a["ln_g"]), "ln_b": _tiles(a["ln_b"]), "ada_b": _tiles(a["ada_b_2"]),
        "mix_g": _tiles(a["mix_norm_g_2"]), "mlp_g": _tiles(a["mlp_norm_g_2"]), "b_in": _tiles(a["conv_b_in_2"]),
        "dw": a["conv_dw_2"][0].reshape(31, 8, 128).transpose(2, 1, 0).reshape(128, 248),
        "dw_b": _tiles(a["conv_dw_b_2"]), "cln_g": _tiles(a["conv_ln_g_2"]), "cln_b": _tiles(a["conv_ln_b_2"]),
        "b_out": _tiles(a["conv_b_out_2"]),
        "qn_g": _np.concatenate([a["attn_q_norm_g_2"][0]] * 2).reshape(128, 1),
        "kn_g": _np.concatenate([a["attn_k_norm_g_2"][0]] * 2).reshape(128, 1),
        "wbg": a["w_in_even"][0][:, 8192:8208].reshape(8, 128, 16).transpose(1, 0, 2).reshape(128, 128),
    }
    cols = _np.ascontiguousarray(_np.concatenate([parts[n] for n, _ in COLS], 1))
    rows = _np.ascontiguousarray(_np.stack([a["a_log"][0], a["dt_bias"][0]], 1))
    xT = _np.ascontiguousarray(a["x"][0].T.reshape(8, 128, T).transpose(1, 0, 2))
    pT = _np.ascontiguousarray(a["p"][:, 0].transpose(0, 2, 1).reshape(2, 2, 128, T).transpose(0, 2, 1, 3))
    cst, late = constants()
    late = _np.ascontiguousarray(late)
    crow = _np.ascontiguousarray(a["c_2"].reshape(1, 1024))
    names = {n: (n if n in a else n + "_2") for n in
             ("w_in_even", "w_out_even", "w_in_odd", "w_out_odd", "w_pl", "w_pl_gate", "ada_w", "conv_w_in", "conv_w_out",
              "attn_w_qkv", "attn_w_o", "mlp_w1", "mlp_w2")}
    f = _mybir.dt.float32

    def build(plan):
        nc = _bacc.Bacc("TRN2", target_bir_lowering=False, num_devices=1)

        def dram(name, shape, dt=f, kind="ExternalInput"):
            return nc.dram_tensor(name, shape, dt, kind=kind).ap()

        specs = program(nc, dram("xT", (128, 8, T)), dram("wst", (max(len(plan), 1), 128, 2048)), dram("cols", cols.shape),
                        dram("rows", rows.shape), dram("crow", crow.shape), dram("pT", pT.shape), dram("cst", cst.shape), dram("late", late.shape),
                        dram("outT", (128, 8, T), kind="ExternalOutput"), plan)
        return nc, specs

    plan = build([])[1]
    wst = _np.empty((len(plan), 128, 2048), _np.float32)
    for u, (name, layer, k0, c0) in enumerate(plan):
        w = a[names[name]][layer]
        if name == "w_pl":
            wst[u] = w.reshape(2, 128, 1024).transpose(1, 0, 2).reshape(128, 2048)
            continue
        if name == "ada_w":
            wst[u] = w[:, c0:c0 + 256].T.reshape(2, 128, 1024).transpose(1, 0, 2).reshape(128, 2048)
            continue
        w = w[128 * k0:128 * k0 + 1024]
        if isinstance(c0, tuple):
            w = _np.concatenate([w[:, c:c + 128] for c in c0], 1)
        else:
            w = w[:, c0:c0 + 256]
        wst[u] = w.reshape(8, 128, 256).transpose(1, 0, 2).reshape(128, 2048)
    nc, _ = build(plan)
    r = _run(nc, [{"xT": xT, "wst": wst, "cols": cols, "rows": rows, "crow": crow, "pT": pT, "cst": cst, "late": late}], core_ids=[0])
    o = _np.asarray(r.results[0]["outT"])
    return _np.ascontiguousarray(o.transpose(2, 1, 0).reshape(1, T, 1024))
```

```python
import numpy as np
import concourse.bass as bass
from concourse import mybir
from contextlib import ExitStack

T = 256
NR, NS = 3, 3
BW = 16448
ALPHA = 4.0 ** 0.25
NEG = -1.0e30


COLS = [("conv_a_w", 24), ("conv_b_w", 96), ("gdn_g", 1), ("lb", 32), ("hgrn_g", 1), ("ln_g", 16), ("ln_b", 16),
        ("ada_b", 96), ("mix_g", 16), ("mlp_g", 16), ("b_in", 16), ("dw", 248), ("dw_b", 8),
        ("cln_g", 8), ("cln_b", 8), ("b_out", 8), ("qn_g", 1), ("kn_g", 1), ("wbg", 128)]
COL0 = {}
_n = 0
for _name, _k in COLS:
    COL0[_name] = (_n, _k)
    _n += _k
NCOL = _n

CST = [("ident", 128), ("ones", 128), ("neg", 128), ("gm", 896)]
CST0 = {}
_n = 0
for _name, _k in CST:
    CST0[_name] = (_n, _k)
    _n += _k
NCST = _n


def constants():
    j = np.arange(128)[:, None]
    i = np.arange(128)[None, :]
    f = np.zeros((128, NCST), np.float32)

    def put(name, v):
        a, n = CST0[name]
        f[:v.shape[0], a:a + n] = v

    put("ident", (i == j).astype(np.float32))
    put("ones", np.ones((128, 128), np.float32))
    put("neg", np.where(i >= j, 0.0, NEG).astype(np.float32))
    lv = [((i // (2 * s) == j // (2 * s)) & ((i // s) % 2 == 1) & ((j // s) % 2 == 0)) for s in (1, 2, 4, 8, 16, 32, 64)]
    put("gm", np.concatenate(lv, 1).astype(np.float32))
    k = np.arange(256)[None, :]
    d0 = np.where(j >= i, -(j - i).astype(np.float32), np.float32(NEG))
    d1 = np.where(j + 128 >= k, -(j + 128 - k).astype(np.float32), np.float32(NEG))
    late = np.concatenate([i // 64 == j // 64, d0, d1], 1).astype(np.float32)
    return f, late


class Lane:

    def __init__(self, sem):
        self.sem, self.q, self.n, self.seen = sem, [], 0, {}

    def wait(self, toks):
        for t in toks:
            if t is None:
                continue
            if isinstance(t, list):
                self.wait(t)
                continue
            sem, v = t
            if self.seen.get(id(sem), 0) < v:
                self.seen[id(sem)] = v
                self.q.append((sem, v))

    def last(self):
        return (self.sem, self.n) if self.n else None

    def do(self, fn, *toks, inc=True):
        self.wait(toks)
        self.q.append((fn, inc))
        if inc:
            self.n += 1
        return (self.sem, self.n)

    def play(self, eng):
        for a, b in self.q:
            if callable(a):
                ins = a(eng)
                if b:
                    ins.then_inc(self.sem, 1)
            else:
                eng.wait_ge(a, b)


def program(nc, xT, wst, wad, cols, rows, crow, pT, cst, late, out, plan):
    f32, fr, i32 = mybir.dt.float32, mybir.dt.float32r, mybir.dt.int32
    ALU, ACT, AX = mybir.AluOpType, mybir.ActivationFunctionType, mybir.AxisListType
    ctx = ExitStack()
    with ctx:
        def sb(name, shape, dt=f32):
            return ctx.enter_context(nc.sbuf_tensor(name, shape, dt))

        def sem(name):
            return ctx.enter_context(nc.semaphore(name))

        RAW = [sb(f"RAW{i}", [128, 2048]) for i in range(NR)]
        WH = [sb(f"WH{i}", [128, 2048], fr) for i in range(NS)]
        WL = [sb(f"WL{i}", [128, 2048], fr) for i in range(NS)]
        X = sb("X", [128, 8, T])
        XH = sb("XH", [128, 8, T], fr)
        XL = sb("XL", [128, 8, T], fr)
        YH = sb("YH", [128, 16, T], fr)
        YL = sb("YL", [128, 16, T], fr)
        C = sb("C", [128, NCOL])
        R8 = sb("R8", [8, 2])
        CB1 = sb("CB1", [128, 1024])
        K = sb("K", [128, NCST])
        MOD = sb("MOD", [128, 96])
        SM = sb("SM", [128, 256])
        BIG = sb("BIG", [128, BW])
        PS = [ctx.enter_context(nc.psum_tensor(f"PS{i}", [128, 512], f32)) for i in range(8)]

        s_pe, s_v, s_a, s_g = sem("s_pe"), sem("s_v"), sem("s_a"), sem("s_g")
        s_in, s_x, s_out = sem("s_in"), sem("s_x"), sem("s_out")
        s_p = [sem("s_p0"), sem("s_p1"), sem("s_late")]
        s_ad = [sem("s_ad0"), sem("s_ad1")]
        s_raw = [sem(f"s_raw{i}") for i in range(NR)]

        def col(name, i=0, n=1, p=128):
            a = COL0[name][0] + i
            return C[0:p, a:a + n]

        def cs(name, i=0, n=128, p=128):
            a = CST0[name][0] + i
            return K[0:p, a:a + n]

        def emit(plan, specs):
            pe, ve, ac, gp, sp = Lane(s_pe), Lane(s_v), Lane(s_a), Lane(s_g), Lane(s_out)

            def V(fn, *w, free=False):
                return ve.do(fn, *(w if free else (ve.last(), *w)))

            def G(fn, *w, free=False):
                return gp.do(fn, *(w if free else (gp.last(), *w)))

            def tt(o, a, b, op, *w, free=False, E=V):
                return E(lambda e: e.tensor_tensor(o, a, b, op), *w, free=free)

            def ts(o, a, s1, s2, op0, op1, *w, free=False, E=V):
                if op1 is None:
                    return E(lambda e: e.tensor_scalar(o, a, s1, None, op0), *w, free=free)
                return E(lambda e: e.tensor_scalar(o, a, s1, s2, op0, op1), *w, free=free)

            def stt(o, a, s, b, op0, op1, *w, free=False):
                return V(lambda e: e.scalar_tensor_tensor(out=o, in0=a, scalar=s, in1=b, op0=op0, op1=op1), *w, free=free)

            def act(o, a, f, *w, free=False, **kw):
                return ac.do(lambda e: e.activation(o, a, f, **kw), *(w if free else (ac.last(), *w)))

            def mm(o, l, r, *w, start=True, stop=True, inc=False):
                return pe.do(lambda e: e.matmul(o, l, r, start=start, stop=stop), *w, inc=inc)

            def tr(o, a, *w, inc=False):
                n = a.shape[0]
                return pe.do(lambda e: e.transpose(o, a, cs("ident", 0, n, n)), *w, inc=inc)

            s_xt = (s_x, 16)
            s_all = (s_in, 64)

            def loads(e):
                e.dma_start(X[:, :, :], xT).then_inc(s_x, 16)

            def load_constants(e):
                for o, i in ((C[:, :], cols), (R8[:, :], rows), (K[:, :], cst), (CB1[:, :], crow.broadcast_to([128, 1024]))):
                    e.dma_start(o, i).then_inc(s_in, 16)

            raw_free = {}
            slot_free = {}
            sp_tok = {}
            st = {"load": 0, "split": 0, "ns": 0, "used": 0}
            slot_of = {}

            def raw_ready(u):
                return (s_raw[u % NR], 16 * (u // NR + 1))

            def load_more():
                while st["load"] < len(plan) and st["load"] != st.get("hold") and (st["load"] < NR or (st["load"] - NR) in raw_free):
                    u = st["load"]
                    sp.wait([raw_free.get(u - NR)])
                    sp.q.append((lambda e, u=u: e.dma_start(RAW[u % NR][:, :], wst[u]).then_inc(s_raw[u % NR], 16), False))
                    st["load"] += 1

            def split_next():
                u = st["split"]
                if u >= len(plan):
                    return False
                if plan[u][0] == "ada_w":
                    load_more()
                    if u >= st["load"]:
                        return False
                    st["split"] += 1
                    ada_unit(u)
                    load_more()
                    return True
                n = st["ns"]
                if n >= NS and (n - NS) not in slot_free:
                    return False
                load_more()
                if u >= st["load"]:
                    return False
                s, free = n % NS, slot_free.get(n - NS)
                r = RAW[u % NR]
                a = act(WH[s][:, :], r[:, :], ACT.Copy, raw_ready(u), free, free=True)
                flush()
                late_lo.append((u, s, r, a, free))
                slot_of[u] = (s, n)
                st["ns"] += 1
                st["split"] += 1
                if st["used"] + 1 >= u:
                    flush()
                return True

            late_lo = []

            def flush():
                if late_lo:
                    u, s, r, a, free = late_lo.pop()
                    b = tt(WL[s][:, :], r[:, :], WH[s][:, :].bitcast(f32), ALU.subtract, a, raw_ready(u), free, free=True)
                    sp_tok[u] = [a, b]
                    raw_free[u] = [a, b]
                    load_more()

            def ada_unit(u):
                raw_free[u] = [ada_ops(RAW[u % NR], plan[u][1] * 24 + plan[u][3] // 256, raw_ready(u))]

            def ada_ops(buf, n, ready):
                for m in range(2):
                    w = buf[:, m * 1024:(m + 1) * 1024]
                    o = MOD[:, 2 * n + m:2 * n + m + 1]
                    t = V(lambda e, w=w, o=o: e.tensor_tensor_reduce(
                        out=w, in0=w, in1=CB1[:, :], scale=1.0, scalar=0.0, op0=ALU.mult, op1=ALU.add, accum_out=o),
                        ready, cb_tok, free=True)
                return t

            def pump():
                load_more()
                while split_next():
                    pass

            def unit(*spec):
                specs.append(spec)
                u = st["used"]
                st["used"] += 1
                if u < len(plan):
                    assert plan[u] == spec, (u, plan[u], spec)
                    pump()
                    if spec[0] != "ada_w":
                        assert u in slot_of
                        if u not in sp_tok:
                            flush()
                return u

            bank = {"n": 0, "of": 3, "w": 0}
            bfree = [None] * 8

            def take_bank():
                b = bank["n"] % bank["of"]
                bank["n"] += 1
                return b

            def wparts(u, nk):
                s = slot_of[u][0] if u in slot_of else 0
                return (WH[s][:, :].rearrange("p (k n) -> p k n", k=nk), WL[s][:, :].rearrange("p (k n) -> p k n", k=nk))

            def release(u, tok):
                if u in slot_of:
                    slot_free[slot_of[u][1]] = tok
                    pump()

            def three(o, l, r, first, lastk, *w, inc=False):
                mm(o, l[0], r[0], *w, start=first, stop=False)
                mm(o, l[0], r[1], start=False, stop=False)
                return mm(o, l[1], r[0], start=False, stop=lastk, inc=inc)

            def work_bank():
                bank["w"] += 1
                return 3 + bank["w"] % 5

            def product(spec, act_hl, k0, post, *w, kw=None):
                u = unit(*spec)
                b = take_bank()
                h, l = act_hl
                wh, wl = wparts(u, 8)
                for n in range(2):
                    for k in range(8):
                        t = three(PS[b][:, n * T:(n + 1) * T],
                                  (wh[:, k, n * 128:(n + 1) * 128], wl[:, k, n * 128:(n + 1) * 128]),
                                  (h[:, k0 + k, :], l[:, k0 + k, :]), k == 0, k == 7, kw[k] if kw else None,
                                  *((sp_tok.get(u), bfree[b], *w) if n == 0 and k == 0 else ()), inc=(k == 7))
                    yield
                    flush()
                if st["early"]:
                    release(u, t)
                bfree[b] = post(PS[b][:, :].rearrange("p (n t) -> p n t", n=2), t)
                if not st["early"]:
                    release(u, t)

            def product_tok(spec, act_hl, post, *w):
                u = unit(*spec)
                b = take_bank()
                h, l = act_hl
                wh, wl = wparts(u, 8)
                for n in range(2):
                    for k in range(8):
                        t = three(PS[b][:, n * T:(n + 1) * T],
                                  (h[:, k, n * 128:(n + 1) * 128], l[:, k, n * 128:(n + 1) * 128]),
                                  (wh[:, k, :], wl[:, k, :]), k == 0, k == 7,
                                  *((sp_tok.get(u), bfree[b], *w) if n == 0 and k == 0 else ()), inc=(k == 7))
                    yield
                    flush()
                if st["early"]:
                    release(u, t)
                bfree[b] = post(PS[b][:, :].rearrange("p (n t) -> p n t", n=2), t)
                if not st["early"]:
                    release(u, t)

            def run(g):
                for _ in g:
                    pass

            def run_last(g, last):
                st["early"] = not last
                run(g)
                st["early"] = True

            ada = {"n": 0, "stop": 0}

            def ada_fill(count):
                for _ in range(count):
                    n = ada["n"]
                    if n == 48:
                        return
                    ada["n"] += 1
                    unit("ada_w", n // 24, 0, (n % 24) * 256)

            AB = [BIG[:, 10240 + 2048 * i:12288 + 2048 * i] for i in range(2)]
            side = {"load": 0, "cnt": [0, 0], "tok": {}, "free": [None, None]}

            def side_load(*w):
                n = max(side["load"], ada["n"])
                if n >= 48 or n >= ada["n"] + 2 or n >= ada["stop"]:
                    return
                side["load"] = n + 1
                i = n % 2
                side["cnt"][i] += 1
                side["tok"][n] = (s_ad[i], 16 * side["cnt"][i])
                gp.do(lambda e: e.dma_start(AB[i], wad[n]).then_inc(s_ad[i], 16), side["free"][i], *w, inc=False)

            def ada_side():
                n = ada["n"]
                if n >= 48 or n >= ada["stop"]:
                    return
                assert n in side["tok"]
                ada["n"] += 1
                side["free"][n % 2] = ada_ops(AB[n % 2], n, side["tok"][n])
                side_load()

            fillers = []

            def fill(n=1, keep=0):
                while n > 0 and fillers:
                    try:
                        next(fillers[0])
                        n -= 1
                    except StopIteration:
                        fillers.pop(0)

            def fill_all():
                while fillers:
                    fill(1)

            st["early"] = False
            st["hold"] = 2
            load_more()
            st["hold"] = None
            sp.q.append((load_constants, False))
            XHL = (XH, XL)
            YHL = (YH, YL)

            def split_act(hl, lo, n, src, *w):
                a = act(hl[0][:, lo:lo + n, :], src, ACT.Copy, *w)
                b = tt(hl[1][:, lo:lo + n, :], src, hl[0][:, lo:lo + n, :].bitcast(f32), ALU.subtract, a, *w)
                return [a, b]

            xs = []
            for k in range(8):
                xs.append(split_act(XHL, k, 1, X[:, k:k + 1, :], s_xt))
            pump()
            cb_tok = act(CB1[:, :], CB1[:, :], ACT.Silu, s_all)

            def view(off, *shape):
                n = int(np.prod(shape))
                assert off + n <= BW, (off, shape)
                v = BIG[:, off:off + n]
                if len(shape) == 2:
                    v = v.rearrange("p (a b) -> p a b", a=shape[0])
                return v

            def bc(ap, n):
                return ap.unsqueeze(2).broadcast_to([ap.shape[0], ap.shape[1], n])

            def bm(ap, n):
                return ap.unsqueeze(1).broadcast_to([ap.shape[0], n, ap.shape[1]])

            GCT = SM[:, 128:144]
            BT = SM[:, 144:160]
            EG = SM[:, 160:176]
            KB = SM[:, 176:192]
            KD = SM[:, 192:200]
            LB, OLB = SM[:, 16:32], SM[:, 32:48]
            RW = ctx_rw
            beta, gc = RW[:, 0, :], RW[:, 1, :]

            gt = {}

            def gates1():
                lb = col("lb", 0, 32)
                mx, e0, e1, sm = SM[:, 48:64], SM[:, 64:80], SM[:, 80:96], SM[:, 96:112]
                tt(mx, lb[:, 0:16], lb[:, 16:32], ALU.max, s_all)
                tt(e0, lb[:, 0:16], mx, ALU.subtract)
                t = tt(e1, lb[:, 16:32], mx, ALU.subtract)
                t = act(SM[:, 64:96], SM[:, 64:96], ACT.Exp, t)
                tt(sm, e0, e1, ALU.add, t)
                V(lambda e: e.reciprocal(sm, sm))
                tt(e0, e0, sm, ALU.mult)
                tt(e1, e1, sm, ALU.mult)
                tt(e1, e1, e0, ALU.add)
                tt(LB, e1, e0, ALU.subtract)
                ts(OLB, LB, -1.0, 1.0, ALU.mult, ALU.add)

                aa, ab = view(15108, 1, T)[0:8, 0, :], view(15620, 1, T)[0:8, 0, :]
                wbg = col("wbg", 0, 128).rearrange("p (k n) -> p k n", k=8)
                for q in range(2):
                    for k in range(8):
                        t = mm(PS[3][0:8, q * T:(q + 1) * T], wbg[:, k, q * 8:(q + 1) * 8], X[:, k, :], s_all, s_xt,
                               start=(k == 0), stop=(k == 7), inc=(k == 7))
                nea = SM[0:8, 120:121]
                act(nea, R8[:, 0:1], ACT.Exp, s_all)
                act(aa, PS[3][0:8, T:2 * T], ACT.Identity, t, bias=R8[:, 1:2])
                act(ab, aa, ACT.Abs)
                ac.do(lambda e: e.preload_act_table_set("natural_log_exp_and_others"), inc=False)
                act(ab, ab, ACT.Exp, scale=-1.0)
                t2 = act(ab, ab, ACT.Ln, bias=1.0)
                stt(aa, aa, 0.0, ab, ALU.max, ALU.add, t2)
                ts(aa, aa, nea, -1.0, ALU.mult, ALU.mult, t2)
                for c in range(2):
                    V(lambda e, c=c: e.tensor_tensor_scan(gc[:, c * 128:(c + 1) * 128], cs("ones", 0, 128, 8),
                                                          aa[:, c * 128:(c + 1) * 128], 0.0, ALU.mult, ALU.add))
                gct = ve.last()
                bt = act(beta, PS[3][0:8, 0:T], ACT.Sigmoid)
                bfree[3] = [gct, bt]
                gt["t"] = [gct, bt]

            def gates2():
                for c in range(2):
                    tr(PS[3][:, c * 8:c * 8 + 8], gc[:, c * 128:(c + 1) * 128], gt["t"], bfree[3])
                    t = tr(PS[3][:, 16 + c * 8:24 + c * 8], beta[:, c * 128:(c + 1) * 128], inc=True)
                V(lambda e: e.tensor_copy(SM[:, 128:160], PS[3][:, 0:32]), t)
                bfree[3] = ve.last()
                return ve.last()

            QKV = view(0, 24, T)
            CB = [view(6144 + 520 * i, 2, 260) for i in range(2)]
            AC = [view(7184 + 512 * i, 2, T) for i in range(2)]
            for i in range(2):
                t = G(lambda e, i=i: e.memset(CB[i][:, :, 0:4], 0.0))
            zt = t
            cb = {"n": 0, "silu": None, "free": [None, None], "acf": [None, None]}
            qkv_tok = {}

            def qkv_post(which, hp):
                def post(ps, t):
                    i = cb["n"] % 2
                    cb["n"] += 1
                    act(CB[i][:, :, 4:260], ps, ACT.Copy, t, cb["free"][i], zt)
                    for m in range(2):
                        j = which * 8 + 2 * hp + m
                        a = act(AC[i][:, m, :], ps[:, m, :], ACT.Copy, cb["acf"][i], scale=col("conv_b_w", j * 4 + 3))
                    if cb["silu"]:
                        cb["silu"]()
                    for q in range(3):
                        for m in range(2):
                            j = which * 8 + 2 * hp + m
                            v = stt(AC[i][:, m, :], CB[i][:, m, 1 + q:257 + q], col("conv_b_w", j * 4 + q), AC[i][:, m, :],
                                    ALU.mult, ALU.add, a)
                    cb["free"][i] = v
                    j = which * 8 + 2 * hp

                    def silu():
                        cb["acf"][i] = qkv_tok[(which, hp)] = act(QKV[:, j:j + 2, :], AC[i], ACT.Silu, v)
                    cb["silu"] = silu
                    return a
                return post

            for hp in range(4):
                for which in range(3):
                    run(product(("w_in_even", 0, 0, 4096 + 1024 * which + 256 * hp), XHL, 0, qkv_post(which, hp), kw=xs))
                    if hp == 0 and which == 0:
                        gates1()
                    if hp == 0 and which == 2:
                        colt = gates2()

            cb["silu"]()

            HS = view(14336, 1, T)
            CH = view(14592, 1, 260)
            AA = view(14852, 1, T)
            YA = view(15108, 2, T)
            ZA = view(15620, 2, T)
            zch = G(lambda e: e.memset(CH[:, :, 0:4], 0.0))
            ga = {"ya": None, "ysplit": [], "pend": None}

            def a_tile(j):
                def post1(ps, t):
                    a = act(HS[:, 0, :], ps[:, 0, :], ACT.Copy, t, ga.get("ch"))
                    v = tt(CH[:, 0, 4:260], ps[:, 1, :], HS[:, 0, :], ALU.mult, a, zch)
                    ga["ch"] = v
                    ts(AA[:, 0, :], CH[:, 0, 2:258], col("conv_a_w", j * 3), None, ALU.mult, None)
                    for q in range(1, 3):
                        stt(AA[:, 0, :], CH[:, 0, 2 + q:258 + q], col("conv_a_w", j * 3 + q), AA[:, 0, :], ALU.mult, ALU.add)
                    return [a, v]

                def post2(ps, t):
                    m = j % 2
                    v = tt(YA[:, m, :], ps[:, 0, :], AA[:, 0, :], ALU.mult, t, ga["ya"])
                    a = act(ZA[:, m, :], ps[:, 1, :], ACT.Copy, t, ga["ya"], v)
                    ga["pend"] = [v, a]
                    if m:
                        a_flush(j - 1)
                    return [v, a]

                yield from product(("w_in_even", 0, 0, (128 * j, 1024 + 128 * j)), XHL, 0, post1, kw=xs)
                yield from product(("w_in_even", 0, 0, (2048 + 128 * j, 3072 + 128 * j)), XHL, 0, post2, kw=xs)

            def a_flush(j):
                a = act(ZA, ZA, ACT.Silu, ga["pend"])
                v = tt(YA, YA, ZA, ALU.mult, a)
                ga["ysplit"] = split_act(YHL, j, 2, YA, v)
                ga["ya"] = ga["ysplit"]

            def chunk_buffers(g):
                return [view(6144 + 4096 * g + 512 * i, 4, 128) for i in range(8)]

            def l2(which, g):
                j = which * 8 + 4 * g
                src = QKV[:, j:j + 4, :]
                base = 6144 + 4096 * g + 2048 * which
                sq, rs = view(base, 4, T), view(base + 1024, 4, T)
                s = act(sq, src, ACT.Square, qkv_tok[(which, 2 * g)], qkv_tok[(which, 2 * g + 1)])
                yield
                for m in range(4):
                    b = GB[g][m // 2]
                    t = mm(PS[b][:, (m % 2) * T:(m % 2 + 1) * T], cs("ones"), sq[:, m, :], s, bfree[b], inc=True)
                    if m % 2:
                        bfree[b] = act(rs[:, m - 1:m + 1, :], PS[b][:, :].rearrange("p (a b) -> p a b", a=2), ACT.Ln, t,
                                       bias=EPSC["1e-6"])
                if which == 0:
                    a = act(rs, rs, ACT.Exp, scale=-0.5, bias=EPSC["lnq"])
                else:
                    a = act(rs, rs, ACT.Exp, scale=-0.5)
                yield
                qk_tok[g] = tt(src, src, rs, ALU.mult, a)

            qk_tok = {}
            GB = [(2, 3, 4), (5, 6, 7)]
            epst = [G(lambda e, o=o, v=v: e.memset(o, v)) for o, v in EPSV]
            epst = epst[-1]
            ac.wait([epst])
            for j in range(8):
                fillers.append(a_tile(j))
            ac.do(lambda e: e.preload_act_table_set("natural_log_exp_and_others"), inc=False)
            act(EG, GCT, ACT.Exp, colt)
            kbt = tt(KB, BT, EG, ALU.mult, ac.last())

            def grp(b):
                return PS[b][:, :].rearrange("p (a b) -> p a b", a=4)

            def row(x, h):
                return cs("ident", h, 1, 8).broadcast_to([8, 128])

            def gdn(g, c):
                b0, b1, b2 = GB[g]
                DD, LT, ML, XX, YY, AT, SS, QD = chunk_buffers(g)
                PP, UU, VB, KBE = DD, LT, ML, XX
                hs = [4 * g + m for m in range(4)]
                tok = slice(c * 128, (c + 1) * 128)
                blk = [slice(m * 128, (m + 1) * 128) for m in range(4)]
                free = gfree[g]
                for m, h in enumerate(hs):
                    t = mm(PS[b0][:, blk[m]], row(gc, h), gc[:, tok], bfree[b0], inc=(m == 3))
                for m, h in enumerate(hs):
                    t2 = mm(PS[b1][:, blk[m]], row(beta, h), beta[:, tok], bfree[b1], inc=(m == 3))
                for m, h in enumerate(hs):
                    kT = QKV[:, 8 + h, tok]
                    t3 = mm(PS[b2][:, blk[m]], kT, kT, qk_tok[g], bfree[b2], inc=(m == 3))
                yield
                v = tt(DD, grp(b0), bc(GCT[:, c * 8 + 4 * g:c * 8 + 4 * g + 4], 128), ALU.subtract, t, free)
                kd = KD[:, 4 * g:4 * g + 4]
                if c == 0:
                    v = tt(kd, grp(b0)[:, :, 127], GCT[:, 4 * g:4 * g + 4], ALU.subtract)
                v = tt(DD, DD, bm(cs("neg"), 4), ALU.add)
                d = act(DD, DD, ACT.Exp, v)
                if c == 0:
                    kdt = act(kd, kd, ACT.Exp)
                    bfree[b0] = v
                else:
                    a = act(QD, grp(b0), ACT.Exp, t, v, free)
                    bfree[b0] = a
                tt(LT, DD, grp(b1), ALU.mult, t2, d, free)
                bfree[b1] = ve.last()
                bfree[b2] = tt(LT, LT, grp(b2), ALU.mult, t3)
                lt = ve.last()
                if c == 1:
                    qd = tt(QD, QD, QKV[:, 4 * g:4 * g + 4, tok], ALU.mult, a, qk_tok[g])
                for m, h in enumerate(hs):
                    t3 = mm(PS[b0][:, blk[m]], QKV[:, 8 + h, tok], QKV[:, h, tok], bfree[b0], inc=(m == 3))
                V(lambda e: e.tensor_copy(XX, bm(cs("ident"), 4)), free)
                V(lambda e: e.tensor_copy(YY, bm(cs("ident"), 4)))
                yield
                at = tt(AT, DD, grp(b0), ALU.mult, t3, free)
                bfree[b0] = at
                for s in range(7):
                    v = tt(ML, LT, bm(cs("gm", 128 * s), 4), ALU.mult, gml[g])
                    for m in range(4):
                        t = mm(PS[b0][:, blk[m]], ML[:, m, :], XX[:, m, :], v, bfree[b0], inc=(m == 3))
                    gml[g] = t
                    yield
                    a = act(PP, grp(b0), ACT.Copy, t, at)
                    bfree[b0] = a
                    for m in range(4):
                        if s < 6:
                            mm(PS[b1][:, blk[m]], YY[:, m, :], PP[:, m, :], a, bfree[b1])
                        t = mm(PS[b2][:, blk[m]], PP[:, m, :], YY[:, m, :], a, bfree[b2], inc=(m == 3))
                    yield
                    if s < 6:
                        bfree[b1] = tt(XX, XX, grp(b1), ALU.subtract, t)
                    bfree[b2] = tt(YY, YY, grp(b2), ALU.subtract, t)
                y = ve.last()
                for m, h in enumerate(hs):
                    tr(PS[b0][:, blk[m]], QKV[:, 8 + h, tok], bfree[b0], qk_tok[g])
                    t4 = tr(PS[b1][:, blk[m]], QKV[:, 16 + h, tok], bfree[b1], qkv_tok[(2, 2 * g)], qkv_tok[(2, 2 * g + 1)],
                            inc=(m == 3))
                yield
                vt = tt(VB, grp(b1), bc(BT[:, c * 8 + 4 * g:c * 8 + 4 * g + 4], 128), ALU.mult, t4, gml[g])
                bfree[b1] = vt
                if c == 0:
                    kt = tt(KBE, grp(b0), bc(kd, 128), ALU.mult, t4, kdt)
                else:
                    kt = tt(KBE, grp(b0), bc(KB[:, 8 + 4 * g:12 + 4 * g], 128), ALU.mult, t4, kbt)
                bfree[b0] = kt
                for m in range(4):
                    t = mm(PS[b2][:, blk[m]], YY[:, m, :], VB[:, m, :], y, vt, bfree[b2], inc=(m == 3))
                if c == 0:
                    yield
                    u = act(UU, grp(b2), ACT.Copy, t, y)
                    bfree[b2] = u
                    for m in range(4):
                        t = mm(PS[b1][:, blk[m]], KBE[:, m, :], UU[:, m, :], u, kt, bfree[b1], inc=(m == 3))
                    yield
                    bfree[b1] = ss_tok[g] = act(SS, grp(b1), ACT.Copy, t)
                else:
                    for m in range(4):
                        t2 = mm(PS[b0][:, blk[m]], KBE[:, m, :], YY[:, m, :], kt, bfree[b0], inc=(m == 3))
                    yield
                    w = act(PP, grp(b0), ACT.Copy, t2)
                    bfree[b0] = w
                    a = act(UU, grp(b2), ACT.Copy, t, y)
                    bfree[b2] = a
                    for m in range(4):
                        t2 = mm(PS[b1][:, blk[m]], PP[:, m, :], SS[:, m, :], w, ss_tok[g], bfree[b1], inc=(m == 3))
                    yield
                    u = tt(UU, UU, grp(b1), ALU.subtract, t2, a)
                    bfree[b1] = u
                for m, h in enumerate(hs):
                    t = mm(PS[b2][:, blk[m]], UU[:, m, :], AT[:, m, :], u, at, bfree[b2], stop=(c == 0), inc=(m == 3))
                    if c == 1:
                        t = mm(PS[b2][:, blk[m]], SS[:, m, :], QD[:, m, :], qd, start=False, inc=(m == 3))
                gfree[g] = [t]
                yield
                bfree[b2] = act(QKV[:, 4 * g:4 * g + 4, tok], grp(b2), ACT.Copy, t)

            ss_tok = [None, None]
            gfree = [None, None]
            gml = [None, None]
            pe_x = [None]

            def resid(n0, first, hook=None):
                def post(ps, t):
                    xv = X[:, 2 * n0:2 * n0 + 2, :]
                    if first:
                        v = stt(xv, xv, ALPHA, ps, ALU.mult, ALU.add, t, pe_x[0])
                    else:
                        v = tt(xv, xv, ps, ALU.add, t)
                    if hook:
                        hook(n0, v)
                    return v
                return post

            def group(g):
                yield from l2(0, g)
                yield from l2(1, g)
                for c in range(2):
                    yield from gdn(g, c)

            def w_out_a():
                for n in range(4):
                    yield from product(("w_out_even", 0, 0, 256 * n), YHL, 0, resid(n, True), ga["ysplit"])

            fillers.append(w_out_a())
            bank["of"], bank["n"] = 2, 0
            gens = [group(0), group(1)]
            rounds = 0
            st["early"] = False
            fill(4)
            while gens:
                for gen in list(gens):
                    try:
                        next(gen)
                    except StopIteration:
                        gens.remove(gen)
                fill(1)
                if rounds % 2 == 0 and ada["n"] < 24 and fillers:
                    ada_fill(1)
                rounds += 1
            late_wait = [ve.last(), ac.last()]
            gp.wait(late_wait)
            bank["of"] = 3

            OT = QKV[:, 0:8, :]

            def rms_heads(g):
                RS, SQ = view(9216 + 2048 * g, 4, T), view(10240 + 2048 * g, 4, T)
                o = OT[:, 4 * g:4 * g + 4, :]
                q = act(SQ, o, ACT.Square, ve.last(), pe.last())
                yield
                for m in range(0, 4, 2):
                    b = 3 + 2 * g + m // 2
                    for i in range(2):
                        t = mm(PS[b][:, i * T:(i + 1) * T], cs("ones"), SQ[:, m + i, :], q, bfree[b], inc=(i == 1))
                    if m == 0:
                        ac.do(lambda e: e.preload_act_table_set("natural_log_exp_and_others"), inc=False)
                    bfree[b] = act(RS[:, m:m + 2, :], PS[b][:, :].rearrange("p (a b) -> p a b", a=2), ACT.Ln, t,
                                   scale=1.0 / 128, bias=EPSC["1e-5"])
                a = act(RS, RS, ACT.Exp, scale=-0.5)
                yield
                stt(o, o, col("gdn_g"), RS, ALU.mult, ALU.mult, a)

            r0, r1 = rms_heads(0), rms_heads(1)
            ys = []
            ZB = [view(8192 + 512 * i, 2, T) for i in range(2)]
            zf = [ac.last(), ac.last()]

            def zb_post(n):
                def post(ps, t):
                    z = ZB[n % 2]
                    a = act(z, ps, ACT.Silu, t, zf[n % 2])
                    v = tt(z, z, OT[:, 2 * n:2 * n + 2, :], ALU.mult, a)
                    zf[n % 2] = split_act(YHL, 8 + 2 * n, 2, z, v)
                    ys.extend(zf[n % 2])
                    return a
                return post

            st["early"] = True
            next(r0)
            next(r1)
            g = product(("w_in_even", 0, 0, 7168), XHL, 0, zb_post(0), kw=xs)
            next(g)
            next(r0)
            next(g)
            next(r1)
            run(r0)
            fill(1)
            run(r1)
            run(g)
            for n in range(1, 4):
                run(product(("w_in_even", 0, 0, 7168 + 256 * n), XHL, 0, zb_post(n), kw=xs))
                fill(1)
            fill_all()

            PTB = view(14336, 2, T)
            LATE = view(14848, 1, 512)[:, 0, :]
            ldt = [ve.last(), ac.last()]
            gp.do(lambda e: e.dma_start(PTB, pT[0]).then_inc(s_p[0], 16), ldt, inc=False)
            gp.do(lambda e: e.dma_start(LATE, late).then_inc(s_p[2], 16), inc=False)

            XC = view(0, 8, T)
            SQP = [view(2048 + 512 * i, 2, T) for i in range(2)]
            ACC = view(3072, 2, T)
            NRS, NMU = view(3584, 1, T)[:, 0, :], view(3840, 1, T)[:, 0, :]
            PL = view(4096, 8, T)
            SG = [view(6144 + 512 * i, 2, T) for i in range(2)]
            hk = {}

            def add_pairs(n, src, prev, *w):
                if n == 0:
                    return None
                if n == 1:
                    return tt(ACC, prev, src, ALU.add, *w, hk.get("acc"))
                return tt(ACC, ACC, src, ALU.add, *w)

            def hook_mean(src):
                def hook(n, t):
                    hk["sum"] = add_pairs(n, src[:, 2 * n:2 * n + 2, :], src[:, 0:2, :], t)
                return hook

            def square(n, src, *w):
                a = act(SQP[n % 2], src[:, 2 * n:2 * n + 2, :], ACT.Square, *w, hk.get(("sq", n % 2)))
                return a

            def log_table():
                ac.do(lambda e: e.preload_act_table_set("natural_log_exp_and_others"), inc=False)

            def hook_sq(src):
                def hook(n, t):
                    if n == 3:
                        log_table()
                    a = square(n, src, t)
                    hk["sum"] = v = add_pairs(n, SQP[n % 2], SQP[0], a)
                    if n:
                        hk[("sq", n % 2)] = v
                        if n == 1:
                            hk[("sq", 0)] = v
                return hook

            def channel_sum():
                b = work_bank()
                mm(PS[b][:, 0:T], cs("ones"), ACC[:, 0, :], hk["sum"], bfree[b], stop=False)
                t = hk["acc"] = mm(PS[b][:, 0:T], cs("ones"), ACC[:, 1, :], start=False, inc=True)
                return b, t

            def rstd(eps, got=None):
                b, t = got or channel_sum()
                bfree[b] = act(NRS, PS[b][:, 0:T], ACT.Ln, t, ve.last(), scale=1.0 / 1024, bias=EPSC[eps])
                return act(NRS, NRS, ACT.Exp, scale=-0.5)

            def layer_norm(src, eps, mid):
                b, t = channel_sum()
                log_table()
                a = act(NMU, PS[b][:, 0:T], ACT.Copy, t, ve.last(), scale=1.0 / 1024)
                bfree[b] = a
                mid()
                b = work_bank()
                for n in range(4):
                    v = tt(XC[:, 2 * n:2 * n + 2, :], src[:, 2 * n:2 * n + 2, :], bm(NMU, 2), ALU.subtract, a, free=(n > 0))
                    q = square(n, XC, v)
                    for m in range(2):
                        t = mm(PS[b][:, 0:T], cs("ones"), SQP[n % 2][:, m, :], q, bfree[b], start=(n + m == 0),
                               stop=(n == 3 and m == 1), inc=(m == 1))
                    hk[("sq", n % 2)] = t
                a = rstd(eps, (b, t))
                mid()
                return a

            def scaled(gain, a, src, finish):
                out, base, old, prev = [], ve.last(), pe.last(), None
                for k in range(9):
                    if k < 8:
                        v = stt(XC[:, k, :], src[:, k, :], gain(k), NRS, ALU.mult, ALU.mult, a, base, free=True)
                        h = finish[0](k, v, old)
                    if k:
                        out.append(finish[1](k - 1, prev))
                    prev = h
                return out

            def plain(hl, shift):
                def hi(k, v, old):
                    return act(hl[0][:, k, :], XC[:, k, :], ACT.Identity, v, old, free=True, bias=shift(k))

                def lo(k, h):
                    return [h, stt(hl[1][:, k, :], XC[:, k, :], shift(k), hl[0][:, k, :].bitcast(f32),
                                   ALU.add, ALU.subtract, h, free=True)]
                return hi, lo

            def rms_mod(g1, sh, hl):
                return scaled(lambda k: g1[:, k:k + 1], rstd("1e-6"), X, plain(hl, lambda k: sh[:, k:k + 1]))

            def pl_layer(i, hook):
                ph = split_act(YHL, 0, 2, PTB, (s_p[i], 16), pe.last())
                if i == 0:
                    gp.do(lambda e: e.dma_start(PTB, pT[1]).then_inc(s_p[1], 16), ph, inc=False)
                u = unit("w_pl", i, 0, 0)
                wh, wl = wparts(u, 2)
                pln = iter((0, 2, 4, 6))
                plt = {}

                def mid():
                    for n in (next(pln), next(pln)):
                        b = take_bank()
                        for m in range(2):
                            for k in range(2):
                                s = slice((n + m) * 128, (n + m + 1) * 128)
                                t = three(PS[b][:, m * T:(m + 1) * T], (wh[:, k, s], wl[:, k, s]), (YH[:, k, :], YL[:, k, :]),
                                          k == 0, k == 1, sp_tok.get(u), bfree[b], ph, inc=(k == 1))
                        bfree[b] = plt[n] = act(PL[:, n:n + 2, :], PS[b][:, :].rearrange("p (a b) -> p a b", a=2), ACT.Copy, t)
                    if n == 6:
                        release(u, t)

                a = layer_norm(X, "1e-5", mid)
                GHL = (YH[:, 8:16, :], YL[:, 8:16, :])
                hi, lo = plain(GHL, lambda k: col("ln_b", 8 * i + k))

                def hi_x(k, v, old):
                    h = hi(k, v, old)
                    act(X[:, k, :], XC[:, k, :], ACT.Identity, v, free=True, bias=col("ln_b", 8 * i + k))
                    return h

                kw = scaled(lambda k: col("ln_g", 8 * i + k), a, XC, (hi_x, lo))

                sgf = [ve.last(), ve.last()]

                def post_n(n):
                    def post(ps, t):
                        g = SG[n % 2]
                        a = act(g, ps, ACT.Sigmoid, t, sgf[n % 2])
                        tt(g, g, PL[:, 2 * n:2 * n + 2, :], ALU.mult, a, plt[2 * n])
                        v = sgf[n % 2] = tt(X[:, 2 * n:2 * n + 2, :], X[:, 2 * n:2 * n + 2, :], g, ALU.add)
                        if hook:
                            hook(n, v)
                        return a
                    return post

                for n in range(4):
                    run_last(product(("w_pl_gate", i, 0, 256 * n), GHL, 0, post_n(n), kw=kw), n == 3)

            for n in range(4):
                run_last(product(("w_out_even", 0, 8, 256 * n), YHL, 8, resid(n, False, hook_mean(X)), ys), n == 3)
            kw = []
            old = [pe.last()]

            def hook_x(n, v):
                kw.extend([split_act(XHL, 2 * n, 2, X[:, 2 * n:2 * n + 2, :], v, old)] * 2)

            st["early"] = True
            pl_layer(0, hook_x)
            st["early"] = False

            HQ = [view(512 * i, 2, T) for i in range(2)]
            HK = [view(1024 + 512 * i, 2, T) for i in range(2)]
            HF = [view(2048 + 512 * i, 2, T) for i in range(2)]
            HT = view(3072, 2, T)
            TOT = BIG[:, 3584:4096]
            ATT = [view(4096 + 512 * i, 4, 128) for i in range(2)]
            AT2 = [view(5120 + 256 * i, 2, 128) for i in range(2)]
            HV = [view(5632 + 512 * i, 2, T) for i in range(2)]
            OH = [view(6656 + 512 * i, 2, T) for i in range(2)]
            HZ = [view(7680 + 512 * i, 2, T) for i in range(2)]
            HR, HSQ = view(8704, 2, T), view(9216, 2, T)
            ys = []
            tk = [dict() for _ in range(9)]
            base_v, base_a = ve.last(), ac.last()

            def old_of(hp, name):
                return tk[hp - 2].get(name) if hp >= 2 else [base_v, base_a]

            def hg_proj(hp):
                i, tn = hp % 2, tk[hp]

                def q_post(ps, t):
                    tn["q"] = act(HQ[i], ps, ACT.Silu, t, old_of(hp, "qk_free"))
                    return tn["q"]

                def f_post(ps, t):
                    tn["sg"] = act(HT, ps, ACT.Sigmoid, t, tk[hp - 1]["k"] if hp else base_v)
                    return tn["sg"]

                def f_rest():
                    for m in range(2):
                        h = 2 * hp + m
                        ts(HF[i][:, m, :], HT[:, m, :], OLB[:, h:h + 1], LB[:, h:h + 1], ALU.mult, ALU.add, tn["sg"])
                    tn["k"] = ts(HK[i], HF[i], -1.0, 1.0, ALU.mult, ALU.add, old_of(hp, "qk_free"))

                def v_post(ps, t):
                    tn["v"] = act(HV[i], ps, ACT.Copy, t, old_of(hp, "av"))
                    return tn["v"]

                def z_post(ps, t):
                    tn["z"] = act(HZ[i], ps, ACT.Silu, t, old_of(hp, "z_free"))
                    return tn["z"]

                yield from product(("w_in_odd", 0, 0, 256 * hp), XHL, 0, q_post, kw=kw)
                yield from product(("w_in_odd", 0, 0, 2048 + 256 * hp), XHL, 0, f_post, kw=kw)
                g = product_tok(("w_in_odd", 0, 0, 4096 + 256 * hp), XHL, v_post, *kw)
                next(g)
                yield
                f_rest()
                yield from g
                yield from product(("w_in_odd", 0, 0, 6144 + 256 * hp), XHL, 0, z_post, kw=kw)

            def hg_attend(hp):
                i, tn = hp % 2, tk[hp]
                b = tn["bank"] = work_bank()
                for m in range(2):
                    h = slice(m * 128, (m + 1) * 128)
                    mm(PS[b][:, m * T:m * T + 128], HV[i][:, 0, h], ATT[i][:, 2 * m, :], tn["v"], tn["fin"], bfree[b])
                    mm(PS[b][:, m * T + 128:m * T + 256], HV[i][:, 0, h], AT2[i][:, m, :], stop=False)
                    t = mm(PS[b][:, m * T + 128:m * T + 256], HV[i][:, 1, h], ATT[i][:, 2 * m + 1, :], start=False, inc=(m == 1))
                tn["av"] = t
                pb = PS[b][:, :].rearrange("p (a b) -> p a b", a=2)
                a = act(OH[i], pb, ACT.Copy, t, old_of(hp, "o_free"))
                tn["sq"] = act(HSQ, pb, ACT.Square, tk[hp - 1].get("ones") if hp else None)
                bfree[b] = tn["sq"]

            def hg_norm(hp):
                i, tn = hp % 2, tk[hp]
                b = work_bank()
                for m in range(2):
                    t = mm(PS[b][:, m * T:(m + 1) * T], cs("ones"), HSQ[:, m, :], tn["sq"], bfree[b], inc=(m == 1))
                tn["ones"] = t
                ac.do(lambda e: e.preload_act_table_set("natural_log_exp_and_others"), inc=False)
                bfree[b] = act(HR, PS[b][:, :].rearrange("p (a b) -> p a b", a=2), ACT.Ln, t, tk[hp - 1].get("n") if hp else None,
                               scale=1.0 / 128, bias=EPSC["1e-5"])
                a = act(HR, HR, ACT.Exp, scale=-0.5)
                yield
                o = OH[i]
                tn["n"] = stt(o, o, col("hgrn_g"), HR, ALU.mult, ALU.mult, a)
                v = tn["z_free"] = tt(o, o, HZ[i], ALU.mult, tn["z"])
                tn["y"] = tn["o_free"] = split_act(YHL, 2 * hp, 2, o, v)
                ys.extend(tn["y"])

            def by_blocks(x, w):
                return x.rearrange("p m (c b i s) -> p (m c) b i s", c=2, i=2, s=w)

            def hg_levels(hp, slot):
                i, tn = hp % 2, tk[hp]
                q, k, f, at = HQ[i], HK[i], HF[i], ATT[i]
                g = G(lambda e: e.memset(at, 0.0), old_of(hp, "av"))
                pt = None
                tot = f.rearrange("p m t -> p (m t)")
                off = 0
                uq, uk, ut = tn["q"], tn["k"], tn["k"]
                fin = None
                for lv in range(-1, 8):
                    if lv == 0:
                        uq = tt(q, q, f, ALU.mult, pt, uq, ut)
                    elif lv > 0:
                        w = 1 << (lv - 1)
                        nb = 2 * T // (2 * w)

                        def pairs(x):
                            return x.rearrange("p m (b i s) -> p (m b) i s", i=2, s=w)
                        tp = tot.rearrange("p (b i) -> p b i", i=2)
                        uk = tt(pairs(k)[:, :, 0, :], pairs(k)[:, :, 0, :], bc(tp[:, :, 1], w), ALU.mult, pt, uk, ut, free=True)
                        uq = tt(pairs(q)[:, :, 1, :], pairs(q)[:, :, 1, :], bc(tp[:, :, 0], w), ALU.mult, pt, uq, ut, free=True)
                        if lv < 7:
                            nt = TOT[:, off:off + nb]
                            off += nb
                            ut = tt(nt, tp[:, :, 0], tp[:, :, 1], ALU.mult, ut, tk[hp - 1].get("lv") if hp else None, free=True)
                            tot = nt
                    b = work_bank()
                    if 0 <= lv < 7:
                        qs = by_blocks(HQ[i], 1 << lv)
                        for m in range(4):
                            s = slice((m % 2) * 128, (m % 2 + 1) * 128)
                            pt = mm(PS[b][:, m * 64:(m + 1) * 64], k[:, m // 2, s], qs[:, m, :, 1, :], uq, uk, bfree[b], inc=(m == 3))
                    elif lv < 0:
                        for m in range(4):
                            s = slice((m % 2) * 128, (m % 2 + 1) * 128)
                            pt = mm(PS[b][:, m * 128:(m + 1) * 128], k[:, m // 2, s], q[:, m // 2, s], uq, uk, bfree[b], inc=(m == 3))
                    else:
                        for m in range(2):
                            pt = mm(PS[b][:, m * 128:(m + 1) * 128], k[:, m, 0:128], q[:, m, 128:256], uq, uk, bfree[b], inc=(m == 1))
                    if fin:
                        fin()

                    def fin(lv=lv, b=b, t=pt):
                        ps = PS[b][:, :].rearrange("p (m t) -> p m t", m=4)
                        half = PS[b][:, 0:256].rearrange("p (m t) -> p m t", m=4)
                        if lv < 0:
                            bfree[b] = V(lambda e: e.copy_predicated(at, bm(cs("ident").bitcast(i32), 4), ps), t, g)
                        elif lv < 5:
                            w = 1 << lv
                            mk = cs("gm", 128 * lv).rearrange("p (b i s) -> p b i s", i=2, s=w)[:, :, 1, :].bitcast(i32)
                            mk = mk.unsqueeze(1).broadcast_to([128, 4, 64 // w, w])
                            to = at.rearrange("p m (b i s) -> p m b i s", i=2, s=w)[:, :, :, 1, :]
                            hw = half.rearrange("p m (b s) -> p m b s", s=w)
                            tn["fv"] = bfree[b] = V(lambda e: e.copy_predicated(to, mk, hw), t)
                        elif lv == 5:
                            act(at[0:32, :, 32:64], half[0:32, :, 0:32], ACT.Copy, t, tn["fv"])
                            bfree[b] = act(at[64:96, :, 96:128], half[64:96, :, 32:64], ACT.Copy)
                        elif lv == 6:
                            bfree[b] = act(at[0:64, :, 64:128], half[0:64, :, :], ACT.Copy, t)
                        else:
                            bfree[b] = act(AT2[i], ps[:, 0:2, :], ACT.Copy, t, old_of(hp, "av"))
                            tn["fin"] = [bfree[b], tn["fv"]]
                    if lv < 7:
                        slot(lv)
                    if hp:
                        if lv == -1:
                            hg_attend(hp - 1)
                        if lv == 1:
                            norm = hg_norm(hp - 1)
                            next(norm)
                        if lv == 2:
                            run(norm)
                fin()
                tn["qk_free"] = pt
                tn["lv"] = ve.last()

            def w_out_first():
                for n in range(4):
                    yield from product(("w_out_odd", 0, 0, 256 * n), YHL, 0, resid(n, True), tk[0]["y"], tk[1]["y"], tk[2]["y"], tk[3]["y"])

            ada["stop"] = max(24, min(48, ada["n"] + 16))
            side_load(base_v, base_a, old)
            side_load()
            run(hg_proj(0))
            for hp in range(8):
                nxt = hg_proj(hp + 1) if hp < 7 else w_out_first()

                def slot(lv):
                    if hp == 7 and lv >= 5:
                        return
                    next(nxt)
                    if lv in (3, 6):
                        ada_side()
                hg_levels(hp, slot)
                if hp < 7:
                    run(nxt)
            hg_attend(7)
            next(nxt)
            run(hg_norm(7))
            run(nxt)
            for n in range(4):
                run_last(product(("w_out_odd", 0, 8, 256 * n), YHL, 8, resid(n, False, hook_mean(X)), ys), n == 3)
            pl_layer(1, hook_sq(X))
            while ada["n"] < ada["stop"]:
                ada_side()

            def mods(i):
                m = MOD[:, 48 * i:48 * i + 48]
                tt(m, m, col("ada_b", 48 * i, 48), ALU.add)
                for q, nm in ((1, "mix_g"), (4, "mlp_g")):
                    m = MOD[:, 48 * i + 8 * q:48 * i + 8 * q + 8]
                    stt(m, m, 1.0, col(nm, 8 * i, 8), ALU.add, ALU.mult)
                ac.wait([ve.last()])

            def mod(i, q):
                return MOD[:, 48 * i + 8 * q:48 * i + 8 * q + 8]

            def gated(i, q, n0, hook=None):
                def post(ps, t):
                    for m in range(2):
                        k = 2 * n0 + m
                        v = stt(X[:, k, :], ps[:, m, :], mod(i, q)[:, k:k + 1], X[:, k, :], ALU.mult, ALU.add, t)
                    if hook:
                        hook(n0, v)
                    return v
                return post

            def mlp(i, hook, adas):
                kw = rms_mod(mod(i, 4), mod(i, 3), XHL)
                RL = [view(7168 + 512 * j, 2, T) for j in range(2)]
                hs = {}
                rl = [None, None]

                def w1_post(n):
                    def post(ps, t):
                        o = 8 * ((n // 4) % 2) + 2 * (n % 4)
                        r = RL[n % 2]
                        a = act(r, ps, ACT.Relu, t, rl[n % 2])
                        v = tt(r, r, r, ALU.mult, a)
                        rl[n % 2] = split_act(YHL, o, 2, r, v, hfree.get(n // 4 - 2))
                        hs.setdefault(n // 4, []).extend(rl[n % 2])
                        return a
                    return post

                hfree = {-1: None}

                def w2(g):
                    for n in range(4):
                        run_last(product(("mlp_w2", i, 8 * g, 256 * n), YHL, 8 * (g % 2), gated(i, 5, n, hook if g == 3 else None), hs[g]),
                                 g == 3 and n == 3)
                        if adas and n % 2:
                            ada_side()
                    hfree[g] = pe.last()

                for g in range(4):
                    for n in range(4 * g, 4 * g + 4):
                        run(product(("mlp_w1", i, 0, 256 * n), XHL, 0, w1_post(n), kw=kw))
                        if adas and n % 2:
                            ada_side()
                    if g:
                        w2(g - 1)
                w2(3)

            mods(0)
            kw = rms_mod(mod(0, 1), mod(0, 0), XHL)
            NV = 18
            NP = 31 - NV
            U = [view(7168 + 288 * i, 1, 286)[:, 0, :] for i in range(2)]
            CO = view(7744, 8, T)
            SGC = [view(9792 + 256 * i, 1, T)[:, 0, :] for i in range(2)]
            CO2 = [view(10304 + 256 * i, 1, T)[:, 0, :] for i in range(2)]
            BG = SM[:, 0:8]
            bgt = tt(BG, col("b_out", 0, 8), mod(0, 2), ALU.mult)
            DG = [view(11072 + NP * 128 * i, NP, 128) for i in range(2)]
            zu = [G(lambda e, i=i: e.memset(U[i][:, 0:30], 0.0), ve.last(), ac.last()) for i in range(2)]
            ut = {}

            def glu_post(j):
                def post(ps, t):
                    u = U[j % 2]
                    a = act(SGC[j % 2], ps[:, 1, :], ACT.Sigmoid, t, ut.get(("sg", j - 2)), bias=col("b_in", 8 + j))
                    v = stt(u[:, 30:286], ps[:, 0, :], col("b_in", j), SGC[j % 2], ALU.add, ALU.mult, a, zu, ut.get(("pe", j - 2)))
                    ut[("sg", j)] = ut[("u", j)] = v
                    c2 = CO2[j % 2]
                    x = [ts(CO[:, j, :], u[:, 0:256], col("dw", 31 * j), col("dw_b", j), ALU.mult, ALU.add),
                         ts(c2, u[:, 1:257], col("dw", 31 * j + 1), None, ALU.mult, None, free=True)]
                    for q in range(2, NV):
                        o = (CO[:, j, :], c2)[q % 2]
                        x[q % 2] = stt(o, u[:, q:256 + q], col("dw", 31 * j + q), o, ALU.mult, ALU.add, x[q % 2], free=True)
                    tt(CO[:, j, :], CO[:, j, :], c2, ALU.add)
                    return [a, v]
                return post

            def diagonals(j):
                for q in range(NP):
                    ut[("dg", j)] = act(DG[j % 2][:, q, :], cs("ident"), ACT.Copy, ut.get(("pe", j - 2), bgt), free=True,
                                        scale=col("dw", 31 * j + NV + q))
                act(X[:, j, :], X[:, j, :], ACT.Identity, bgt, free=True, bias=BG[:, j:j + 1])

            def taps(j):
                b = work_bank()
                u = U[j % 2]
                for q in range(NP):
                    t = mm(PS[b][:, 0:T], DG[j % 2][:, q, :], u[:, NV + q:NV + q + 256], ut[("dg", j)], ut[("u", j)], bfree[b],
                           start=(q == 0), stop=(q == NP - 1), inc=(q == NP - 1))
                ut[("pe", j)] = t
                v = bfree[b] = tt(CO[:, j, :], CO[:, j, :], PS[b][:, 0:T], ALU.add, t)
                if j % 2:
                    hook_mean(CO)(j // 2, v)

            for j in range(8):
                g = product(("conv_w_in", 0, 0, (128 * j, 1024 + 128 * j)), XHL, 0, glu_post(j), kw=kw)
                next(g)
                if j:
                    taps(j - 1)
                diagonals(j)
                run(g)
            taps(7)
            def silu_hi(k, v, old):
                act(CO[:, k, :], XC[:, k, :], ACT.Silu, v, free=True, bias=col("cln_b", k))
                return act(XH[:, k, :], CO[:, k, :], ACT.Copy, old)

            def silu_lo(k, h):
                return [h, tt(XL[:, k, :], CO[:, k, :], XH[:, k, :].bitcast(f32), ALU.subtract, h, free=True)]

            kw = scaled(lambda k: col("cln_g", k), layer_norm(CO, "1e-6", lambda: None), XC, (silu_hi, silu_lo))

            for n in range(4):
                run_last(product(("conv_w_out", 0, 0, 256 * n), XHL, 0, gated(0, 2, n, hook_sq(X)), kw=kw), n == 3)
            ada["stop"] = 48
            side_load(ve.last(), ac.last(), pe.last())
            side_load()
            mlp(0, hook_sq(X), True)
            while ada["n"] < 48:
                ada_side()
            mods(1)

            kw = rms_mod(mod(1, 1), mod(1, 0), XHL)
            AQ = view(4096, 16, T)
            AV2 = view(8192, 2, 1024)
            NB = [(view(10240 + 2048 * i, 4, T), view(11264 + 2048 * i, 4, T)) for i in range(2)]
            ones64, dist = LATE[:, 0:128], LATE[:, 128:512]
            qt = {}

            def qk_post(n):
                def post(ps, t):
                    qt[n] = act(AQ[:, n:n + 2, :], ps, ACT.Copy, t)
                    return qt[n]
                return post

            def av_post(n):
                def post(ps, t):
                    qt["v", n] = act(AV2[:, :, 256 * n:256 * n + 256], ps, ACT.Copy, t)
                    return qt["v", n]
                return post

            def qk_norm(g):
                sq, rs = NB[g % 2]
                src = AQ[:, 4 * g:4 * g + 4, :]
                s = act(sq, src, ACT.Square, qt.get(("pe", g - 2)))
                yield
                for m in range(0, 4, 2):
                    b = work_bank()
                    for i in range(2):
                        t = mm(PS[b][:, i * T:(i + 1) * T], ones64, sq[:, m + i, :], s, bfree[b], (s_p[2], 16), inc=(i == 1))
                    if m == 0:
                        ac.do(lambda e: e.preload_act_table_set("natural_log_exp_and_others"), inc=False)
                    bfree[b] = act(rs[:, m:m + 2, :], PS[b][:, :].rearrange("p (a b) -> p a b", a=2), ACT.Ln, t,
                                   qt.get(("n", g - 2)), scale=1.0 / 64, bias=EPSC["1e-6"])
                qt[("pe", g)] = t
                yield
                a = act(rs, rs, ACT.Exp, scale=-0.5)
                yield
                for m, nm in ((0, "qn_g"), (2, "kn_g")):
                    qt[("n", g)] = stt(src[:, m:m + 2, :], src[:, m:m + 2, :], col(nm), rs[:, m:m + 2, :], ALU.mult, ALU.mult, a)
                yield

            bg = []

            def step():
                for x in list(bg):
                    try:
                        next(x)
                    except StopIteration:
                        bg.remove(x)

            def halves(gen):
                for _ in gen:
                    step()

            SCB = [view(768 * i, 2, 384) for i in range(2)]
            PTA = [view(1536 + 768 * i, 2, 384) for i in range(2)]
            mxs = [SM[:, 200 + 8 * i:208 + 8 * i] for i in range(2)]
            sct = {}

            def scores(p):
                i = p % 2
                sc = SCB[i]
                for hh in range(2):
                    h = 2 * p + hh
                    b = 3 + hh
                    c = 4 * (p // 2) + p % 2
                    q, k = AQ[64 * hh:64 * hh + 64, c, :], AQ[64 * hh:64 * hh + 64, c + 2, :]
                    mm(PS[b][:, 0:128], q[:, 0:128], k[:, 0:128], qt["n", p // 2], bfree[b])
                    t = mm(PS[b][:, 128:384], q[:, 128:256], k, inc=True)
                    slope = float(2.0 ** (-0.5 * (h + 1)))
                    bfree[b] = stt(sc[:, hh, :], dist, slope * 8.0, PS[b][:, 0:384], ALU.mult, ALU.add, t, sct.get(("tr", p - 2)))
                mx = mxs[i][:, 0:4].rearrange("p (h q) -> p h q", h=2)
                rs = mxs[i][:, 4:8].rearrange("p (h q) -> p h q", h=2)
                V(lambda e: e.tensor_reduce(mx[:, :, 0], sc[:, :, 0:128], AX.X, ALU.max))
                V(lambda e: e.tensor_reduce(mx[:, :, 1], sc[:, :, 128:384], AX.X, ALU.max), free=True)
                v = ts(mxs[i][:, 0:4], mxs[i][:, 0:4], -0.125, None, ALU.mult, None)
                sct[("mx", p)] = v

                def rest():
                    for hh in range(2):
                        act(sc[:, hh, 0:128], sc[:, hh, 0:128], ACT.Exp, v, bias=mx[:, hh, 0:1], scale=0.125, accum_out=rs[:, hh, 0:1])
                        a = act(sc[:, hh, 128:384], sc[:, hh, 128:384], ACT.Exp, bias=mx[:, hh, 1:2], scale=0.125,
                                accum_out=rs[:, hh, 1:2])
                    V(lambda e: e.reciprocal(mxs[i][:, 4:8], mxs[i][:, 4:8]), a)
                    tt(sc[:, :, 0:128], sc[:, :, 0:128], bc(rs[:, :, 0], 128), ALU.mult)
                    sct[p] = tt(sc[:, :, 128:384], sc[:, :, 128:384], bc(rs[:, :, 1], 256), ALU.mult)
                return rest

            def values(p):
                sc, pt = SCB[p % 2], PTA[p % 2]
                for hh in range(2):
                    b = 5 + hh
                    for q in range(3):
                        t = tr(PS[b][:, q * 128:(q + 1) * 128], sc[:, hh, q * 128:(q + 1) * 128], sct[p], bfree[b], inc=(q == 2))
                    a = bfree[b] = act(pt[:, hh, :], PS[b][:, 0:384], ACT.Copy, t, sct.get(("pv", p - 2)))
                sct[("tr", p)] = t
                for hh in range(2):
                    hc = slice(64 * (2 * p + hh), 64 * (2 * p + hh) + 64)
                    o = PS[7][64 * hh:64 * hh + 64, :]
                    mm(o[:, 0:128], AV2[:, 0, hc], pt[:, hh, 0:128], a, bfree[7], qt["v", p // 2])
                    mm(o[:, 128:256], AV2[:, 0, hc], pt[:, hh, 128:256], stop=False)
                    t = mm(o[:, 128:256], AV2[:, 1, hc], pt[:, hh, 256:384], start=False, inc=True)
                sct[("pv", p)] = t
                o = PS[7][:, 0:T]
                h = act(YH[:, p, :], o, ACT.Copy, t)
                bfree[7] = tt(YL[:, p, :], o, YH[:, p, :].bitcast(f32), ALU.subtract, h)
                return [h, bfree[7]]

            yt = []

            def attend(n):
                yield from qk_norm(n)
                r0 = scores(2 * n)
                yield
                r0()
                yield
                r1 = scores(2 * n + 1)
                yt.append(values(2 * n))
                yield
                r1()
                yield
                yt.append(values(2 * n + 1))

            for n in range(4):
                halves(product(("attn_w_qkv", 0, 0, 256 * n), XHL, 0, qk_post(4 * n), kw=kw))
                halves(product(("attn_w_qkv", 0, 0, 1024 + 256 * n), XHL, 0, qk_post(4 * n + 2), kw=kw))
                halves(product_tok(("attn_w_qkv", 0, 0, 2048 + 256 * n), XHL, av_post(n), *kw))
                bg.append(attend(n))
            while bg:
                step()
            for n in range(4):
                run_last(product(("attn_w_o", 0, 0, 256 * n), YHL, 0, gated(1, 2, n, hook_sq(X)), kw=yt), n == 3)

            def store(n, t):
                sp.wait([t])
                sp.q.append((lambda e: e.dma_start(out[:, 2 * n:2 * n + 2, :], X[:, 2 * n:2 * n + 2, :]).then_inc(s_out, 16), False))

            mlp(1, store, False)
            sp.q.append((s_out, 64))
            if plan:
                assert st["used"] == len(plan) == st["load"], (st, len(plan))
            return pe, ve, ac, gp, sp, loads

        ctx_rw = sb("RW", [8, 2, T])
        EP = sb("EP", [128, 4])
        EPSC = {"1e-6": EP[:, 0:1], "1e-5": EP[:, 1:2], "lnq": EP[:, 2:3]}
        EPSV = [(EP[:, 0:1], 1e-6), (EP[:, 1:2], 1e-5), (EP[:, 2:3], float(np.log(128.0 ** -0.5)))]
        specs = []
        pe, ve, ac, gp, sp, loads = emit(plan, specs)
        if not plan:
            return specs
        block = ctx.enter_context(nc.Block())

        @block.sync
        def _(eng):
            loads(eng)
            sp.play(eng)

        @block.gpsimd
        def _(eng):
            gp.play(eng)

        @block.scalar
        def _(eng):
            ac.play(eng)

        @block.vector
        def _(eng):
            ve.play(eng)

        @block.tensor
        def _(eng):
            pe.play(eng)
    return specs


def _tiles(v):
    import numpy as _np
    return _np.ascontiguousarray(v.reshape(-1, 128).T)


def kernel(**inputs):
    import numpy as _np
    import concourse.bacc as _bacc
    from concourse import mybir as _mybir
    from concourse.bass_utils import run_bass_kernel_spmd as _run

    a = {k: _np.asarray(v) for k, v in inputs.items()}
    parts = {
        "conv_a_w": a["conv_a_w"][0].reshape(3, 8, 128).transpose(2, 1, 0).reshape(128, 24),
        "conv_b_w": a["conv_b_w"][0].reshape(4, 24, 128).transpose(2, 1, 0).reshape(128, 96),
        "gdn_g": _tiles(a["gdn_norm_g"]), "lb": _tiles(a["lower_bounds"]), "hgrn_g": _tiles(a["hgrn_norm_g"]),
        "ln_g": _tiles(a["ln_g"]), "ln_b": _tiles(a["ln_b"]), "ada_b": _tiles(a["ada_b_2"]),
        "mix_g": _tiles(a["mix_norm_g_2"]), "mlp_g": _tiles(a["mlp_norm_g_2"]), "b_in": _tiles(a["conv_b_in_2"]),
        "dw": a["conv_dw_2"][0].reshape(31, 8, 128).transpose(2, 1, 0).reshape(128, 248),
        "dw_b": _tiles(a["conv_dw_b_2"]), "cln_g": _tiles(a["conv_ln_g_2"]), "cln_b": _tiles(a["conv_ln_b_2"]),
        "b_out": _tiles(a["conv_b_out_2"]),
        "qn_g": _np.concatenate([a["attn_q_norm_g_2"][0]] * 2).reshape(128, 1),
        "kn_g": _np.concatenate([a["attn_k_norm_g_2"][0]] * 2).reshape(128, 1),
        "wbg": a["w_in_even"][0][:, 8192:8208].reshape(8, 128, 16).transpose(1, 0, 2).reshape(128, 128),
    }
    cols = _np.ascontiguousarray(_np.concatenate([parts[n] for n, _ in COLS], 1))
    rows = _np.ascontiguousarray(_np.stack([a["a_log"][0], a["dt_bias"][0]], 1))
    xT = _np.ascontiguousarray(a["x"][0].T.reshape(8, 128, T).transpose(1, 0, 2))
    pT = _np.ascontiguousarray(a["p"][:, 0].transpose(0, 2, 1).reshape(2, 2, 128, T).transpose(0, 2, 1, 3))
    cst, late = constants()
    late = _np.ascontiguousarray(late)
    crow = _np.ascontiguousarray(a["c_2"].reshape(1, 1024))
    names = {n: (n if n in a else n + "_2") for n in
             ("w_in_even", "w_out_even", "w_in_odd", "w_out_odd", "w_pl", "w_pl_gate", "ada_w", "conv_w_in", "conv_w_out",
              "attn_w_qkv", "attn_w_o", "mlp_w1", "mlp_w2")}
    f = _mybir.dt.float32

    def build(plan):
        nc = _bacc.Bacc("TRN2", target_bir_lowering=False, num_devices=1)

        def dram(name, shape, dt=f, kind="ExternalInput"):
            return nc.dram_tensor(name, shape, dt, kind=kind).ap()

        specs = program(nc, dram("xT", (128, 8, T)), dram("wst", (max(len(plan), 1), 128, 2048)), dram("wad", (48, 128, 2048)), dram("cols", cols.shape),
                        dram("rows", rows.shape), dram("crow", crow.shape), dram("pT", pT.shape), dram("cst", cst.shape), dram("late", late.shape),
                        dram("outT", (128, 8, T), kind="ExternalOutput"), plan)
        return nc, specs

    plan = build([])[1]
    wst = _np.empty((len(plan), 128, 2048), _np.float32)
    for u, (name, layer, k0, c0) in enumerate(plan):
        w = a[names[name]][layer]
        if name == "w_pl":
            wst[u] = w.reshape(2, 128, 1024).transpose(1, 0, 2).reshape(128, 2048)
            continue
        if name == "ada_w":
            wst[u] = w[:, c0:c0 + 256].T.reshape(2, 128, 1024).transpose(1, 0, 2).reshape(128, 2048)
            continue
        w = w[128 * k0:128 * k0 + 1024]
        if isinstance(c0, tuple):
            w = _np.concatenate([w[:, c:c + 128] for c in c0], 1)
        else:
            w = w[:, c0:c0 + 256]
        wst[u] = w.reshape(8, 128, 256).transpose(1, 0, 2).reshape(128, 2048)
    wad = _np.ascontiguousarray(a["ada_w_2"].transpose(0, 2, 1).reshape(48, 2, 128, 1024).transpose(0, 2, 1, 3)).reshape(48, 128, 2048)
    nc, _ = build(plan)
    r = _run(nc, [{"xT": xT, "wst": wst, "wad": wad, "cols": cols, "rows": rows, "crow": crow, "pT": pT, "cst": cst, "late": late}], core_ids=[0])
    o = _np.asarray(r.results[0]["outT"])
    return _np.ascontiguousarray(o.transpose(2, 1, 0).reshape(1, T, 1024))
```
